# Optimizing a Trainium2 kernel written in Bass

```python
import math
import jax, jax.numpy as jnp
from jax import lax
import numpy as np

D_MODEL = 2048
BATCH = 1
SEQ = 256
DEPTH = 2

N_META = 16
N_A = DEPTH // 2
N_B = DEPTH - N_A
HG_KDIM = 128
HG_HEADS = D_MODEL // HG_KDIM
HG_FDIM = HG_HEADS * HG_KDIM
HG_VDIM = D_MODEL // HG_HEADS
CHUNK = 64
FOX_HEADS = 16
FOX_HDIM = D_MODEL // FOX_HEADS
Q_BLOCK = 128
EPS = 1e-6
MASK_VALUE = -1e30


def rms_norm(x, g):
    xf = x.astype(jnp.float32)
    y = xf * lax.rsqrt(jnp.mean(xf * xf, axis=-1, keepdims=True) + EPS)
    return (y * g.astype(jnp.float32)).astype(x.dtype)

def hgrn2_mix(h, g_norm, w_in, g_out, w_out, lb):
    bsz, L, _ = h.shape
    u = rms_norm(h, g_norm) @ w_in
    q = u[..., :HG_FDIM]
    f = u[..., HG_FDIM:2 * HG_FDIM]
    i = u[..., 2 * HG_FDIM:2 * HG_FDIM + D_MODEL]
    z = u[..., 2 * HG_FDIM + D_MODEL:]
    q = jax.nn.silu(q).astype(jnp.float32)
    fg = lb + (1.0 - lb) * jax.nn.sigmoid(f.astype(jnp.float32))
    logf = jnp.log(fg)
    k = 1.0 - fg
    v = i.astype(jnp.float32)
    n_pad = CHUNK - N_META
    padf = lambda a: jnp.pad(a, ((0, 0), (n_pad, 0), (0, 0)))
    q, logf, k, v = padf(q), padf(logf), padf(k), padf(v)
    Lp = L + n_pad
    nc = Lp // CHUNK
    to_chunks = lambda a, d: a.reshape(bsz, nc, CHUNK, HG_HEADS, d).transpose(0, 3, 1, 2, 4)
    q = to_chunks(q, HG_KDIM)
    logf = to_chunks(logf, HG_KDIM)
    k = to_chunks(k, HG_KDIM)
    v = to_chunks(v, HG_VDIM)
    b = jnp.cumsum(logf, axis=3)
    b_last = b[..., CHUNK - 1:CHUNK, :]
    b_mid = b[..., CHUNK // 2 - 1:CHUNK // 2, :]
    q_intra = q * jnp.exp(b - b_mid)
    k_intra = k * jnp.exp(b_mid - b)
    causal = jnp.tril(jnp.ones((CHUNK, CHUNK), dtype=bool))
    A = jnp.einsum('bhntd,bhnsd->bhnts', q_intra, k_intra)
    A = jnp.where(causal, A, 0.0)
    o_intra = jnp.einsum('bhnts,bhnse->bhnte', A, v)
    dS = jnp.einsum('bhnsd,bhnse->bhnde', k * jnp.exp(b_last - b), v)
    decay = jnp.exp(b_last[..., 0, :])

    def step(S, inp):
        dec, ds = inp
        return dec[..., None] * S + ds, S

    S0 = jnp.zeros((bsz, HG_HEADS, HG_KDIM, HG_VDIM), jnp.float32)
    _, S_prev = lax.scan(step, S0, (jnp.moveaxis(decay, 2, 0), jnp.moveaxis(dS, 2, 0)))
    S_prev = jnp.moveaxis(S_prev, 0, 2)
    o_inter = jnp.einsum('bhntd,bhnde->bhnte', q * jnp.exp(b), S_prev)
    o = (o_intra + o_inter).transpose(0, 2, 3, 1, 4).reshape(bsz, Lp, HG_HEADS, HG_VDIM)
    o = o[:, n_pad:].astype(h.dtype)
    o = rms_norm(o, g_out.reshape(HG_HEADS, HG_VDIM)).reshape(bsz, L, D_MODEL)
    return (o * jax.nn.silu(z)) @ w_out

def fox_shared_kv(h, g_kv, w_kv, b_f, g_k):
    bsz, L, _ = h.shape
    u = rms_norm(h, g_kv) @ w_kv
    k = u[..., :D_MODEL].reshape(bsz, L, FOX_HEADS, FOX_HDIM)
    v = u[..., D_MODEL:2 * D_MODEL].reshape(bsz, L, FOX_HEADS, FOX_HDIM)
    fl = u[..., 2 * D_MODEL:]
    k = rms_norm(k, g_k)
    logf = jax.nn.log_sigmoid(fl.astype(jnp.float32) + b_f.astype(jnp.float32))
    n_pad = Q_BLOCK - N_META
    k = jnp.pad(k, ((0, 0), (n_pad, 0), (0, 0), (0, 0)))
    v = jnp.pad(v, ((0, 0), (n_pad, 0), (0, 0), (0, 0)))
    logf = jnp.pad(logf, ((0, 0), (n_pad, 0), (0, 0)))
    F = jnp.cumsum(logf, axis=1).transpose(0, 2, 1)
    valid = jnp.arange(L + n_pad) >= n_pad
    return k, v, F, valid

def fox_mix(h, g_norm, w_in, g_q, w_out, k, v, F, valid):
    bsz, L, _ = h.shape
    u = rms_norm(h, g_norm) @ w_in
    q = rms_norm(u[..., :D_MODEL].reshape(bsz, L, FOX_HEADS, FOX_HDIM), g_q)
    z = u[..., D_MODEL:]
    n_pad = Q_BLOCK - N_META
    q = jnp.pad(q, ((0, 0), (n_pad, 0), (0, 0), (0, 0)))
    Lp = L + n_pad
    scale = FOX_HDIM ** -0.5
    outs = []
    for blk in range(Lp // Q_BLOCK):
        s0 = blk * Q_BLOCK
        s1 = s0 + Q_BLOCK
        logits = jnp.einsum('bqhd,bkhd->bhqk', q[:, s0:s1], k[:, :s1]).astype(jnp.float32) * scale
        logits = logits + F[:, :, s0:s1, None] - F[:, :, None, :s1]
        qi = jnp.arange(s0, s1)[:, None]
        ki = jnp.arange(s1)[None, :]
        mask = (ki <= qi) & valid[None, :s1]
        logits = jnp.where(mask, logits, MASK_VALUE)
        p = jax.nn.softmax(logits, axis=-1).astype(v.dtype)
        outs.append(jnp.einsum('bhqk,bkhd->bqhd', p, v[:, :s1]))
    o = jnp.concatenate(outs, axis=1)[:, n_pad:].reshape(bsz, L, D_MODEL)
    return (o * jax.nn.silu(z)) @ w_out

def first_inputs(seed: int = 0) -> dict:
    key = jax.random.key(seed)
    ks = jax.random.split(key, 16)
    f32 = jnp.float32
    nrm = lambda k, shape, s: jax.random.normal(k, shape, f32) * s
    gain = lambda k, shape: 1.0 + 0.02 * jax.random.normal(k, shape, f32)
    sd = D_MODEL ** -0.5
    return {
        "x": nrm(ks[0], (BATCH, SEQ, D_MODEL), 1.0),
        "meta": nrm(ks[1], (N_META, D_MODEL), 1.0),
        "gamma_lb": nrm(ks[2], (N_A + 1, HG_FDIM), 0.1),
        "a_norm": gain(ks[3], (N_A, D_MODEL)),
        "a_w_in": nrm(ks[4], (N_A, D_MODEL, 2 * HG_FDIM + 2 * D_MODEL), sd),
        "a_out_norm": gain(ks[5], (N_A, D_MODEL)),
        "a_w_out": nrm(ks[6], (N_A, D_MODEL, D_MODEL), sd),
        "kv_norm": gain(ks[7], (D_MODEL,)),
        "kv_w": nrm(ks[8], (D_MODEL, 2 * D_MODEL + FOX_HEADS), sd),
        "fox_b_f": 3.0 + 0.1 * jax.random.normal(ks[9], (FOX_HEADS,), f32),
        "fox_k_norm": gain(ks[10], (FOX_HEADS, FOX_HDIM)),
        "b_norm": gain(ks[11], (N_B, D_MODEL)),
        "b_w_in": nrm(ks[12], (N_B, D_MODEL, 2 * D_MODEL), sd),
        "b_q_norm": gain(ks[13], (N_B, FOX_HEADS, FOX_HDIM)),
        "b_w_out": nrm(ks[14], (N_B, D_MODEL, D_MODEL), sd),
    }

def first_block(x, meta, gamma_lb, a_norm, a_w_in, a_out_norm, a_w_out, kv_norm, kv_w,
              fox_b_f, fox_k_norm, b_norm, b_w_in, b_q_norm, b_w_out):
    bsz = x.shape[0]
    h = jnp.concatenate(
        [jnp.broadcast_to(meta[None].astype(x.dtype), (bsz, N_META, D_MODEL)), x], axis=1)
    lbs = jnp.cumsum(jax.nn.softmax(gamma_lb.astype(jnp.float32), axis=0), axis=0)
    shared = None
    for layer in range(DEPTH):
        if layer < N_A:
            h = h + hgrn2_mix(h, a_norm[layer], a_w_in[layer], a_out_norm[layer],
                              a_w_out[layer], lbs[layer])
        else:
            if layer == N_A:
                shared = fox_shared_kv(h, kv_norm, kv_w, fox_b_f, fox_k_norm)
            j = layer - N_A
            k_s, v_s, F_s, valid_s = shared
            h = h + fox_mix(h, b_norm[j], b_w_in[j], b_q_norm[j], b_w_out[j],
                            k_s, v_s, F_s, valid_s)
    return h[:, N_META:]


DEPTH_2 = 1

D_MIX = D_MODEL
CONV_CH = D_MIX // 2
HEAD_DIM = 64
N_Q_HEADS = (D_MIX - CONV_CH) // HEAD_DIM
N_KV_HEADS = 2
GQA_GROUP = N_Q_HEADS // N_KV_HEADS
ATTN_CH = N_Q_HEADS * HEAD_DIM
KV_CH = N_KV_HEADS * HEAD_DIM
IN_COLS = 2 * CONV_CH + ATTN_CH + 2 * KV_CH
CONV_K = 31
WINDOW = 128
BLOCK = 128
ROT_DIM = HEAD_DIM // 4
ROPE_THETA = 500000.0
N_KEYS = 128
N_EXPERTS = N_KEYS * N_KEYS
PEER_HEADS = 8
PEER_KEY_DIM = 256
PEER_HALF = PEER_KEY_DIM // 2
PEER_TOPK = 16
PEER_CHUNK = 128


def rms_norm_2(x, g):
    xf = x.astype(jnp.float32)
    y = xf * lax.rsqrt(jnp.mean(xf * xf, axis=-1, keepdims=True) + EPS)
    return (y * g.astype(jnp.float32)).astype(x.dtype)

def layer_norm(x, g, b):
    xf = x.astype(jnp.float32)
    mu = jnp.mean(xf, axis=-1, keepdims=True)
    var = jnp.mean(jnp.square(xf - mu), axis=-1, keepdims=True)
    y = (xf - mu) * lax.rsqrt(var + EPS)
    return (y * g.astype(jnp.float32) + b.astype(jnp.float32)).astype(x.dtype)

def partial_rotary(t, cos, sin):
    half = ROT_DIM // 2
    r1 = t[..., :half]
    r2 = t[..., half:ROT_DIM]
    return jnp.concatenate([r1 * cos - r2 * sin, r2 * cos + r1 * sin, t[..., ROT_DIM:]], axis=-1)

def conv_group(u, conv_dw_w, conv_dw_b, conv_ln_g, conv_ln_b):
    a, gate = jnp.split(u, 2, axis=-1)
    h = a * jax.nn.sigmoid(gate)
    h = lax.conv_general_dilated(
        h, conv_dw_w[:, None, :].astype(h.dtype), window_strides=(1,),
        padding=[(CONV_K - 1, 0)], dimension_numbers=("NWC", "WIO", "NWC"),
        feature_group_count=CONV_CH) + conv_dw_b
    h = layer_norm(h, conv_ln_g, conv_ln_b)
    return jax.nn.silu(h)

def swa_group(q, k, v, positions, q_norm_g, k_norm_g, attn_sinks):
    B, S, _ = q.shape
    nb = S // BLOCK
    q = rms_norm_2(q.reshape(B, S, N_Q_HEADS, HEAD_DIM), q_norm_g)
    k = rms_norm_2(k.reshape(B, S, N_KV_HEADS, HEAD_DIM), k_norm_g)
    v = v.reshape(B, S, N_KV_HEADS, HEAD_DIM)
    inv_freq = ROPE_THETA ** (-jnp.arange(0, ROT_DIM, 2, dtype=jnp.float32) / ROT_DIM)
    ang = positions.astype(jnp.float32)[..., None] * inv_freq
    cos = jnp.cos(ang)[:, :, None, :].astype(q.dtype)
    sin = jnp.sin(ang)[:, :, None, :].astype(q.dtype)
    q = partial_rotary(q, cos, sin)
    k = partial_rotary(k, cos, sin)

    qb = q.reshape(B, nb, BLOCK, N_KV_HEADS, GQA_GROUP, HEAD_DIM)
    pad = ((0, 0), (BLOCK, 0), (0, 0), (0, 0))
    kb = jnp.pad(k, pad).reshape(B, nb + 1, BLOCK, N_KV_HEADS, HEAD_DIM)
    vb = jnp.pad(v, pad).reshape(B, nb + 1, BLOCK, N_KV_HEADS, HEAD_DIM)
    k_band = jnp.concatenate([kb[:, :-1], kb[:, 1:]], axis=2)
    v_band = jnp.concatenate([vb[:, :-1], vb[:, 1:]], axis=2)

    scores = jnp.einsum("bnqhgd,bnshd->bnhgqs", qb, k_band).astype(jnp.float32)
    scores = scores * (1.0 / math.sqrt(HEAD_DIM))
    blk = jnp.arange(nb)[:, None, None]
    qpos = blk * BLOCK + jnp.arange(BLOCK)[None, :, None]
    kpos = (blk - 1) * BLOCK + jnp.arange(2 * BLOCK)[None, None, :]
    mask = (kpos <= qpos) & (qpos - kpos < WINDOW) & (kpos >= 0)
    scores = jnp.where(mask[None, :, None, None], scores, -1e30)

    sink = attn_sinks.astype(jnp.float32).reshape(1, 1, N_KV_HEADS, GQA_GROUP, 1, 1)
    m = jnp.maximum(jnp.max(scores, axis=-1, keepdims=True), sink)
    p = jnp.exp(scores - m)
    denom = jnp.sum(p, axis=-1, keepdims=True) + jnp.exp(sink - m)
    probs = (p / denom).astype(v.dtype)
    out = jnp.einsum("bnhgqs,bnshd->bnqhgd", probs, v_band)
    return out.reshape(B, S, ATTN_CH)

def peer(xn, peer_w_q, peer_sub_keys, peer_u, peer_v):
    B, S, D = xn.shape
    T = B * S
    xt = xn.reshape(T, D)
    qh = (xt @ peer_w_q).reshape(T, PEER_HEADS, 2, PEER_HALF)
    sub = jnp.einsum("thpc,hpnc->thpn", qh, peer_sub_keys).astype(jnp.float32)
    v1, i1 = lax.top_k(sub[:, :, 0], PEER_TOPK)
    v2, i2 = lax.top_k(sub[:, :, 1], PEER_TOPK)
    cand = (v1[..., :, None] + v2[..., None, :]).reshape(T, PEER_HEADS, PEER_TOPK * PEER_TOPK)
    vals, cidx = lax.top_k(cand, PEER_TOPK)
    e1 = jnp.take_along_axis(i1, cidx // PEER_TOPK, axis=-1)
    e2 = jnp.take_along_axis(i2, cidx % PEER_TOPK, axis=-1)
    experts = e1 * N_KEYS + e2
    gates = jax.nn.softmax(vals, axis=-1).astype(xn.dtype)

    nc = T // PEER_CHUNK

    def chunk_fn(args):
        xc, ec, gc = args
        u_sel = jnp.take(peer_u, ec, axis=0)
        h = jnp.einsum("cd,chkd->chk", xc, u_sel)
        a = jax.nn.gelu(h, approximate=False) * gc
        v_sel = jnp.take(peer_v, ec, axis=0)
        return jnp.einsum("chk,chkd->cd", a, v_sel)

    y = lax.map(chunk_fn, (xt.reshape(nc, PEER_CHUNK, D),
                           experts.reshape(nc, PEER_CHUNK, PEER_HEADS, PEER_TOPK),
                           gates.reshape(nc, PEER_CHUNK, PEER_HEADS, PEER_TOPK)))
    return y.reshape(B, S, D)

def second_inputs(seed: int = 0) -> dict:
    key = jax.random.key(seed)
    ks = jax.random.split(key, 20)
    f32 = jnp.float32
    nrm = lambda k, shape, s: jax.random.normal(k, shape, f32) * s
    positions = jnp.broadcast_to(jnp.arange(SEQ, dtype=jnp.int32)[None, :], (BATCH, SEQ))
    return {
        "x": nrm(ks[0], (BATCH, SEQ, D_MODEL), 1.0),
        "positions": positions,
        "norm1_g": 1.0 + nrm(ks[1], (D_MODEL,), 0.02),
        "w_in": nrm(ks[2], (D_MODEL, IN_COLS), D_MODEL ** -0.5),
        "b_in": nrm(ks[3], (IN_COLS,), 0.02),
        "conv_dw_w": nrm(ks[4], (CONV_K, CONV_CH), CONV_K ** -0.5),
        "conv_dw_b": nrm(ks[5], (CONV_CH,), 0.02),
        "conv_ln_g": 1.0 + nrm(ks[6], (CONV_CH,), 0.02),
        "conv_ln_b": nrm(ks[7], (CONV_CH,), 0.02),
        "q_norm_g": 1.0 + nrm(ks[8], (HEAD_DIM,), 0.02),
        "k_norm_g": 1.0 + nrm(ks[9], (HEAD_DIM,), 0.02),
        "attn_sinks": nrm(ks[10], (N_Q_HEADS,), 0.5),
        "w_out": nrm(ks[11], (D_MIX, D_MODEL), D_MIX ** -0.5),
        "norm2_g": 1.0 + nrm(ks[12], (D_MODEL,), 0.02),
        "peer_w_q": nrm(ks[13], (D_MODEL, PEER_HEADS * PEER_KEY_DIM), D_MODEL ** -0.5),
        "peer_sub_keys": nrm(ks[14], (PEER_HEADS, 2, N_KEYS, PEER_HALF), PEER_HALF ** -0.5),
        "peer_u": nrm(ks[15], (N_EXPERTS, D_MODEL), D_MODEL ** -0.5),
        "peer_v": nrm(ks[16], (N_EXPERTS, D_MODEL), PEER_HEADS ** -0.5),
    }

def second_block(x, positions, norm1_g, w_in, b_in, conv_dw_w, conv_dw_b, conv_ln_g, conv_ln_b,
              q_norm_g, k_norm_g, attn_sinks, w_out, norm2_g, peer_w_q, peer_sub_keys,
              peer_u, peer_v):
    for _ in range(DEPTH_2):
        xn = rms_norm_2(x, norm1_g)
        proj = xn @ w_in + b_in
        c0 = 2 * CONV_CH
        conv_in = proj[..., :c0]
        q = proj[..., c0:c0 + ATTN_CH]
        k = proj[..., c0 + ATTN_CH:c0 + ATTN_CH + KV_CH]
        v = proj[..., c0 + ATTN_CH + KV_CH:]
        conv_out = conv_group(conv_in, conv_dw_w, conv_dw_b, conv_ln_g, conv_ln_b)
        attn_out = swa_group(q, k, v, positions, q_norm_g, k_norm_g, attn_sinks)
        mixed = jnp.concatenate([conv_out, attn_out], axis=-1)
        x = x + mixed @ w_out
        x = x + peer(rms_norm_2(x, norm2_g), peer_w_q, peer_sub_keys, peer_u, peer_v)
    return x


def setup_inputs(seed=0):
    out = dict(first_inputs(seed))
    for name, value in second_inputs(seed + 1).items():
        if name != "x":
            out[name + "_2"] = value
    return out


def reference(
    x, meta, gamma_lb, a_norm, a_w_in, a_out_norm, a_w_out, kv_norm, kv_w, fox_b_f, fox_k_norm,
    b_norm, b_w_in, b_q_norm, b_w_out, positions_2, norm1_g_2, w_in_2, b_in_2, conv_dw_w_2,
    conv_dw_b_2, conv_ln_g_2, conv_ln_b_2, q_norm_g_2, k_norm_g_2, attn_sinks_2, w_out_2,
    norm2_g_2, peer_w_q_2, peer_sub_keys_2, peer_u_2, peer_v_2,
):
    x = first_block(
        x, meta, gamma_lb, a_norm, a_w_in, a_out_norm, a_w_out, kv_norm, kv_w, fox_b_f,
        fox_k_norm, b_norm, b_w_in, b_q_norm, b_w_out,
    )
    return second_block(
        x, positions_2, norm1_g_2, w_in_2, b_in_2, conv_dw_w_2, conv_dw_b_2, conv_ln_g_2,
        conv_ln_b_2, q_norm_g_2, k_norm_g_2, attn_sinks_2, w_out_2, norm2_g_2, peer_w_q_2,
        peer_sub_keys_2, peer_u_2, peer_v_2,
    )


_drawn_inputs = setup_inputs


def setup_inputs(seed=0):
    import zlib

    import numpy as np

    out = dict(_drawn_inputs(seed))
    spreads = {}
    factors = {'gamma_lb': 3.989,
     'a_out_norm': 2.921,
     'kv_norm': 5.494,
     'fox_b_f': 3.08,
     'fox_k_norm': 7.097,
     'b_norm': 5.394,
     'b_q_norm': 7.122,
     'norm1_g_2': 9.299,
     'conv_ln_g_2': 28.96,
     'conv_ln_b_2': 30.04,
     'q_norm_g_2': 31.841,
     'k_norm_g_2': 32.836,
     'attn_sinks_2': 57.656,
     'norm2_g_2': 21.488,
     'b_in_2': 8.0,
     'conv_dw_b_2': 8.0}
    for name, (base, spread) in spreads.items():
        noise = np.random.default_rng([zlib.crc32(name.encode()), seed]).standard_normal(out[name].shape)
        drawn = base * np.exp(spread * noise) if base else spread * noise
        out[name] = __import__('jax').numpy.asarray(drawn.astype(out[name].dtype))
    for name, factor in factors.items():
        out[name] = (out[name] * factor).astype(out[name].dtype)
    return out
```

```python
from contextlib import ExitStack

import numpy as np

import concourse.bass as bass
from concourse import mybir

ALU = mybir.AluOpType
ACT = mybir.ActivationFunctionType
F32 = mybir.dt.float32
F32R = mybir.dt.float32r
U32 = mybir.dt.uint32
I32 = mybir.dt.int32
AX_X = mybir.AxisListType.X

P = 128
D = 2048
KT = D // P
META = 16
SEQ = 256
L = META + SEQ
HEADS = 16
EPS = 1e-6
NEG = -1e30

CH = 64
NCH = SEQ // CH
MID = CH // 2 - 1

CONV_T = 8
TAPS = 31
HD = 64
PEER_HEADS = 8
TOPK = 16
SLOTS = PEER_HEADS * TOPK
GROUPS = SEQ // P

T_HGRN = 0
T_AOUT = T_HGRN + 4 * HEADS
T_KV = T_AOUT + KT
T_FORGET = T_KV + 2 * HEADS
T_QZ = T_FORGET + 1
T_BOUT = T_QZ + 2 * HEADS
T_CONV = T_BOUT + KT
T_SWK = T_CONV + 2 * CONV_T
T_SWV = T_SWK + 1
T_SWQ = T_SWV + 1
T_WOUT = T_SWQ + 8
T_PEERQ = T_WOUT + KT
TILES = T_PEERQ + 2 * PEER_HEADS

PARAMS = {}
_at = 0
for _name, _n in (("a_norm", KT), ("gamma0", KT), ("gamma1", KT), ("a_out_norm", HEADS), ("kv_norm", KT),
                  ("k_norm", HEADS), ("b_norm", KT), ("q_norm", HEADS), ("norm1", KT), ("b_in", 26),
                  ("conv_w", CONV_T * TAPS), ("conv_b", CONV_T), ("ln_g", CONV_T), ("ln_b", CONV_T),
                  ("swq_g", 1), ("swk_g", 1), ("norm2", KT), ("b_f", 1), ("sinks", 16)):
    PARAMS[_name] = (_at, _n)
    _at += _n
N_PARAMS = _at

CONSTS = {}
_at = 0
for _name, _n in (("ident", P), ("ones", P), ("iota", TOPK),
                  ("onehot", HEADS), ("freq", 1), ("eps", 1), ("one", 1)):
    CONSTS[_name] = (_at, _n)
    _at += _n
N_CONSTS = _at
MASK_H = P + META
TAB_H = MASK_H + L
MASK_F = 2 * META + 3 * P
MASK_S = 3 * P
TAB_S = MASK_S + 2 * P


def constants():
    c = np.zeros((P, N_CONSTS), np.float32)

    def put(name, a):
        at, n = CONSTS[name]
        c[:, at:at + n] = a

    r = np.arange(P)
    put("ident", np.eye(P))
    put("ones", 1.0)
    rot = np.zeros((P, P), np.float32)
    freq = np.zeros((P, 1), np.float32)
    inv = (np.float32(500000.0) ** (-np.arange(0, 16, 2, dtype=np.float32) / np.float32(16))).astype(np.float32)
    for base in (0, HD):
        for i in range(8):
            rot[base + 8 + i, base + i] = -1.0
            rot[base + i, base + 8 + i] = 1.0
            freq[base + i] = freq[base + 8 + i] = inv[i]
    put("freq", freq)
    reset = np.ones(L, np.float32)
    reset[0] = 0.0
    reset[META::CH] = 0.0
    put("iota", np.arange(TOPK))
    onehot = np.zeros((P, HEADS), np.float32)
    onehot[r[:HEADS], r[:HEADS]] = 1.0
    onehot[32 + r[:HEADS], r[:HEADS]] = 1.0
    put("onehot", onehot)
    put("eps", EPS)
    put("one", 1.0)
    m = np.zeros((P, TAB_H + MASK_F + TAB_S), np.float32)
    m[:, MASK_H:TAB_H] = reset
    m[:, TAB_H + MASK_F + MASK_S:-P] = rot
    m[:, -P:] = r[:, None] // HD == r[None, :] // HD
    s, t = r[:, None] % CH, np.arange(CH)[None, :]
    m[:, 0:P] = np.tile(s <= t, (1, 2))
    m[:META, P:MASK_H] = r[:META, None] <= r[None, :META]
    k1, k2 = np.arange(META + P)[None, :], np.arange(L)[None, :]
    f = m[:, TAB_H:TAB_H + MASK_F]
    f[:, :META + P] = np.where(k1 <= META + r[:, None], 0.0, NEG)
    f[:, META + P:] = np.where(k2 <= META + P + r[:, None], 0.0, NEG)
    w = m[:, TAB_H + MASK_F:TAB_H + MASK_F + MASK_S]
    kpos = np.arange(P)[None, :]
    w[:, :P] = np.where(kpos <= r[:, None], 0.0, NEG)
    kpos = np.arange(2 * P)[None, :]
    qpos = P + r[:, None]
    w[:, P:] = np.where((kpos <= qpos) & (qpos - kpos < 128), 0.0, NEG)
    return c, m


def static(v):
    return isinstance(v, int)


def need(eng, sem, value):
    if not static(value) or value > 0:
        eng.wait_ge(sem, value)


def within(i, n):
    return not static(i) or 0 <= i < n


class Chain:

    def __init__(self, eng, sem):
        self.eng, self.sem, self.base, self.n = eng, sem, 0, 0

    def link(self, ins):
        ins.then_inc(self.sem, 1)
        self.n += 1
        self.eng.wait_ge(self.sem, self.base + self.n)

    def run(self, body, full, count, tail):
        for i in range(full + 1):
            before = self.n
            body(i)
        per = self.n - before
        total = self.base + self.n
        with self.eng.Fori(full + 1, count) as i:
            self.base, self.n = total + (i - (full + 1)) * per, 0
            body(i)
            assert self.n == per
        self.base, self.n = total + (count - full - 1) * per, 0
        for i in range(count, count + tail):
            body(i)


class Named:
    pass


class Tile:

    def __init__(self, base, i, s):
        self.q = (base + s) % 4
        self.m = i + (base + s) // 4
        self.n = 4 * self.m + self.q

    def next(self):
        t = Tile.__new__(Tile)
        t.q = (self.q + 1) % 4
        t.m = self.m + (self.q == 3)
        t.n = self.n + 1
        return t


def build(nc, hT_in, params_in, consts_in, masks_in, pos_in, keys_in, w_in, u_in, v_in, out):
    with ExitStack() as ctx:
        def sem(name):
            return ctx.enter_context(nc.semaphore(name))

        def tensor(stack, name, shape, dt=F32, **kw):
            return stack.enter_context(nc.sbuf_tensor(name, shape, dt, **kw))

        params = tensor(ctx, "params", [P, N_PARAMS])
        consts = tensor(ctx, "consts", [P, N_CONSTS])
        rinv = tensor(ctx, "rinv", [P, L])
        root = tensor(ctx, "root", [P, L])
        sq2 = tensor(ctx, "sq2", [P, 2, L])
        raw = tensor(ctx, "raw", [P, 4, D])
        zt = tensor(ctx, "zeros", [P, P])
        token = tensor(ctx, "token", [P, 96])
        inner = ExitStack()
        whi = tensor(inner, "whi", [P, 4, D // 2], F32R)
        wlo = tensor(inner, "wlo", [P, 4, D // 2], F32R)
        hT = tensor(inner, "hT", [P, KT, L])
        xb = (tensor(inner, "xb_hi", [P, KT, L], F32R), tensor(inner, "xb_lo", [P, KT, L], F32R))
        innermost = ExitStack()
        xa = (tensor(innermost, "xa_hi", [P, KT, L], F32R), tensor(innermost, "xa_lo", [P, KT, L], F32R))
        bank = [ctx.enter_context(nc.psum_tensor(f"bank{i}", [P, 512], F32)) for i in range(8)]

        g = Named()
        with ExitStack() as st:
            (g.qr, g.fr, g.vr, g.zr, g.qs, g.fg, g.kk, g.zs, g.sq_q, g.sq_f, g.sq_z, g.logf, g.cum, g.dmid, g.dlast,
             g.e_mid, g.e_nmid, g.e_cum, g.e_last, g.qi, g.ki, g.qe, g.ks, g.osq, g.lnv, g.rn, g.on, g.mm) = (
                tensor(st, "g_" + name, [P, L]) for name in ("qr", "fr", "vr", "zr", "qs", "fg", "kk", "zs", "sq_q",
                                                             "sq_f", "sq_z", "logf", "cum", "dmid", "dlast", "e_mid",
                                                             "e_nmid", "e_cum", "e_last", "qi", "ki", "qe", "ks",
                                                             "osq", "lnv", "rn", "on", "mm"))
            g.v = tensor(st, "g_v", [P, 3, P])
            g.kst = tensor(st, "g_kst", [P, 3, P])
            g.att = tensor(st, "g_att", [P, MASK_H])
            g.state = tensor(st, "g_state", [P, NCH, P])
            g.lb = tensor(st, "g_lb", [P, KT])
            g.oml = tensor(st, "g_oml", [P, KT])
            g.tmp = tensor(st, "g_tmp", [P, 4, KT])
            g.mask = tensor(st, "g_mask", [P, TAB_H])
        f = Named()
        with ExitStack() as st:
            f.kT = tensor(st, "f_kT", [P, HEADS, L])
            f.vT = tensor(st, "f_vT", [P, HEADS, L])
            f.LF = tensor(st, "f_LF", [P, SEQ])
            f.LA = tensor(st, "f_LA", [P, SEQ])
            f.RA = tensor(st, "f_RA", [P, L])
            f.mask = tensor(st, "f_mask", [P, MASK_F])
            f.stat = tensor(st, "f_stat", [P, 8])
            f.qg = tensor(st, "f_qg", [P, HEADS])
            with ExitStack() as s2:
                (f.kr, f.ksq, f.lnv, f.rn) = (
                    tensor(s2, "fk_" + name, [P, L]) for name in ("kr", "ksq", "lnv", "rn"))
                (f.fx, f.fa, f.fl, f.fF, f.ones) = (
                    tensor(s2, "ff_" + name, [HEADS, L]) for name in ("fx", "fa", "fl", "fF", "ones"))
            with ExitStack() as s2:
                (f.qr, f.qn, f.zr, f.zz, f.mm) = (
                    tensor(s2, "fq_" + name, [P, SEQ]) for name in ("qr", "qn", "zr", "zz", "mm"))
                f.qsq, f.zsig, f.qrn = sq2[:, 0, 0:SEQ], sq2[:, 1, 0:SEQ], root[:, 0:SEQ]
                f.vs = tensor(s2, "f_vs", [P, L])
                f.pr = tensor(s2, "f_pr", [P, MASK_F])
                f.pt = tensor(s2, "f_pt", [P, 4, P])
                f.v1 = tensor(s2, "f_v1", [P, P])
                f.pm = tensor(s2, "f_pm", [META, 3, P])
        c = Named()
        with ExitStack() as st:
            (c.gr, c.ar, c.sg, c.kr, c.vr, c.v1, c.k1, c.kn, c.kf, c.qr, c.q1, c.qsq, c.qln, c.qrn, c.qn, c.qf, c.t1,
             c.mm, c.cos, c.sin, c.mu, c.rstd, c.lnv, c.ct, c.cy, c.csig, c.cm) = (
                tensor(st, "c_" + name, [P, SEQ]) for name in ("gr", "ar", "sg", "kr", "vr", "v1", "k1", "kn", "kf",
                                                               "qr", "q1", "qsq", "qln", "qrn", "qn", "qf", "t1",
                                                               "mm", "cos", "sin", "mu", "rstd", "lnv", "ct", "cy",
                                                               "csig", "cm"))
            c.csq = tensor(st, "c_csq", [P, SEQ])
            c.ksq, c.kln, c.krn = c.csq, c.lnv, c.rstd
            c.hc = tensor(st, "c_hc", [P, SEQ + TAPS - 1])
            c.acc = tensor(st, "c_acc", [P, SEQ])
            c.wt = tensor(st, "c_wt", [P, TAPS + 1])
            c.cv = tensor(st, "c_cv", [P, CONV_T, SEQ])
            c.v = tensor(st, "c_v", [P, 2, P])
            c.pr = [tensor(st, f"c_pr{i}", [P, MASK_S]) for i in range(2)]
            c.pt = [tensor(st, f"c_pt{i}", [P, 3, P]) for i in range(2)]
            c.mask = tensor(st, "c_mask", [P, TAB_S])
            c.stat = tensor(st, "c_stat", [P, 2, 16])
            c.posi = tensor(st, "c_posi", [P, SEQ], I32)
        e = Named()
        e.xtok = tensor(ctx, "e_xtok", [P, GROUPS, D], side="right")
        e.ytok = tensor(ctx, "e_ytok", [P, GROUPS, D], side="right")
        e.idx = tensor(ctx, "e_idx", [P, GROUPS, SLOTS], U32, side="right")
        e.gate = tensor(ctx, "e_gate", [P, GROUPS, SLOTS], side="right")
        e.hid = tensor(ctx, "e_hid", [P, 2, 4], side="right")
        e.act = tensor(ctx, "e_act", [P, 2, 4], side="right")
        e.coef = tensor(ctx, "e_coef", [P, 2, 4], side="right")
        e.idn = tensor(ctx, "e_idn", [P, 2, 4], U32, side="right")
        innermost.close()
        r = Named()
        with ExitStack() as st:
            r.keys = tensor(st, "r_keys", [P, 2 * PEER_HEADS, P])
            r.qT = tensor(st, "r_qT", [P, SEQ])
            r.hc = tensor(st, "r_hc", [P, SEQ])
            r.gained = tensor(st, "r_gained", [P, SEQ])
            r.rtok = tensor(st, "r_rtok", [P, GROUPS])
            r.work = tensor(st, "r_work", [P, SEQ])
            r.top = tensor(st, "r_top", [P, GROUPS, 2, TOPK])
            r.topi = tensor(st, "r_topi", [P, GROUPS, 2, TOPK], U32)
            r.topf = tensor(st, "r_topf", [P, GROUPS, 2, TOPK])
            r.cand = tensor(st, "r_cand", [P, GROUPS, TOPK * TOPK])
            r.val = tensor(st, "r_val", [P, GROUPS, TOPK])
            r.ci = tensor(st, "r_ci", [P, GROUPS, TOPK], U32)
            r.cij = tensor(st, "r_cij", [P, 2, GROUPS, TOPK], U32)
            r.cf = tensor(st, "r_cf", [P, 2, GROUPS, TOPK])
            r.oh = tensor(st, "r_oh", [P, GROUPS, TOPK, TOPK])
            r.ex = tensor(st, "r_ex", [P, 2, GROUPS, TOPK])
            r.st = tensor(st, "r_st", [P, 2, GROUPS * PEER_HEADS])
            r.vals = tensor(st, "r_vals", [P, GROUPS, SLOTS])
        inner.close()
        vrow = tensor(ctx, "vrow", [P, 4, D])

        def par(name, j=0, n=1, rows=P):
            at = PARAMS[name][0]
            return params[0:rows, bass.ds(at + j, n)]

        def con(name, rows=P):
            at, n = CONSTS[name]
            return consts[0:rows, at:at + n]

        token_at = {nc.scalar: 0, nc.vector: 0, nc.gpsimd: 0}

        def lone(eng):
            token_at[eng] = (token_at[eng] + 1) % 32
            k = 32 * list(token_at).index(eng) + token_at[eng]
            if eng is nc.scalar:
                eng.activation(token[:, k:k + 1], con("one"), ACT.Copy)
            elif eng is nc.vector:
                eng.memset(token[:, k:k + 1], 0.0)
            else:
                eng.tensor_tensor(token[:, k:k + 1], con("one"), con("one"), ALU.add)

        def at3(t, j, cols=slice(None)):
            return t[:, bass.ds(j, 1), cols]

        def one3(ap):
            return ap.rearrange("p (a n) -> p a n", a=1)

        inputs_in = sem("inputs_in")
        w_loaded = [sem(f"w_loaded{i}") for i in range(4)]
        w_hi_done = sem("w_hi_done")
        w_lo_done = [sem("w_lo_done0"), sem("w_lo_done1")]
        halves_done = sem("halves_done")
        evacuated = sem("evacuated")
        x_hi_done = sem("x_hi_done")
        x_split = sem("x_split")
        sq_done = sem("sq_done")
        sum_done = sem("sum_done")
        root_done = sem("root_done")
        rinv_done = sem("rinv_done")
        act_chain = sem("act_chain")
        dve_chain = sem("dve_chain")
        pool_chain = sem("pool_chain")
        preset = sem("preset")
        ones_set = sem("ones_set")
        cols_all, cols_q = slice(0, L), slice(META, L)

        block = ctx.enter_context(nc.Block())

        def split_hi(act, t):
            act.wait_ge(w_loaded[t.q], 16 * t.m + 16)
            for half in range(2):
                need(act, halves_done, 2 * t.n + half - 3)
                act.activation(whi[:, (2 * t.q + half) % 4, :], raw[:, t.q, half * 1024:(half + 1) * 1024],
                               ACT.Copy).then_inc(w_hi_done, 1)

        def split_lo(eng, t, half):
            eng.wait_ge(w_hi_done, 2 * t.n + half + 1)
            slot = (2 * t.q + half) % 4
            eng.tensor_tensor(wlo[:, slot, :], raw[:, t.q, half * 1024:(half + 1) * 1024],
                              whi[:, slot, :].bitcast(F32), ALU.subtract).then_inc(w_lo_done[half], 1)

        def project(te, t, x, cols):
            n = cols.stop - cols.start
            need(te, evacuated, t.n - 1)
            ps = bank[t.q % 2][:, 0:n]
            for half in range(2):
                te.wait_ge(w_lo_done[half], t.n + 1)
                slot = (2 * t.q + half) % 4
                for k in range(8):
                    kk = half * 8 + k
                    hi, lo = whi[:, slot, k * P:(k + 1) * P], wlo[:, slot, k * P:(k + 1) * P]
                    te.matmul(ps, hi, x[0][:, kk, cols], start=(kk == 0), stop=False)
                    te.matmul(ps, hi, x[1][:, kk, cols], start=False, stop=False)
                    last = te.matmul(ps, lo, x[0][:, kk, cols], start=False, stop=(kk == KT - 1))
                last.then_inc(halves_done, 1)

        def landed(eng, t):
            eng.wait_ge(halves_done, 2 * t.n + 2)

        def proj_ps(t, n):
            return bank[t.q % 2][:, 0:n]

        SUM = bank[2]

        def out_steps(base, i, s):
            j = 4 * i + s
            return j, Tile(base, i, s)

        OUT = ((T_AOUT, xb, cols_all, "kv_norm", xa, 1), (T_BOUT, xa, cols_q, "norm1", xb, 3),
               (T_WOUT, xa, cols_q, "norm2", xb, 4))
        SPLITS = {T_HGRN: 16, T_AOUT: 32, T_KV: 48, T_QZ: 64, T_BOUT: 80, T_CONV: 96, T_WOUT: 112, T_PEERQ: 128}
        SQ_BEFORE = {T_AOUT: 4, T_BOUT: 4 + 16, T_WOUT: 4 + 32}

        def out_tensor(te, ch, spec):
            base, x, cols, _, _, _ = spec
            n = cols.stop - cols.start
            need(te, x_split, SPLITS[base])
            te.wait_ge(root_done, {T_AOUT: 1, T_BOUT: 2, T_WOUT: 3}[base])
            te.matmul(SUM[:, 0:n], zeros_l, hT[:, 0, 0:n], start=True, stop=False)

            def body(i):
                for s in range(4):
                    j, t = out_steps(base, i, s)
                    if within(j, KT):
                        project(te, t, x, slice(0, n))
                    if within(j - 1, KT):
                        te.wait_ge(sq_done, SQ_BEFORE[base] + j)
                        last = te.matmul(SUM[:, 0:n], con("ones"), sq2[:, (s - 1) % 2, 0:n], start=False,
                                         stop=(static(j) and j == KT))
                        last.then_inc(sum_done, 1)
                    if static(j) and j == KT:
                        break
            ch.run(body, 1, 4, 1)

        def out_scalar(act, ch, spec):
            base, _, cols, gain, y, _ = spec
            n = cols.stop - cols.start

            def body(i):
                for s in range(4):
                    j, t = out_steps(base, i, s)
                    if within(j, KT):
                        split_hi(act, t.next())
                    if within(j - 1, KT):
                        act.wait_ge(evacuated, t.n)
                        lone(act)
                        act.activation(at3(y[0], j - 1, slice(0, n)), at3(hT, j - 1, cols), ACT.Copy,
                                       scale=par(gain, j - 1)).then_inc(x_hi_done, 1)
                        need(act, sum_done, SUM_BEFORE[base] + j - 2)
                        lone(act)
                        act.activation(one3(sq2[:, (s - 1) % 2, 0:n]), at3(hT, j - 1, cols), ACT.Square)\
                            .then_inc(sq_done, 1)
                    if static(j) and j == KT:
                        break
            ch.run(body, 1, 4, 1)
            act.wait_ge(sum_done, SUM_BEFORE[base] + KT)
            act.activation(root[:, 0:n], SUM[:, 0:n], ACT.Sqrt, bias=con("eps"), scale=1.0 / D)\
                .then_inc(root_done, 1)

        SUM_BEFORE = {T_AOUT: 1, T_BOUT: 1 + 16, T_WOUT: 1 + 32}

        def out_vector(ve, ch, spec, halves):
            base, _, cols, gain, y, nroot = spec
            n = cols.stop - cols.start

            def body(i):
                for s in range(4):
                    j, t = out_steps(base, i, s)
                    if within(j - 1, KT):
                        ve.wait_ge(halves_done, 2 * t.n)
                        ve.tensor_tensor(at3(hT, j - 1, cols), one3(bank[(t.q + 3) % 4 % 2][:, 0:n]),
                                         at3(hT, j - 1, cols), ALU.add).then_inc(evacuated, 1)
                    if within(j, KT):
                        for half in halves:
                            split_lo(ve, t.next(), half)
                    if within(j - 1, KT):
                        ve.wait_ge(x_hi_done, SPLITS[base] + j)
                        ve.scalar_tensor_tensor(at3(y[1], j - 1, slice(0, n)), at3(hT, j - 1, cols),
                                                par(gain, j - 1), at3(y[0], j - 1, slice(0, n)).bitcast(F32),
                                                ALU.mult, ALU.subtract).then_inc(x_split, 1)
                    if static(j) and j == KT:
                        break
            ve.wait_ge(w_lo_done[0], base + 1)
            ch.run(body, 1, 4, 1)
            ve.wait_ge(root_done, ROOT_AFTER[base])
            ve.reciprocal(rinv[:, 0:n], root[:, 0:n]).then_inc(rinv_done, 1)

        ROOT_AFTER = {T_AOUT: 2, T_BOUT: 3, T_WOUT: 4}

        def out_pool(po, ch, spec, halves):
            base = spec[0]

            def body(i):
                for s in range(4):
                    for half in halves:
                        split_lo(po, Tile(base, i, s).next(), half)
            ch.run(body, 0, 4, 0)

        zeros_l = zt[:]

        masks_f, masks_c, masks_r = sem("masks_f"), sem("masks_c"), sem("masks_r")
        gates_done = sem("gates_done")
        fg_done = sem("fg_done")
        logf_done = sem("logf_done")
        cum_done = sem("cum_done")
        exps_done = sem("exps_done")
        factors_done = sem("factors_done")
        vT_done = sem("vT_done")
        v_done = sem("v_done")
        kT_done = sem("kT_done")
        kst_done = sem("kst_done")
        att_done = sem("att_done")
        masked_done = sem("masked_done")
        ds_done = sem("ds_done")
        lower_rows = sem("lower_rows")
        states_done = sem("states_done")
        o_done = sem("o_done")
        osq_done = sem("osq_done")
        osum_done = sem("osum_done")
        orn_done = sem("orn_done")
        m_done = sem("m_done")
        mhi_done = x_hi_done

        B_VT, B_KT, B_AT, B_DS, B_O = bank[3], bank[4], bank[5], bank[6], bank[7]
        tok = [slice(META, META + P), slice(META + P, L)]

        def span(c_):
            if c_ == 0:
                return slice(0, META), slice(0, META), 2
            c1 = c_ - 1
            return (slice(META + CH * c1, META + CH * (c1 + 1)), slice(CH * (c1 % 2), CH * (c1 % 2) + CH), c1 // 2)

        def att_cols(c_):
            return slice(P, P + META) if c_ == 0 else slice(CH * ((c_ - 1) // 2), CH * ((c_ - 1) // 2) + CH)

        def hgrn_tensor(te, ch):
            te.wait_ge(inputs_in, IN_ALL)
            for k in range(4):
                te.wait_ge(sq_done, k + 1)
                for kk in range(4):
                    last = te.matmul(SUM[:, 0:L], con("ones"), sqi[:, 4 * k + kk, :], start=(k + kk == 0),
                                     stop=(k + kk == 6))
            last.then_inc(sum_done, 1)
            te.wait_ge(x_split, SPLITS[T_HGRN])

            def body(h):
                t = [Tile(T_HGRN, h, s) for s in range(4)]
                p = h - 1
                if within(h, HEADS):
                    project(te, t[0], xa, cols_all)
                if within(h - 2, HEADS):
                    te.wait_ge(osq_done, h - 1)
                    te.matmul(SUM[:, 0:L], con("ones"), g.osq[:], start=True, stop=True).then_inc(osum_done, 1)
                if within(p, HEADS):
                    te.wait_ge(evacuated, 4 * p + 3)
                    need(te, v_done, p)
                    for n, cs in enumerate(tok):
                        te.transpose(B_VT[:, n * P:(n + 1) * P], g.vr[:, cs], con("ident"))
                    te.transpose(B_VT[0:META, 2 * P:3 * P], g.vr[:, 0:META], con("ident")).then_inc(vT_done, 1)
                if within(h, HEADS):
                    project(te, t[1], xa, cols_all)
                if within(p, HEADS):
                    te.wait_ge(factors_done, h)
                    need(te, kst_done, p)
                    te.transpose(B_KT[:, 0:P], g.ks[:, tok[0]], con("ident"))
                    te.transpose(B_KT[0:CH, P:2 * P], g.ks[:, META + P:META + P + CH], con("ident"))
                    te.transpose(B_KT[0:META, 2 * P:3 * P], g.ks[:, 0:META], con("ident")).then_inc(kT_done, 1)
                    need(te, masked_done, p)
                    for c_ in range(NCH + 1):
                        cs, rows, _ = span(c_)
                        last = te.matmul(B_AT[rows, att_cols(c_)], g.ki[:, cs], g.qi[:, cs], start=True, stop=True)
                    last.then_inc(att_done, 1)
                if within(h, HEADS):
                    project(te, t[2], xa, cols_all)
                if within(p, HEADS):
                    te.wait_ge(kst_done, h)
                    te.wait_ge(v_done, h)
                    need(te, states_done, p)
                    te.wait_ge(masked_done, h)
                    need(te, m_done, p)
                    te.matmul(B_O[:, 0:L], zeros_l, g.qe[:], start=True, stop=False)
                    for chs in ((0, 1, 3), (2, 4)):
                        for c_ in chs:
                            cs, rows, n = span(c_)
                            if c_ < NCH:
                                ds = te.matmul(B_DS[:, c_ * P:(c_ + 1) * P], g.kst[rows, n, :], g.v[rows, n, :],
                                               start=True, stop=True)
                                if c_ == 2:
                                    ds.then_inc(ds_done, 1)
                            last = te.matmul(B_O[:, cs], g.v[rows, n, :], g.att[rows, att_cols(c_)], start=False,
                                             stop=False)
                        if chs[0] == 0:
                            last.then_inc(lower_rows, 1)
                            te.wait_ge(lower_rows, h)
                if within(h, HEADS):
                    project(te, t[3], xa, cols_all)
                if within(p, HEADS):
                    te.wait_ge(states_done, h)
                    for c_ in range(1, NCH + 1):
                        cs, _, _ = span(c_)
                        last = te.matmul(B_O[:, cs], g.state[:, c_ - 1, :], g.qe[:, cs], start=False,
                                         stop=(c_ == NCH))
                    last.then_inc(o_done, 1)
            ch.run(body, 2, HEADS, 2)

        def hgrn_scalar(act, ch):
            act.wait_ge(inputs_in, IN_ALL)
            act.wait_ge(preset, 2)
            act.activation(g.tmp[:, 0:2, :], g.tmp[:, 2:4, :], ACT.Exp).then_inc(act_chain, 1)
            ch.n += 1
            for k in range(4):
                act.activation(sqi[:, 4 * k:4 * k + 4, :], hT[:, 4 * k:4 * k + 4, :], ACT.Square)\
                    .then_inc(sq_done, 1)
                for kk in range(4 * k, 4 * k + 4):
                    act.activation(xa[0][:, kk, :], hT[:, kk, :], ACT.Copy, scale=par("a_norm", kk))\
                        .then_inc(x_hi_done, 1)
                if k == 0:
                    split_hi(act, Tile(T_HGRN, 0, 0))
            act.wait_ge(sum_done, 1)
            act.activation(root[:], SUM[:, 0:L], ACT.Sqrt, bias=con("eps"), scale=1.0 / D).then_inc(root_done, 1)

            def body(h):
                t = [Tile(T_HGRN, h, s) for s in range(4)]
                p = h - 1
                if within(h, HEADS):
                    split_hi(act, t[0].next())
                if within(h - 2, HEADS):
                    act.wait_ge(o_done, h - 1)
                    act.activation(g.osq[:], B_O[:, 0:L], ACT.Square).then_inc(osq_done, 1)
                if within(p, HEADS):
                    act.wait_ge(evacuated, 4 * p + 4)
                    act.activation(g.sq_f[:], g.fr[:], ACT.Sigmoid).then_inc(gates_done, 1)
                    act.activation(g.sq_q[:], g.qr[:], ACT.Sigmoid)
                    act.activation(g.sq_z[:], g.zr[:], ACT.Sigmoid).then_inc(gates_done, 1)
                    act.wait_ge(fg_done, h)
                    act.activation(g.logf[:], g.fg[:], ACT.Ln).then_inc(logf_done, 1)
                if within(h, HEADS):
                    split_hi(act, t[1].next())
                if within(p, HEADS):
                    act.wait_ge(vT_done, h)
                    act.activation(g.v[:, 0:2, :], B_VT[:, 0:2 * P].rearrange("p (a b) -> p a b", a=2), ACT.Copy)
                    act.activation(g.v[0:META, 2, :], B_VT[0:META, 2 * P:3 * P], ACT.Copy).then_inc(v_done, 1)
                    act.wait_ge(cum_done, h)
                    act.activation(g.e_mid[:], g.dmid[:], ACT.Exp)
                    act.activation(g.e_nmid[:], g.dmid[:], ACT.Exp, scale=-1.0)
                    act.activation(g.e_cum[:], g.cum[:], ACT.Exp)
                    act.activation(g.e_last[:], g.dlast[:], ACT.Exp, scale=-1.0).then_inc(exps_done, 1)
                if within(h - 2, HEADS):
                    act.wait_ge(osum_done, h - 1)
                    ch.link(act.activation(g.lnv[:], SUM[:, 0:L], ACT.Ln, bias=con("eps"), scale=1.0 / P))
                    act.activation(g.rn[:], g.lnv[:], ACT.Exp, scale=-0.5).then_inc(orn_done, 1)
                if within(h, HEADS):
                    split_hi(act, t[2].next())
                if within(p, HEADS):
                    act.wait_ge(kT_done, h)
                    act.activation(g.kst[:, 0, :], B_KT[:, 0:P], ACT.Copy)
                    act.activation(g.kst[0:CH, 1, :], B_KT[0:CH, P:2 * P], ACT.Copy)
                    act.activation(g.kst[0:META, 2, :], B_KT[0:META, 2 * P:3 * P], ACT.Copy).then_inc(kst_done, 1)
                if within(h - 2, HEADS):
                    act.wait_ge(m_done, h - 1)
                    lone(act)
                    act.activation(at3(xb[0], h - 2), one3(g.mm[:]), ACT.Copy).then_inc(mhi_done, 1)
                if within(h, HEADS):
                    split_hi(act, t[3].next())
            ch.run(body, 2, HEADS, 2)

        def chunks(ap):
            return ap[:, META:L].rearrange("p (c t) -> p c t", t=CH)

        def hgrn_vector(ve, ch):
            ve.memset(zt[:], 0.0).then_inc(preset, 1)
            ve.memset(g.att[:], 0.0)
            ve.wait_ge(inputs_in, IN_ALL)
            ch.link(ve.tensor_tensor(g.tmp[:, 0, :], par("gamma0", 0, KT), par("gamma1", 0, KT), ALU.max))
            ve.tensor_tensor(g.tmp[:, 2, :], par("gamma0", 0, KT), g.tmp[:, 0, :], ALU.subtract)
            ve.tensor_tensor(g.tmp[:, 3, :], par("gamma1", 0, KT), g.tmp[:, 0, :], ALU.subtract).then_inc(preset, 1)
            for k in range(KT):
                if k == 4:
                    split_lo(ve, Tile(T_HGRN, 0, 0), 0)
                ve.wait_ge(x_hi_done, k + 1)
                ve.scalar_tensor_tensor(xa[1][:, k, :], hT[:, k, :], par("a_norm", k), xa[0][:, k, :].bitcast(F32),
                                        ALU.mult, ALU.subtract).then_inc(x_split, 1)
            ve.wait_ge(act_chain, 1)
            ch.link(ve.tensor_tensor(g.tmp[:, 2, :], g.tmp[:, 0, :], g.tmp[:, 1, :], ALU.add))
            ch.link(ve.reciprocal(g.tmp[:, 3, :], g.tmp[:, 2, :]))
            ch.link(ve.tensor_tensor(g.lb[:], g.tmp[:, 0, :], g.tmp[:, 3, :], ALU.mult))
            ch.link(ve.tensor_scalar(g.oml[:], g.lb[:], -1.0, 1.0, ALU.mult, ALU.add))
            ve.wait_ge(root_done, 1)
            ch.link(ve.reciprocal(rinv[:], root[:]))

            def evac(t, dst):
                landed(ve, t)
                ve.tensor_tensor(dst[:], proj_ps(t, L), rinv[:], ALU.mult).then_inc(evacuated, 1)

            def body(h):
                t = [Tile(T_HGRN, h, s) for s in range(4)]
                p = h - 1
                if within(p, HEADS):
                    evac(Tile(T_HGRN, p, 3), g.zr)
                if within(h, HEADS):
                    split_lo(ve, t[0].next(), 0)
                if within(p, HEADS):
                    ve.wait_ge(gates_done, 2 * h - 1)
                    ch.link(ve.tensor_scalar(g.fg[:], g.sq_f[:], g.oml[:, bass.ds(p, 1)], g.lb[:, bass.ds(p, 1)],
                                             ALU.mult, ALU.add))
                    ve.tensor_scalar(g.kk[:], g.fg[:], -1.0, 1.0, ALU.mult, ALU.add).then_inc(fg_done, 1)
                    ve.wait_ge(gates_done, 2 * h)
                    ve.tensor_tensor(g.qs[:], g.qr[:], g.sq_q[:], ALU.mult)
                    ve.wait_ge(logf_done, h)
                    ch.link(ve.tensor_tensor_scan(g.cum[:], g.mask[:, MASK_H:TAB_H], g.logf[:], 0.0, ALU.mult, ALU.add))
                    ve.tensor_copy(g.dmid[:, 0:META], g.cum[:, 0:META])
                    cc = chunks(g.cum)
                    ve.tensor_tensor(chunks(g.dmid), cc, cc[:, :, MID:MID + 1].broadcast_to([P, NCH, CH]),
                                     ALU.subtract)
                    ve.tensor_scalar(g.dlast[:, 0:META], g.cum[:, 0:META], g.cum[:, META - 1:META], None,
                                     ALU.subtract)
                    ve.tensor_tensor(chunks(g.dlast), cc, cc[:, :, CH - 1:CH].broadcast_to([P, NCH, CH]),
                                     ALU.subtract).then_inc(cum_done, 1)
                if within(h, HEADS):
                    evac(t[0], g.qr)
                    split_lo(ve, t[1].next(), 0)
                if within(p, HEADS):
                    ve.wait_ge(exps_done, h)
                    ve.tensor_tensor(g.ks[:], g.kk[:], g.e_last[:], ALU.mult)
                    ve.tensor_tensor(g.ki[:], g.kk[:], g.e_nmid[:], ALU.mult)
                    ve.tensor_tensor(g.qi[:], g.qs[:], g.e_mid[:], ALU.mult)
                    ve.tensor_tensor(g.qe[:], g.qs[:], g.e_cum[:], ALU.mult).then_inc(factors_done, 1)
                if within(h - 2, HEADS):
                    ve.wait_ge(orn_done, h - 1)
                    ch.link(ve.scalar_tensor_tensor(g.on[:], B_O[:, 0:L], par("a_out_norm", h - 2), g.rn[:],
                                                    ALU.mult, ALU.mult))
                    ve.tensor_tensor(g.mm[:], g.on[:], g.zs[:], ALU.mult).then_inc(m_done, 1)
                if within(h, HEADS):
                    evac(t[1], g.fr)
                    split_lo(ve, t[2].next(), 0)
                if within(p, HEADS):
                    ve.wait_ge(att_done, h)
                    lone(ve)
                    ve.copy_predicated(g.att[:, 0:P], g.mask[:, 0:P].bitcast(U32), B_AT[:, 0:P])
                    ve.copy_predicated(g.att[0:META, P:MASK_H], g.mask[0:META, P:MASK_H].bitcast(U32),
                                       B_AT[0:META, P:MASK_H]).then_inc(masked_done, 1)
                if within(h - 2, HEADS):
                    ve.wait_ge(mhi_done, 16 + h - 1)
                    ve.tensor_tensor(at3(xb[1], h - 2), one3(g.mm[:]), at3(xb[0], h - 2).bitcast(F32),
                                     ALU.subtract).then_inc(x_split, 1)
                if within(p, HEADS):
                    ve.tensor_tensor(g.zs[:], g.zr[:], g.sq_z[:], ALU.mult)
                if within(h, HEADS):
                    evac(t[2], g.vr)
                    split_lo(ve, t[3].next(), 0)
                if within(p, HEADS):
                    ve.wait_ge(ds_done, h)
                    ch.link(ve.tensor_copy(g.state[:, 0, :], B_DS[:, 0:P]))
                    for c_ in range(1, NCH):
                        end = META + CH * c_ - 1
                        ins = ve.scalar_tensor_tensor(g.state[:, c_, :], g.state[:, c_ - 1, :],
                                                      g.e_cum[:, end:end + 1], B_DS[:, c_ * P:(c_ + 1) * P],
                                                      ALU.mult, ALU.add)
                        if c_ < NCH - 1:
                            ch.link(ins)
                    ins.then_inc(states_done, 1)
            ch.run(body, 2, HEADS, 2)

        def hgrn_pool(po, ch):
            split_lo(po, Tile(T_HGRN, 0, 0), 1)

            def body(h):
                for s in range(4):
                    split_lo(po, Tile(T_HGRN, h, s).next(), 1)
            ch.run(body, 0, HEADS, 0)

        sqi = f.kT

        ksq_done = sem("ksq_done")
        ksum_done = sem("ksum_done")
        krn_done = sem("krn_done")
        kn_done = sem("kn_done")
        fpart = sem("fpart")

        def kv_tensor(te, ch):
            te.wait_ge(x_split, SPLITS[T_KV])

            def body(i):
                for u in range(2):
                    h = 2 * i + u
                    if within(h, HEADS):
                        project(te, Tile(T_KV, i, 2 * u), xa, cols_all)
                        project(te, Tile(T_KV, i, 2 * u + 1), xa, cols_all)
                        te.wait_ge(ksq_done, h + 1)
                        need(te, krn_done, h)
                        te.matmul(SUM[:, 0:L], con("ones"), f.ksq[:], start=True, stop=True).then_inc(ksum_done, 1)
            te.wait_ge(root_done, 2)
            ch.run(body, 0, HEADS // 2, 0)
            project(te, Tile(T_FORGET, 0, 0), xa, cols_all)

        def kv_scalar(act, ch):
            def body(i):
                for u in range(2):
                    h = 2 * i + u
                    tk, tv = Tile(T_KV, i, 2 * u), Tile(T_KV, i, 2 * u + 1)
                    if within(h, HEADS):
                        split_hi(act, tk.next())
                    if within(h - 1, HEADS):
                        act.wait_ge(ksum_done, h)
                        ch.link(act.activation(f.lnv[:], SUM[:, 0:L], ACT.Ln, bias=con("eps"), scale=1.0 / P))
                        act.activation(f.rn[:], f.lnv[:], ACT.Exp, scale=-0.5).then_inc(krn_done, 1)
                    if within(h, HEADS):
                        lone(act)
                        act.activation(at3(xb[0], h), at3(hT, h), ACT.Copy, scale=par("b_norm", h))\
                            .then_inc(x_hi_done, 1)
                        split_hi(act, tv.next())
                        act.wait_ge(evacuated, tk.n + 1)
                        act.activation(f.ksq[:], f.kr[:], ACT.Square).then_inc(ksq_done, 1)
                    if static(h) and h == HEADS:
                        break
            ch.run(body, 1, HEADS // 2, 1)
            split_hi(act, Tile(T_QZ, 0, 0))
            act.wait_ge(evacuated, T_FORGET + 1)
            ch.link(act.activation(f.fa[:], f.fx[:], ACT.Abs, bias=par("b_f", rows=HEADS)))
            ch.link(act.activation(f.fl[:], f.fa[:], ACT.Exp, scale=-1.0))
            act.activation(f.fa[:], f.fl[:], ACT.Ln, bias=con("one", HEADS)).then_inc(fpart, 1)

        def kv_vector(ve, ch):
            def body(i):
                for u in range(2):
                    h = 2 * i + u
                    tk, tv = Tile(T_KV, i, 2 * u), Tile(T_KV, i, 2 * u + 1)
                    if within(h - 1, HEADS):
                        pv_ = Tile(T_KV, i, 2 * u - 1)
                        landed(ve, pv_)
                        ve.tensor_tensor(at3(f.vT, h - 1), one3(proj_ps(pv_, L)), one3(rinv[:]), ALU.mult)\
                            .then_inc(evacuated, 1)
                    if within(h, HEADS):
                        split_lo(ve, tk.next(), 0)
                    if within(h - 1, HEADS):
                        ve.wait_ge(krn_done, h)
                        ve.scalar_tensor_tensor(at3(f.kT, h - 1), one3(f.kr[:]), par("k_norm", h - 1), one3(f.rn[:]),
                                                ALU.mult, ALU.mult).then_inc(kn_done, 1)
                    if within(h, HEADS):
                        landed(ve, tk)
                        need(ve, kn_done, h)
                        ve.tensor_tensor(f.kr[:], proj_ps(tk, L), rinv[:], ALU.mult).then_inc(evacuated, 1)
                        split_lo(ve, tv.next(), 0)
                        ve.wait_ge(x_hi_done, SPLITS[T_KV] + h + 1)
                        ve.scalar_tensor_tensor(at3(xb[1], h), at3(hT, h), par("b_norm", h),
                                                at3(xb[0], h).bitcast(F32), ALU.mult, ALU.subtract)\
                            .then_inc(x_split, 1)
                    if static(h) and h == HEADS:
                        break
            ve.wait_ge(rinv_done, 1)
            ch.run(body, 1, HEADS // 2, 1)
            ve.memset(f.LF[:], 0.0)
            ve.memset(f.RA[:], 0.0)
            tf = Tile(T_FORGET, 0, 0)
            landed(ve, tf)
            ve.tensor_tensor(f.fx[:], bank[tf.q % 2][0:HEADS, 0:L], rinv[0:HEADS, :], ALU.mult).then_inc(evacuated, 1)
            split_lo(ve, tf.next(), 0)
            ve.wait_ge(evacuated, T_FORGET + 1)
            ch.link(ve.tensor_scalar(f.fF[:], f.fx[:], par("b_f", rows=HEADS), 0.0, ALU.add, ALU.min))
            ve.wait_ge(fpart, 1)
            ch.link(ve.tensor_tensor(f.fl[:], f.fF[:], f.fa[:], ALU.subtract))
            ch.link(ve.tensor_tensor_scan(f.fF[:], con_row_ones, f.fl[:], 0.0, ALU.mult, ALU.add))
            ch.link(ve.memset(f.LF[32:32 + HEADS, :], 1.0))
            ve.tensor_copy(f.LF[0:HEADS, :], f.fF[:, META:L])
            ve.memset(f.RA[0:HEADS, :], 1.0)
            ve.tensor_scalar(f.RA[32:32 + HEADS, :], f.fF[:], -1.0, None, ALU.mult)
            ve.tensor_scalar(f.qg[:], par("q_norm", 0, HEADS), float(P) ** -0.5, None, ALU.mult).then_inc(fpart, 1)

        con_row_ones = f.ones[:]

        def kv_pool(po, ch):
            po.memset(f.ones[:], 1.0).then_inc(ones_set, 1)

            def body(i):
                for s in range(4):
                    split_lo(po, Tile(T_KV, i, s).next(), 1)
            ch.run(body, 0, HEADS // 2, 0)
            split_lo(po, Tile(T_QZ, 0, 0), 1)

        qsq_done = sem("qsq_done")
        qsum_done = sem("qsum_done")
        qrn_done = sem("qrn_done")
        qn_done = sem("qn_done")
        aug_done = sem("aug_done")
        vs_done = sem("vs_done")
        zsig_done = sem("zsig_done")
        zz_done = sem("zz_done")
        scores_done = sem("scores_done")
        logits_done = sem("logits_done")
        expp_done = sem("expp_done")
        probs_done = sem("probs_done")
        pt_done = sem("pt_done")
        ptc_done = sem("ptc_done")
        fo_done = sem("fo_done")
        fm_done = sem("fm_done")
        B_SC, B_PT, B_PM, B_FO = bank[3], bank[4], bank[5], bank[6]
        K0 = META + P
        GS = (slice(0, K0), slice(K0, MASK_F))

        def qz_tensor(te, ch):
            te.wait_ge(x_split, SPLITS[T_QZ])
            te.wait_ge(fpart, 2)

            def body(i):
                for u in range(2):
                    h = 2 * i + u
                    if within(h, HEADS):
                        project(te, Tile(T_QZ, i, 2 * u), xb, cols_q)
                    if within(h - 2, HEADS):
                        te.wait_ge(ptc_done, h - 1)
                        need(te, fm_done, h - 2)
                        te.matmul(B_FO[:, 0:SEQ], f.pt[:, 3, :], f.pt[:, 0:2, :], start=True, stop=False)
                        te.matmul(B_FO[:, 0:SEQ], f.pm[:, 2, :], f.pm[:, 0:2, :], start=False, stop=False)
                        te.matmul(B_FO[:, P:SEQ], f.v1[:], f.pt[:, 2, :], start=False, stop=True)\
                            .then_inc(fo_done, 1)
                    if within(h - 1, HEADS):
                        te.wait_ge(qn_done, h)
                        te.wait_ge(aug_done, h)
                        need(te, logits_done, h - 1)
                        for n in range(2):
                            qs = slice(n * P, (n + 1) * P)
                            keys = slice(0, K0) if n == 0 else slice(0, L)
                            te.matmul(one3(B_SC[:, GS[n]]), f.qn[:, qs], at3(f.kT, h - 1, keys), start=True,
                                      stop=False)
                            last = te.matmul(B_SC[:, GS[n]], f.LA[:, qs], f.RA[:, keys], start=False, stop=True)
                        last.then_inc(scores_done, 1)
                    if within(h, HEADS):
                        project(te, Tile(T_QZ, i, 2 * u + 1), xb, cols_q)
                        te.wait_ge(qsq_done, h + 1)
                        need(te, qrn_done, h)
                        te.matmul(SUM[:, 0:SEQ], con("ones"), f.qsq, start=True, stop=True).then_inc(qsum_done, 1)
                    if within(h - 1, HEADS):
                        te.wait_ge(vs_done, h)
                        need(te, ptc_done, h - 1)
                        te.transpose(B_PT[:, 3 * P:4 * P], f.vs[:, META:K0], con("ident"))
                        te.transpose(B_PM[:, 3 * P:4 * P], f.vs[:, K0:L], con("ident"))
                        te.transpose(B_PM[0:META, 2 * P:3 * P], f.vs[:, 0:META], con("ident"))
                        te.wait_ge(probs_done, h)
                        te.transpose(B_PT[:, 0:P], f.pr[:, META:K0], con("ident"))
                        te.transpose(B_PT[:, P:2 * P], f.pr[:, K0 + META:K0 + META + P], con("ident"))
                        te.transpose(B_PT[:, 2 * P:3 * P], f.pr[:, K0 + META + P:MASK_F], con("ident"))
                        te.transpose(B_PM[0:META, 0:P], f.pr[:, 0:META], con("ident"))
                        te.transpose(B_PM[0:META, P:2 * P], f.pr[:, K0:K0 + META], con("ident"))\
                            .then_inc(pt_done, 1)
            ch.run(body, 1, HEADS // 2, 1)

        def qz_scalar(act, ch):
            def body(i):
                for u in range(2):
                    h = 2 * i + u
                    if within(h, HEADS):
                        split_hi(act, Tile(T_QZ, i, 2 * u).next())
                    if within(h - 2, HEADS):
                        act.wait_ge(pt_done, h - 1)
                        need(act, fo_done, h - 2)
                        act.activation(f.pt[:], B_PT[:].rearrange("p (a b) -> p a b", a=4), ACT.Copy)
                        act.activation(f.pm[:], B_PM[0:META, 0:3 * P].rearrange("p (a b) -> p a b", a=3), ACT.Copy)
                        act.activation(f.v1[:], B_PM[:, 3 * P:4 * P], ACT.Copy).then_inc(ptc_done, 1)
                    if within(h - 1, HEADS):
                        act.wait_ge(qsum_done, h)
                        ch.link(act.activation(f.qrn, SUM[:, 0:SEQ], ACT.Ln, bias=con("eps"), scale=1.0 / P))
                        act.activation(f.qrn, f.qrn, ACT.Exp, scale=-0.5).then_inc(qrn_done, 1)
                    if within(h, HEADS):
                        split_hi(act, Tile(T_QZ, i, 2 * u + 1).next())
                        act.wait_ge(evacuated, Tile(T_QZ, i, 2 * u).n + 1)
                        act.activation(f.qsq, f.qr[:], ACT.Square).then_inc(qsq_done, 1)
                    if within(h - 1, HEADS):
                        act.wait_ge(logits_done, h)
                        act.activation(f.pr[:, GS[0]], f.pr[:, GS[0]], ACT.Exp, bias=f.stat[:, 0:1],
                                       accum_out=f.stat[:, 2:3])
                        act.activation(f.pr[:, GS[1]], f.pr[:, GS[1]], ACT.Exp, bias=f.stat[:, 1:2],
                                       accum_out=f.stat[:, 3:4]).then_inc(expp_done, 1)
                        act.activation(f.zsig, f.zr[:], ACT.Sigmoid).then_inc(zsig_done, 1)
                    if within(h - 2, HEADS):
                        act.wait_ge(fm_done, h - 1)
                        lone(act)
                        act.activation(at3(xa[0], h - 2, slice(0, SEQ)), one3(f.mm[:]), ACT.Copy)\
                            .then_inc(x_hi_done, 1)
            ch.run(body, 1, HEADS // 2, 1)

        def qz_vector(ve, ch):
            def body(i):
                for u in range(2):
                    h = 2 * i + u
                    tq, tz = Tile(T_QZ, i, 2 * u), Tile(T_QZ, i, 2 * u + 1)
                    if within(h - 1, HEADS):
                        tp = Tile(T_QZ, i, 2 * u - 1)
                        landed(ve, tp)
                        need(ve, zz_done, h - 1)
                        ve.tensor_tensor(f.zr[:], proj_ps(tp, SEQ), rinv[:, cols_q], ALU.mult).then_inc(evacuated, 1)
                    if within(h, HEADS):
                        split_lo(ve, tq.next(), 0)
                    if within(h - 1, HEADS):
                        ve.wait_ge(qrn_done, h)
                        need(ve, scores_done, h - 1)
                        ve.scalar_tensor_tensor(f.qn[:], f.qr[:], f.qg[:, bass.ds(h - 1, 1)], f.qrn,
                                                ALU.mult, ALU.mult).then_inc(qn_done, 1)
                    if within(h, HEADS):
                        landed(ve, tq)
                        need(ve, qn_done, h)
                        ve.tensor_tensor(f.qr[:], proj_ps(tq, SEQ), rinv[:, cols_q], ALU.mult).then_inc(evacuated, 1)
                        split_lo(ve, tz.next(), 0)
                    if within(h - 1, HEADS):
                        ve.wait_ge(scores_done, h)
                        need(ve, pt_done, h - 1)
                        ch.link(ve.tensor_tensor(f.pr[:], B_SC[:, 0:MASK_F], f.mask[:], ALU.add))
                        ve.tensor_reduce(f.stat[:, 0:1], f.pr[:, GS[0]], AX_X, ALU.max, negate=True)
                        ve.tensor_reduce(f.stat[:, 1:2], f.pr[:, GS[1]], AX_X, ALU.max, negate=True)\
                            .then_inc(logits_done, 1)
                    if within(h - 2, HEADS):
                        ve.wait_ge(fo_done, h - 1)
                        need(ve, zz_done, h - 1)
                        ve.wait_ge(x_split, SPLITS[T_QZ] + h - 2)
                        ve.tensor_tensor(f.mm[:], B_FO[:, 0:SEQ], f.zz[:], ALU.mult).then_inc(fm_done, 1)
                    if within(h - 1, HEADS):
                        ve.wait_ge(expp_done, h)
                        ch.link(ve.reciprocal(f.stat[:, 4:6], f.stat[:, 2:4]))
                        ve.tensor_scalar(f.pr[:, GS[0]], f.pr[:, GS[0]], f.stat[:, 4:5], None, ALU.mult)
                        ve.tensor_scalar(f.pr[:, GS[1]], f.pr[:, GS[1]], f.stat[:, 5:6], None, ALU.mult)\
                            .then_inc(probs_done, 1)
                        ve.wait_ge(zsig_done, h)
                        ve.tensor_tensor(f.zz[:], f.zr[:], f.zsig, ALU.mult).then_inc(zz_done, 1)
                    if within(h - 2, HEADS):
                        ve.wait_ge(x_hi_done, SPLITS[T_QZ] + h - 1)
                        ve.tensor_tensor(at3(xa[1], h - 2, slice(0, SEQ)), one3(f.mm[:]),
                                         at3(xa[0], h - 2, slice(0, SEQ)).bitcast(F32), ALU.subtract)\
                            .then_inc(x_split, 1)
            ch.run(body, 1, HEADS // 2, 1)

        def qz_pool(po, ch):
            po.wait_ge(fpart, 2)
            po.wait_ge(kn_done, HEADS)

            def body(i):
                for u in range(2):
                    h = 2 * i + u
                    if within(h, HEADS):
                        split_lo(po, Tile(T_QZ, i, 2 * u).next(), 1)
                    if within(h - 1, HEADS):
                        need(po, scores_done, h - 1)
                        po.tensor_tensor(f.LA[:], f.LF[:], con_onehot(h - 1).broadcast_to([P, SEQ]), ALU.mult).then_inc(aug_done, 1)
                        need(po, pt_done, h - 1)
                        po.tensor_copy(one3(f.vs[:]), at3(f.vT, h - 1)).then_inc(vs_done, 1)
                    if within(h, HEADS):
                        split_lo(po, Tile(T_QZ, i, 2 * u + 1).next(), 1)
                    if static(h) and h == HEADS:
                        break
            ch.run(body, 1, HEADS // 2, 1)

        def con_onehot(h):
            return consts[:, bass.ds(CONSTS["onehot"][0] + h, 1)]

        csig_done = sem("csig_done")
        hconv_done = sem("hconv_done")
        cv_done = sem("cv_done")

        def conv_tensor(te, ch):
            te.wait_ge(x_split, SPLITS[T_CONV])

            def body(i):
                for s in range(4):
                    project(te, Tile(T_CONV, i, s), xb, slice(0, SEQ))
            ch.run(body, 0, CONV_T // 2, 0)

        def conv_scalar(act, ch):
            def body(i):
                for u in range(2):
                    j = 2 * i + u
                    if within(j, CONV_T):
                        split_hi(act, Tile(T_CONV, i, 2 * u).next())
                    if within(j - 1, CONV_T):
                        act.wait_ge(evacuated, Tile(T_CONV, i, 2 * u).n)
                        need(act, hconv_done, j - 1)
                        act.activation(c.sg[:], c.gr[:], ACT.Sigmoid, bias=par("b_in", CONV_T + j - 1))\
                            .then_inc(csig_done, 1)
                    if within(j, CONV_T):
                        split_hi(act, Tile(T_CONV, i, 2 * u + 1).next())
            ch.run(body, 1, CONV_T // 2, 0)

        def conv_steps(ve, ch, i, u, first):
            j = 2 * i + u
            if first:
                ve.wait_ge(csig_done, j)
                ve.scalar_tensor_tensor(c.hc[:, TAPS - 1:], c.ar[:], par("b_in", j - 1), c.sg[:], ALU.add, ALU.mult)\
                    .then_inc(hconv_done, 1)
                ch.link(ve.tensor_copy(c.wt[:, 0:TAPS], par("conv_w", (j - 1) * TAPS, TAPS)))
                ch.link(ve.tensor_scalar(c.acc[:], c.hc[:, 0:SEQ], c.wt[:, 0:1], par("conv_b", j - 1),
                                         ALU.mult, ALU.add))
                for k in range(1, 15):
                    ch.link(ve.scalar_tensor_tensor(c.acc[:], c.hc[:, k:k + SEQ], c.wt[:, k:k + 1], c.acc[:],
                                                    ALU.mult, ALU.add))
            else:
                for k in range(15, TAPS - 1):
                    ch.link(ve.scalar_tensor_tensor(c.acc[:], c.hc[:, k:k + SEQ], c.wt[:, k:k + 1], c.acc[:],
                                                    ALU.mult, ALU.add))
                ve.scalar_tensor_tensor(at3(c.cv, j - 1), one3(c.hc[:, TAPS - 1:]), c.wt[:, TAPS - 1:TAPS],
                                        one3(c.acc[:]), ALU.mult, ALU.add).then_inc(cv_done, 1)

        def conv_vector(ve, ch):
            ve.memset(c.hc[:], 0.0)
            ve.wait_ge(rinv_done, 2)

            def body(i):
                for u in range(2):
                    j = 2 * i + u
                    ta = Tile(T_CONV, i, 2 * u)
                    if within(j - 1, CONV_T):
                        tp = Tile(T_CONV, i, 2 * u - 1)
                        landed(ve, tp)
                        need(ve, csig_done, j - 1)
                        ve.tensor_tensor(c.gr[:], proj_ps(tp, SEQ), rinv[:, 0:SEQ], ALU.mult).then_inc(evacuated, 1)
                        conv_steps(ve, ch, i, u, True)
                    if within(j, CONV_T):
                        landed(ve, ta)
                        ve.tensor_tensor(c.ar[:], proj_ps(ta, SEQ), rinv[:, 0:SEQ], ALU.mult).then_inc(evacuated, 1)
                    if within(j - 1, CONV_T):
                        conv_steps(ve, ch, i, u, False)
                    if static(j) and j == CONV_T:
                        break
            ch.run(body, 1, CONV_T // 2, 0)

        def conv_pool(po, ch):
            po.wait_ge(w_lo_done[0], T_CONV + 1)
            def body(i):
                for s in range(4):
                    for half in range(2):
                        split_lo(po, Tile(T_CONV, i, s).next(), half)
            ch.run(body, 0, CONV_T // 2, 0)

        NQ = 8
        NSLOT = 2 + NQ
        S = Named()
        (S.k_bias, S.k_sum, S.k_rn, S.k_n, S.k_rot, S.v_bias, S.v_tr, S.v_copy, S.q_bias, S.q_sum, S.q_rn, S.q_n,
         S.q_rot, S.q_f, S.sc, S.mx, S.ex, S.pr, S.tr, S.trc, S.o, S.m, S.mean, S.mu, S.cen, S.csq, S.var, S.rstd,
         S.ct, S.cy, S.cm, S.table) = (
            sem("s_" + name) for name in ("k_bias", "k_sum", "k_rn", "k_n", "k_rot", "v_bias", "v_tr", "v_copy",
                                          "q_bias", "q_sum", "q_rn", "q_n", "q_rot", "q_f", "sc", "mx", "ex", "pr",
                                          "tr", "trc", "o", "m", "mean", "mu", "cen", "csq", "var", "rstd", "ct",
                                          "cy", "cm", "table"))
        B_RO, B_SA, B_SB, B_TA, B_TB = bank[3], bank[4], bank[5], bank[6], bank[7]
        B_SCS, B_TR = (B_SA, B_SB), (B_TA, B_TB)
        half_p = (slice(0, HD), slice(HD, P))

        def swa_tensor(te, ch):
            for s in range(NSLOT + 6):
                if s < NSLOT:
                    project(te, Tile(T_SWK, 0, s), xb, slice(0, SEQ))
                if s == 1:
                    te.wait_ge(S.k_bias, 1)
                    te.matmul(SUM[:, 0:SEQ], c.mask[:, MASK_S + P:TAB_S], c.ksq[:], start=True, stop=True).then_inc(S.k_sum, 1)
                if s == 2:
                    te.wait_ge(S.k_n, 1)
                    te.matmul(B_RO[:, 0:SEQ], c.mask[:, MASK_S:MASK_S + P], c.kn[:], start=True, stop=True).then_inc(S.k_rot, 1)
                    te.wait_ge(S.v_bias, 1)
                    for n in range(2):
                        last = te.transpose(B_SB[:, n * P:(n + 1) * P], c.v1[:, n * P:(n + 1) * P], con("ident"))
                    last.then_inc(S.v_tr, 1)
                    te.wait_ge(cv_done, CONV_T)
                    for k in range(CONV_T):
                        last = te.matmul(B_TB[:, 0:SEQ], con("ones"), c.cv[:, k, :], start=(k == 0),
                                         stop=(k == CONV_T - 1))
                    last.then_inc(S.mean, 1)
                if s == 4:
                    for k in range(CONV_T):
                        te.wait_ge(S.csq, k + 1)
                        te.matmul(B_TA[:, 0:SEQ], con("ones"), c.csqs[k % 2], start=(k == 0),
                                  stop=(k == CONV_T - 1)).then_inc(S.var, 1)
                j = s - 7
                if 0 <= j < NQ:
                    te.wait_ge(S.trc, j + 1)
                    need(te, S.m, j)
                    te.wait_ge(S.q_f, min(j + 3, NQ))
                    for hh in range(2):
                        o = B_RO[half_p[hh], SEQ:2 * SEQ]
                        vv = [c.v[:, n, half_p[hh]] for n in range(2)]
                        te.matmul(o[:, 0:SEQ], vv[0], c.pt[hh][:, 0:2, :], start=True, stop=False)
                        last = te.matmul(o[:, P:SEQ], vv[1], c.pt[hh][:, 2, :], start=False, stop=True)
                    last.then_inc(S.o, 1)
                j = s - 3
                if 0 <= j < NQ:
                    te.wait_ge(S.q_bias, j + 1)
                    need(te, S.q_rn, j)
                    if j == 0:
                        te.wait_ge(S.k_rn, 1)
                    te.matmul(SUM[:, 0:SEQ], c.mask[:, MASK_S + P:TAB_S], c.qsq[:], start=True, stop=True).then_inc(S.q_sum, 1)
                j = s - 4
                if 0 <= j < NQ:
                    te.wait_ge(S.q_n, j + 1)
                    if j == 0:
                        te.wait_ge(S.q_f_k, 1)
                    need(te, S.q_f, j)
                    need(te, S.m, j - 3)
                    te.matmul(B_RO[:, 0:SEQ], c.mask[:, MASK_S:MASK_S + P], c.qn[:], start=True, stop=True).then_inc(S.q_rot, 1)
                j = s - 5
                if 0 <= j < NQ:
                    te.wait_ge(S.q_f, j + 1)
                    need(te, S.mx, j)
                    te.wait_ge(S.v_copy, 1)
                    for hh in range(2):
                        hp = half_p[hh]
                        te.matmul(B_SCS[hh][:, 0:P], c.qf[hp, 0:P], c.kf[hp, 0:P], start=True, stop=True)
                        last = te.matmul(B_SCS[hh][:, P:3 * P], c.qf[hp, P:SEQ], c.kf[hp, :], start=True, stop=True)
                    last.then_inc(S.sc, 1)
                j = s - 6
                if 0 <= j < NQ:
                    te.wait_ge(S.pr, j + 1)
                    te.wait_ge(S.rstd, 1)
                    need(te, S.trc, j)
                    for hh in range(2):
                        for n in range(3):
                            last = te.transpose(B_TR[hh][:, n * P:(n + 1) * P], c.pr[hh][:, n * P:(n + 1) * P],
                                                con("ident"))
                    last.then_inc(S.tr, 1)

        def swa_scalar(act, ch):
            for s in range(NSLOT + 6):
                if s < NSLOT:
                    split_hi(act, Tile(T_SWK, 0, s).next())
                if s == 0:
                    act.wait_ge(evacuated, T_SWK)
                    act.wait_ge(hconv_done, CONV_T - 1)
                    act.activation(c.sg[:], c.gr[:], ACT.Sigmoid, bias=par("b_in", 2 * CONV_T - 1))\
                        .then_inc(csig_done, 1)
                    act.wait_ge(S.table, 1)
                    act.activation(c.sin[:], c.t1[:], ACT.Sin)
                    act.activation(c.cos[:], c.mm[:], ACT.Sin).then_inc(S.table, 1)
                if s == 1:
                    act.wait_ge(evacuated, T_SWK + 1)
                    act.activation(c.k1[:], c.kr[:], ACT.Identity, bias=par("b_in", 24))
                    act.activation(c.ksq[:], c.kr[:], ACT.Square, bias=par("b_in", 24)).then_inc(S.k_bias, 1)
                if s == 2:
                    act.wait_ge(evacuated, T_SWK + 2)
                    act.activation(c.v1[:], c.vr[:], ACT.Identity, bias=par("b_in", 25)).then_inc(S.v_bias, 1)
                    act.wait_ge(S.k_sum, 1)
                    ch.link(act.activation(c.kln[:], SUM[:, 0:SEQ], ACT.Ln, bias=con("eps"), scale=1.0 / HD))
                    act.activation(c.krn[:], c.kln[:], ACT.Exp, scale=-0.5).then_inc(S.k_rn, 1)
                if s == 3:
                    act.wait_ge(S.mean, 1)
                    act.activation(c.mu[:], B_TB[:, 0:SEQ], ACT.Copy, scale=1.0 / (CONV_T * P)).then_inc(S.mu, 1)
                    act.wait_ge(S.v_tr, 1)
                    act.activation(c.v[:], B_SB[:, 0:2 * P].rearrange("p (a b) -> p a b", a=2), ACT.Copy)\
                        .then_inc(S.v_copy, 1)
                if s == 4:
                    act.wait_ge(S.cen, 1)
                    for k in range(CONV_T):
                        need(act, S.var, k - 1)
                        act.activation(c.csqs[k % 2], c.cv[:, k, :], ACT.Square).then_inc(S.csq, 1)
                if s == 5:
                    act.wait_ge(S.var, CONV_T)
                    ch.link(act.activation(c.lnv[:], B_TA[:, 0:SEQ], ACT.Ln, bias=con("eps"),
                                           scale=1.0 / (CONV_T * P)))
                    act.activation(c.rstd[:], c.lnv[:], ACT.Exp, scale=-0.5).then_inc(S.rstd, 1)
                j = s - 4
                if 0 <= j < NQ:
                    act.wait_ge(S.q_sum, j + 1)
                    ch.link(act.activation(c.qln[:], SUM[:, 0:SEQ], ACT.Ln, bias=con("eps"), scale=1.0 / HD))
                    act.activation(c.qrn[:], c.qln[:], ACT.Exp, scale=-0.5).then_inc(S.q_rn, 1)
                j = s - 3
                if 0 <= j < NQ:
                    act.wait_ge(evacuated, T_SWQ + j + 1)
                    need(act, S.q_sum, j)
                    need(act, S.q_n, j)
                    act.activation(c.q1[:], c.qr[:], ACT.Identity, bias=par("b_in", 16 + j))
                    act.activation(c.qsq[:], c.qr[:], ACT.Square, bias=par("b_in", 16 + j)).then_inc(S.q_bias, 1)
                j = s - 6
                if 0 <= j < NQ:
                    act.wait_ge(S.mx, j + 1)
                    for hh in range(2):
                        st_ = c.stat[:, hh, :]
                        for n, cs in enumerate((slice(0, P), slice(P, 3 * P))):
                            act.activation(c.pr[hh][:, cs], c.pr[hh][:, cs], ACT.Exp, bias=st_[:, 2 + n:3 + n],
                                           accum_out=st_[:, 4 + n:5 + n])
                            last = act.activation(st_[:, 6 + n:7 + n], st_[:, 2 + n:3 + n], ACT.Exp,
                                                  bias=par("sinks", j + 8 * hh))
                    last.then_inc(S.ex, 1)
                j = s - 7
                if 0 <= j < NQ:
                    act.wait_ge(S.tr, j + 1)
                    need(act, S.o, j)
                    for hh in range(2):
                        last = act.activation(c.pt[hh][:], B_TR[hh][:, 0:3 * P].rearrange("p (a b) -> p a b", a=3),
                                              ACT.Copy)
                    last.then_inc(S.trc, 1)
                for k in conv_at(s):
                    act.wait_ge(S.ct, k + 1)
                    act.activation(c.cy[:], c.ct[:], ACT.Identity, scale=par("ln_g", k), bias=par("ln_b", k))
                    act.activation(c.csig[:], c.ct[:], ACT.Sigmoid, scale=par("ln_g", k), bias=par("ln_b", k))\
                        .then_inc(S.cy, 1)
                    act.wait_ge(S.cm, k + 1)
                    act.activation(xa[0][:, k, 0:SEQ], c.cm[:], ACT.Copy).then_inc(x_hi_done, 1)
                j = s - 8
                if 0 <= j < NQ:
                    act.wait_ge(S.m, j + 1)
                    act.activation(xa[0][:, CONV_T + j, 0:SEQ], c.mm[:], ACT.Copy).then_inc(x_hi_done, 1)

        def conv_at(s):
            return {6: (0, 1, 2), 7: (3, 4, 5, 6, 7)}.get(s, ())

        def swa_vector(ve, ch):
            xcount = [0]

            def lo_part(tile_k, src):
                xcount[0] += 1
                ve.wait_ge(x_hi_done, SPLITS[T_CONV] + xcount[0])
                ve.tensor_tensor(xa[1][:, tile_k, 0:SEQ], src, xa[0][:, tile_k, 0:SEQ].bitcast(F32),
                                 ALU.subtract).then_inc(x_split, 1)

            for s in range(NSLOT + 6):
                t = Tile(T_SWK, 0, s)
                if s == 0:
                    tp = Tile(T_CONV, 0, 2 * CONV_T - 1)
                    landed(ve, tp)
                    ve.wait_ge(csig_done, CONV_T - 1)
                    ve.tensor_tensor(c.gr[:], proj_ps(tp, SEQ), rinv[:, 0:SEQ], ALU.mult).then_inc(evacuated, 1)
                    two_pi = 2 * np.pi
                    c1 = float(np.float32(6.28125))
                    c2 = float(np.float32(two_pi - c1) - np.float32(two_pi - c1) % np.float32(2.0 ** -20))
                    c3 = float(two_pi - c1 - c2)
                    ch.link(ve.tensor_copy(c.q1[:], c.posi[:]))
                    ch.link(ve.tensor_scalar(c.q1[:], c.q1[:], con("freq"), None, ALU.mult))
                    ch.link(ve.tensor_scalar(c.qn[:], c.q1[:], 1.0 / two_pi, 12582912.0, ALU.mult, ALU.add))
                    ch.link(ve.tensor_scalar(c.qn[:], c.qn[:], -12582912.0, None, ALU.add))
                    for cc in (c1, c2, c3):
                        ch.link(ve.scalar_tensor_tensor(c.q1[:], c.qn[:], -cc, c.q1[:], ALU.mult, ALU.add))
                    ch.link(ve.tensor_scalar(c.t1[:], c.q1[:], 3.1415925, -3.1415925, ALU.min, ALU.max))
                    ve.tensor_scalar(c.mm[:], c.t1[:], 0.5, None, ALU.mult).then_inc(S.table, 1)
                    conv_steps(ve, ch, CONV_T // 2, 0, True)
                if s == 1:
                    landed(ve, Tile(T_SWK, 0, 0))
                    ve.tensor_tensor(c.kr[:], proj_ps(Tile(T_SWK, 0, 0), SEQ), rinv[:, 0:SEQ], ALU.mult)\
                        .then_inc(evacuated, 1)
                    conv_steps(ve, ch, CONV_T // 2, 0, False)
                    ve.wait_ge(S.table, 2)
                    ch.link(ve.tensor_tensor(c.cos[:], c.cos[:], c.cos[:], ALU.mult))
                    ch.link(ve.tensor_scalar(c.cos[:], c.cos[:], -2.0, 1.0, ALU.mult, ALU.add))
                if s == 2:
                    landed(ve, Tile(T_SWV, 0, 0))
                    ve.tensor_tensor(c.vr[:], proj_ps(Tile(T_SWV, 0, 0), SEQ), rinv[:, 0:SEQ], ALU.mult)\
                        .then_inc(evacuated, 1)
                    ve.wait_ge(S.k_rn, 1)
                    ve.scalar_tensor_tensor(c.kn[:], c.k1[:], par("swk_g"), c.krn[:], ALU.mult, ALU.mult)\
                        .then_inc(S.k_n, 1)
                    ch.link(ve.tensor_scalar(c.wt[:, TAPS:TAPS + 1], par("swq_g"), HD ** -0.5, None, ALU.mult))
                j = s - 3
                if 0 <= j < NQ:
                    tq = Tile(T_SWQ, 0, j)
                    landed(ve, tq)
                    need(ve, S.q_bias, j)
                    ve.tensor_tensor(c.qr[:], proj_ps(tq, SEQ), rinv[:, 0:SEQ], ALU.mult).then_inc(evacuated, 1)
                j = s - 5
                if 0 <= j < NQ:
                    ve.wait_ge(S.q_rot, j + 1)
                    if j > 0:
                        ve.wait_ge(S.sc, j)
                    rotary(ve, ch, c.qn, c.qf, S.q_f)
                j = s - 4
                if 0 <= j < NQ:
                    ve.wait_ge(S.q_rn, j + 1)
                    ve.scalar_tensor_tensor(c.qn[:], c.q1[:], c.wt[:, TAPS:TAPS + 1], c.qrn[:], ALU.mult, ALU.mult)\
                        .then_inc(S.q_n, 1)
                if s == 3:
                    ve.wait_ge(S.k_rot, 1)
                    rotary(ve, ch, c.kn, c.kf, S.q_f_k)
                    ve.wait_ge(S.mu, 1)
                    ve.tensor_tensor(c.cv[:], c.cv[:], one3(c.mu[:]).broadcast_to([P, CONV_T, SEQ]),
                                     ALU.subtract).then_inc(S.cen, 1)
                j = s - 8
                if 0 <= j < NQ:
                    ve.wait_ge(S.o, j + 1)
                    ve.wait_ge(x_split, SPLITS[T_CONV] + xcount[0])
                    ve.tensor_copy(c.mm[:], B_RO[:, SEQ:2 * SEQ]).then_inc(S.m, 1)
                j = s - 6
                if 0 <= j < NQ:
                    ve.wait_ge(S.sc, j + 1)
                    need(ve, S.tr, j)
                    for hh in range(2):
                        last = ve.tensor_tensor(c.pr[hh][:], B_SCS[hh][:, 0:3 * P], c.mask[:, 0:MASK_S], ALU.add)
                    ch.link(last)
                    for hh in range(2):
                        ve.tensor_reduce(c.stat[:, hh, 0:1], c.pr[hh][:, 0:P], AX_X, ALU.max)
                        last = ve.tensor_reduce(c.stat[:, hh, 1:2], c.pr[hh][:, P:3 * P], AX_X, ALU.max)
                    ch.link(last)
                    for hh in range(2):
                        last = ve.tensor_scalar(c.stat[:, hh, 2:4], c.stat[:, hh, 0:2], par("sinks", j + 8 * hh),
                                                -1.0, ALU.max, ALU.mult)
                    last.then_inc(S.mx, 1)
                j = s - 6
                if 0 <= j < NQ:
                    ve.wait_ge(S.ex, j + 1)
                    ch.link(ve.tensor_tensor(c.stat[:, :, 8:10], c.stat[:, :, 4:6], c.stat[:, :, 6:8], ALU.add))
                    ch.link(ve.reciprocal(c.stat[:, :, 10:12], c.stat[:, :, 8:10]))
                    for hh in range(2):
                        ve.tensor_scalar(c.pr[hh][:, 0:P], c.pr[hh][:, 0:P], c.stat[:, hh, 10:11], None, ALU.mult)
                        last = ve.tensor_scalar(c.pr[hh][:, P:3 * P], c.pr[hh][:, P:3 * P], c.stat[:, hh, 11:12],
                                                None, ALU.mult)
                    last.then_inc(S.pr, 1)
                for k in conv_at(s):
                    if k == 0:
                        ve.wait_ge(S.rstd, 1)
                    if k > 0:
                        ve.wait_ge(S.cy, k)
                    ve.tensor_tensor(c.ct[:], c.cv[:, k, :], c.rstd[:], ALU.mult).then_inc(S.ct, 1)
                    ve.wait_ge(S.cy, k + 1)
                    ve.tensor_tensor(c.cm[:], c.cy[:], c.csig[:], ALU.mult).then_inc(S.cm, 1)
                    lo_part(k, c.cm[:])
                j = s - 8
                if 0 <= j < NQ:
                    lo_part(CONV_T + j, c.mm[:])

        def rotary(ve, ch, src, dst, done):
            ve.tensor_tensor(dst[:], src[:], c.cos[:], ALU.mult)
            ch.link(ve.tensor_tensor(c.t1[:], B_RO[:, 0:SEQ], c.sin[:], ALU.mult))
            ve.tensor_tensor(dst[:], dst[:], c.t1[:], ALU.add).then_inc(done, 1)

        S.q_f_k = sem("s_k_f")
        c.csqs = [c.csq[:], c.acc[:]]

        def swa_pool(po, ch):
            for s in range(NSLOT):
                for half in range(2):
                    split_lo(po, Tile(T_SWK, 0, s).next(), half)

        R = Named()
        (R.q, R.sub, R.top, R.hc, R.tr, R.trc, R.rt, R.rtc, R.head, R.soft) = (
            sem("r_" + name) for name in ("q", "sub", "top", "hc", "tr", "trc", "rt", "rtc", "head", "soft"))
        B_SUB, B_TOK = (bank[3], bank[4]), (bank[5], bank[6])

        def route_tensor(te, ch):
            te.wait_ge(x_split, SPLITS[T_PEERQ])
            te.wait_ge(rinv_done, 3)
            for n in range(2):
                last = te.transpose(bank[7][:, n * P:(n + 1) * P], rinv[:, n * P:(n + 1) * P], con("ident"))
            last.then_inc(R.rt, 1)

            def body(i):
                for s in range(4):
                    j, t = 4 * i + s, Tile(T_PEERQ, i, s)
                    if within(j, 16):
                        project(te, t, xb, slice(0, SEQ))
                        te.wait_ge(R.hc, j + 1)
                        need(te, R.trc, j - 1)
                        bk = B_TOK[s % 2]
                        for n in range(2):
                            te.transpose(bk[:, n * P:(n + 1) * P], r.hc[:, n * P:(n + 1) * P], con("ident"))
                        for n in range(2):
                            last = te.transpose(bk[:, (2 + n) * P:(3 + n) * P], r.gained[:, n * P:(n + 1) * P],
                                                con("ident"))
                        last.then_inc(R.tr, 1)
                    if within(j - 1, 16):
                        te.wait_ge(evacuated, t.n)
                        need(te, R.top, 2 * (j - 2))
                        for n in range(2):
                            last = te.matmul(one3(B_SUB[(s - 1) % 2][:, n * P:(n + 1) * P]),
                                             r.qT[:, n * P:(n + 1) * P], at3(r.keys, j - 1), start=True, stop=True)
                        last.then_inc(R.sub, 1)
                    if static(j) and j == 16:
                        break
            ch.run(body, 1, 4, 1)

        def route_scalar(act, ch):
            act.wait_ge(R.rt, 1)
            ch.link(act.activation(r.rtok[:], bank[7][:, 0:2 * P].rearrange("p (a b) -> p a b", a=2)[:, :, 0:1]
                                   .rearrange("p a b -> p (a b)"), ACT.Copy))

            def body(i):
                for s in range(4):
                    j, t = 4 * i + s, Tile(T_PEERQ, i, s)
                    if within(j, 16):
                        if s < 3 or not (static(i) and i == 3):
                            split_next(act, i, s, split_hi)
                        need(act, R.tr, j)
                        lone(act)
                        act.activation(one3(r.hc[:]), at3(hT, j, cols_q), ACT.Copy)
                        lone(act)
                        act.activation(one3(r.gained[:]), at3(hT, j, cols_q), ACT.Copy, scale=par("norm2", j))\
                            .then_inc(R.hc, 1)
                        act.wait_ge(R.tr, j + 1)
                        bk = B_TOK[s % 2]
                        lone(act)
                        act.activation(e.ytok[:, :, bass.ds(j * P, P)],
                                       bk[:, 0:2 * P].rearrange("p (a b) -> p a b", a=2), ACT.Copy)
                        for n in range(2):
                            lone(act)
                            last = act.activation(e.xtok[:, n, bass.ds(j * P, P)], bk[:, (2 + n) * P:(3 + n) * P],
                                                  ACT.Copy, scale=r.rtok[:, n:n + 1])
                        last.then_inc(R.trc, 1)
            for i in range(4):
                body(i)
            act.wait_ge(R.soft, 1)
            act.activation(e.gate[:], e.gate[:], ACT.Exp).then_inc(R.soft, 1)

        def split_next(eng, i, s, fn):
            t = Tile(T_PEERQ, i, s).next()
            if static(t.n) and t.n >= TILES:
                return
            fn(eng, t)

        def route_vector(ve, ch):
            def head(h):
                for n in range(GROUPS):
                    cand3 = r.cand[:, n, :].rearrange("p (a b) -> p a b", a=TOPK)
                    ch.link(ve.tensor_tensor(
                        cand3, r.top[:, n, 0, :].rearrange("p (a b) -> p a b", b=1).broadcast_to([P, TOPK, TOPK]),
                        r.top[:, n, 1, :].rearrange("p (a b) -> p a b", a=1).broadcast_to([P, TOPK, TOPK]), ALU.add))
                for n in range(GROUPS):
                    top16(ve, ch, r.cand[:, n, :], r.val[:, n, :], r.ci[:, n, :], r.work[:])
                ve.tensor_single_scalar(r.cij[:, 0, :, :], r.ci[:], 4, op=ALU.logical_shift_right)
                ve.tensor_single_scalar(r.cij[:, 1, :, :], r.ci[:], 15, op=ALU.bitwise_and)
                ch.link(ve.tensor_copy(r.topf[:], r.topi[:]))
                ch.link(ve.tensor_copy(r.cf[:], r.cij[:]))
                iota = con("iota").rearrange("p (a b) -> p a b", a=1).broadcast_to([P, TOPK, TOPK])
                for w in range(2):
                    for n in range(GROUPS):
                        last = ve.tensor_tensor(
                            r.oh[:, n, :, :],
                            r.cf[:, w, n, :].rearrange("p (a b) -> p a b", b=1).broadcast_to([P, TOPK, TOPK]),
                            iota, ALU.is_equal)
                    ch.link(last)
                    for n in range(GROUPS):
                        last = ve.tensor_tensor(
                            r.oh[:, n, :, :], r.oh[:, n, :, :],
                            r.topf[:, n, w, :].rearrange("p (a b) -> p a b", a=1).broadcast_to([P, TOPK, TOPK]),
                            ALU.mult)
                    ch.link(last)
                    ch.link(ve.tensor_reduce(r.ex[:, w, :, :], r.oh[:], AX_X, ALU.add))
                ch.link(ve.scalar_tensor_tensor(r.ex[:, 0, :, :], r.ex[:, 0, :, :], 128.0, r.ex[:, 1, :, :],
                                                ALU.mult, ALU.add))
                ve.tensor_copy(e.idx[:, :, bass.ds(h * TOPK, TOPK)], r.ex[:, 0, :, :])
                ch.link(ve.tensor_copy(r.vals[:, :, bass.ds(h * TOPK, TOPK)], r.val[:]))

            def body(i):
                for s in range(4):
                    j, t = 4 * i + s, Tile(T_PEERQ, i, s)
                    if within(j, 16):
                        landed(ve, t)
                        need(ve, R.sub, j)
                        ve.tensor_tensor(r.qT[:], proj_ps(t, SEQ), rinv[:, 0:SEQ], ALU.mult).then_inc(evacuated, 1)
                    if within(j - 1, 16):
                        ve.wait_ge(R.sub, j)
                        w = (s - 1) % 2
                        for n in range(GROUPS):
                            top16(ve, ch, B_SUB[w][:, n * P:(n + 1) * P], r.top[:, n, w, :],
                                         r.topi[:, n, w, :], r.work[:, 0:P], 2 * (j - 1) + n + 1)
                        if w == 1:
                            head((j - 2) // 2 if static(j) else 2 * i + (s - 2) // 2)
                    if static(j) and j == 16:
                        break
            ch.run(body, 1, 4, 1)
            v4 = r.vals[:].rearrange("p g (h k) -> p (g h) k", k=TOPK)
            g4 = e.gate[:].rearrange("p g (h k) -> p (g h) k", k=TOPK)
            ve.tensor_tensor(g4, v4, v4[:, :, 0:1].broadcast_to([P, GROUPS * PEER_HEADS, TOPK]), ALU.subtract)\
                .then_inc(R.soft, 1)
            ve.wait_ge(R.soft, 2)
            ch.link(ve.tensor_reduce(r.st[:, 0, :], g4, AX_X, ALU.add))
            ch.link(ve.reciprocal(r.st[:, 1, :], r.st[:, 0, :]))
            rs = r.st[:, 1, :].rearrange("p (a b) -> p a b", b=1)
            ve.tensor_tensor(g4, g4, rs.broadcast_to([P, GROUPS * PEER_HEADS, TOPK]), ALU.mult).then_inc(R.soft, 1)
            ve.wait_ge(R.soft, 3)

        def top16(ve, ch, src, val, idx, work, bank_read=None):
            lone(ve)
            ch.link(ve.max(val[:, 0:8], src))
            lone(ve)
            ve.max_index(idx[:, 0:8], val[:, 0:8], src)
            replaced = ve.match_replace(work, val[:, 0:8], src, -3.0e38)
            if bank_read is None:
                ch.link(replaced)
            else:
                replaced.then_inc(R.top, 1)
                ve.wait_ge(R.top, bank_read)
            lone(ve)
            ch.link(ve.max(val[:, 8:16], work))
            lone(ve)
            ch.link(ve.max_index(idx[:, 8:16], val[:, 8:16], work))

        def route_pool(po, ch):
            po.wait_ge(w_lo_done[0], T_PEERQ + 1)
            for i in range(4):
                for s in range(4):
                    for half in range(2):
                        split_next(po, i, s, lambda eng, t: split_lo(eng, t, half))

        u_in_s = [sem(f"u_in{i}") for i in range(4)]
        v_in_s = [sem(f"v_in{i}") for i in range(4)]
        u_used = sem("u_used")
        v_used = sem("v_used")
        gelu_done = sem("gelu_done")
        stored = sem("stored")
        QUADS = SLOTS // 4

        def expert_ids(po, n, i, parity, total):
            pass

        def experts_pool(po, ch):
            for n in range(GROUPS):
                if n == 0:
                    po.wait_ge(R.soft, 3)

                def body(i, n=n):
                    for b in range(2):
                        q = 2 * i + b
                        qq = n * QUADS + q
                        need(po, v_used, 4 * (qq - 1))
                        ch.link(po.tensor_copy(e.idn[:, b, :], e.idx[:, n, bass.ds(4 * q, 4)]))
                        for k in range(4):
                            need(po, u_used, 4 * qq + k - 3)
                            lone(po)
                            po.indirect_dma_start(raw[:, k, :], None, u_in,
                                                  bass.IndirectOffsetOnAxis(ap=e.idn[:, b, k:k + 1], axis=0))\
                                .then_inc(u_in_s[k], 16)
                        for k in range(4):
                            need(po, v_used, 4 * qq + k - 3)
                            lone(po)
                            po.indirect_dma_start(vrow[:, k, :], None, v_in,
                                                  bass.IndirectOffsetOnAxis(ap=e.idn[:, b, k:k + 1], axis=0))\
                                .then_inc(v_in_s[k], 16)
                ch.run(body, 0, QUADS // 2, 0)

        def experts_scalar(act, ch):
            for n in range(GROUPS):
                def body(i, n=n):
                    for b in range(2):
                        qq = n * QUADS + 2 * i + b
                        act.wait_ge(u_used, 4 * qq + 4)
                        need(act, v_used, 4 * (qq - 2))
                        act.activation(e.act[:, b, :], e.hid[:, b, :], ACT.Gelu).then_inc(gelu_done, 1)
                ch.run(body, 1, QUADS // 2, 0)

        def experts_vector(ve, ch):
            def use_v(n, qq, b, q):
                ve.wait_ge(gelu_done, qq + 1)
                ch.link(ve.tensor_tensor(e.coef[:, b, :], e.act[:, b, :], e.gate[:, n, bass.ds(4 * q, 4)], ALU.mult))
                for k in range(4):
                    ve.wait_ge(v_in_s[k], 16 * qq + 16)
                    ve.scalar_tensor_tensor(e.ytok[:, n, :], vrow[:, k, :], e.coef[:, b, k:k + 1], e.ytok[:, n, :],
                                            ALU.mult, ALU.add).then_inc(v_used, 1)
                    ve.wait_ge(v_used, 4 * qq + k + 1)

            ve.wait_ge(R.trc, 16)
            for n in range(GROUPS):
                def body(i, n=n):
                    for b in range(2):
                        q = 2 * i + b
                        qq = n * QUADS + q
                        for k in range(4):
                            ve.wait_ge(u_in_s[k], 16 * qq + 16)
                            last = ve.tensor_tensor_reduce(raw[:, k, :], raw[:, k, :], e.xtok[:, n, :], 1.0, 0.0, ALU.mult,
                                                           ALU.add, e.hid[:, b, k:k + 1])
                            last.then_inc(u_used, 1)
                        use_v(n, qq, b, q)
                ch.run(body, 0, QUADS // 2, 0)

        IN_ALL = 16 * 7

        @block.sync
        def _(sp):
            sp.dma_start(params[:], params_in).then_inc(inputs_in, 16)
            sp.dma_start(consts[:], consts_in).then_inc(inputs_in, 16)
            for k in range(4):
                sp.dma_start(hT[:, 4 * k:4 * k + 4, :], hT_in[:, 4 * k:4 * k + 4, :]).then_inc(inputs_in, 16)
                if k == 0:
                    sp.dma_start(raw[:, 0, :], w_in[0]).then_inc(w_loaded[0], 16)
            sp.dma_start(g.mask[:], masks_in[:, 0:TAB_H]).then_inc(inputs_in, 16)
            for q in range(1, 4):
                sp.dma_start(raw[:, q, :], w_in[q]).then_inc(w_loaded[q], 16)

            def weights(n0, n1):
                def load(q, m):
                    n = 4 * m + q
                    for half in range(2):
                        sp.wait_ge(w_lo_done[half], n - 3)
                    sp.dma_start(raw[:, q, :].rearrange("p (a b) -> p a b", a=1),
                                 w_in[bass.ds(n, 1)].rearrange("a p c -> p a c")).then_inc(w_loaded[q], 16)
                while n0 % 4 and n0 < n1:
                    load(n0 % 4, n0 // 4)
                    n0 += 1
                if n1 // 4 > n0 // 4:
                    with sp.Fori(n0 // 4, n1 // 4) as m:
                        for q in range(4):
                            load(q, m)
                for n in range(n1 // 4 * 4, n1):
                    load(n % 4, n // 4)

            weights(4, TILES)
            for n in range(GROUPS):
                sp.wait_ge(v_used, (n + 1) * SLOTS)
                sp.dma_start(out[n * P:(n + 1) * P, :], e.ytok[:, n, :]).then_inc(stored, 16)
            sp.wait_ge(stored, 16 * GROUPS)


        @block.tensor
        def _(te):
            ch = Chain(te, pool_chain)
            te.wait_ge(preset, 1)
            hgrn_tensor(te, ch)
            out_tensor(te, ch, OUT[0])
            kv_tensor(te, ch)
            qz_tensor(te, ch)
            out_tensor(te, ch, OUT[1])
            conv_tensor(te, ch)
            swa_tensor(te, ch)
            out_tensor(te, ch, OUT[2])
            te.wait_ge(masks_r, 16)
            route_tensor(te, ch)

        @block.scalar
        def _(act):
            ch = Chain(act, act_chain)
            hgrn_scalar(act, ch)
            out_scalar(act, ch, OUT[0])
            act.dma_start(f.mask[:], masks_in[:, TAB_H:TAB_H + MASK_F]).then_inc(masks_f, 16)
            kv_scalar(act, ch)
            qz_scalar(act, ch)
            out_scalar(act, ch, OUT[1])
            act.wait_ge(fo_done, HEADS)
            act.dma_start(c.mask[:], masks_in[:, TAB_H + MASK_F:]).then_inc(masks_c, 16)
            act.dma_start(c.posi[:], pos_in.partition_broadcast(P)).then_inc(masks_c, 16)
            conv_scalar(act, ch)
            swa_scalar(act, ch)
            out_scalar(act, ch, OUT[2])
            act.dma_start(r.keys[:], keys_in).then_inc(masks_r, 16)
            route_scalar(act, ch)
            experts_scalar(act, ch)

        @block.vector
        def _(ve):
            ch = Chain(ve, dve_chain)
            hgrn_vector(ve, ch)
            out_vector(ve, ch, OUT[0], (0,))
            ve.wait_ge(ones_set, 1)
            kv_vector(ve, ch)
            ve.wait_ge(masks_f, 16)
            qz_vector(ve, ch)
            out_vector(ve, ch, OUT[1], (0,))
            conv_vector(ve, ch)
            ve.wait_ge(masks_c, 32)
            swa_vector(ve, ch)
            out_vector(ve, ch, OUT[2], (0,))
            route_vector(ve, ch)
            experts_vector(ve, ch)

        @block.gpsimd
        def _(po):
            ch = Chain(po, pool_chain)
            hgrn_pool(po, ch)
            out_pool(po, ch, OUT[0], (1,))
            kv_pool(po, ch)
            qz_pool(po, ch)
            out_pool(po, ch, OUT[1], (1,))
            conv_pool(po, ch)
            swa_pool(po, ch)
            out_pool(po, ch, OUT[2], (1,))
            route_pool(po, ch)
            experts_pool(po, ch)


def kernel(**inputs):
    import concourse.bacc as bacc
    from concourse.bass_utils import run_bass_kernel_spmd

    a = {k: np.asarray(v) for k, v in inputs.items()}

    def cols(v):
        return v.reshape(-1, P).T

    def tiles(w):
        n = w.shape[1] // P
        return w.reshape(KT, P, n, P).transpose(2, 1, 0, 3).reshape(n, P, D)

    def interleave(*ws):
        return np.stack(ws, 1).reshape(-1, P, D)

    w_a = tiles(a["a_w_in"][0])
    kv = a["kv_w"]
    forget = np.zeros((D, P), np.float32)
    forget[:, :HEADS] = kv[:, 2 * D:]
    kvt, bt = tiles(kv[:, :2 * D]), tiles(a["b_w_in"][0])
    qmap = np.concatenate([np.r_[j * HD:(j + 1) * HD, (j + 8) * HD:(j + 9) * HD] for j in range(8)])
    w2, b2 = a["w_in_2"], a["b_in_2"]
    C = CONV_T * P
    q_w, q_b = w2[:, 2 * C:3 * C][:, qmap], b2[2 * C:3 * C][qmap]
    wo2 = np.concatenate([a["w_out_2"][:C], a["w_out_2"][C:][qmap]], 0)
    w_all = np.concatenate([
        interleave(w_a[:16], w_a[16:32], w_a[32:48], w_a[48:]), tiles(a["a_w_out"][0]),
        interleave(kvt[:16], kvt[16:]), tiles(forget), interleave(bt[:16], bt[16:]), tiles(a["b_w_out"][0]),
        interleave(tiles(w2[:, :C]), tiles(w2[:, C:2 * C])), tiles(w2[:, 3 * C:]), tiles(q_w), tiles(wo2),
        tiles(a["peer_w_q_2"])])
    assert w_all.shape[0] == TILES
    pk = np.zeros((P, N_PARAMS), np.float32)

    def put(name, v):
        at, n = PARAMS[name]
        pk[:v.shape[0], at:at + n] = v

    put("a_norm", cols(a["a_norm"][0]))
    put("gamma0", cols(a["gamma_lb"][0]))
    put("gamma1", cols(a["gamma_lb"][1]))
    put("a_out_norm", cols(a["a_out_norm"][0]))
    put("kv_norm", cols(a["kv_norm"]))
    put("k_norm", a["fox_k_norm"].T)
    put("b_norm", cols(a["b_norm"][0]))
    put("q_norm", a["b_q_norm"][0].T)
    put("norm1", cols(a["norm1_g_2"]))
    put("b_in", cols(np.concatenate([b2[:2 * C], q_b, b2[3 * C:]])))
    put("conv_w", a["conv_dw_w_2"].T.reshape(CONV_T, P, TAPS).transpose(1, 0, 2).reshape(P, -1))
    put("conv_b", cols(a["conv_dw_b_2"]))
    put("ln_g", cols(a["conv_ln_g_2"]))
    put("ln_b", cols(a["conv_ln_b_2"]))
    put("swq_g", np.tile(a["q_norm_g_2"], 2)[:, None])
    put("swk_g", np.tile(a["k_norm_g_2"], 2)[:, None])
    put("norm2", cols(a["norm2_g_2"]))
    put("b_f", a["fox_b_f"][:, None])
    put("sinks", np.tile(a["attn_sinks_2"][None], (P, 1)))
    h0 = np.concatenate([a["meta"], a["x"][0]], 0).T.reshape(KT, P, L).transpose(1, 0, 2)
    cst, msk = constants()
    arrays = {
        "hT": h0, "params": pk, "consts": cst, "masks": msk, "pos": a["positions_2"].reshape(SEQ),
        "keys": a["peer_sub_keys_2"].transpose(3, 0, 1, 2).reshape(P, 2 * PEER_HEADS, P),
        "w": w_all, "u": a["peer_u_2"], "v": a["peer_v_2"],
    }
    arrays = {k: np.ascontiguousarray(v) for k, v in arrays.items()}
    nc = bacc.Bacc("TRN2", target_bir_lowering=False, num_devices=1)
    args = [nc.dram_tensor("in_" + k, v.shape, mybir.dt.from_np(v.dtype), kind="ExternalInput").ap()
            for k, v in arrays.items()]
    res = nc.dram_tensor("out", (SEQ, D), F32, kind="ExternalOutput").ap()
    build(nc, *args, res)
    r = run_bass_kernel_spmd(nc, [{"in_" + k: v for k, v in arrays.items()}], core_ids=[0])
    return r.results[0]["out"].reshape(1, SEQ, D)
```

```python
from contextlib import ExitStack

import numpy as np

import concourse.bass as bass
from concourse import mybir

ALU = mybir.AluOpType
ACT = mybir.ActivationFunctionType
F32 = mybir.dt.float32
F32R = mybir.dt.float32r
BF16 = mybir.dt.bfloat16
U32 = mybir.dt.uint32
I32 = mybir.dt.int32
AX_X = mybir.AxisListType.X

P = 128
D = 2048
KT = D // P
META = 16
SEQ = 256
L = META + SEQ
HEADS = 16
EPS = 1e-6
NEG = -1e30

CH = 64
NCH = SEQ // CH
MID = CH // 2 - 1

CONV_T = 8
TAPS = 31
HD = 64
PEER_HEADS = 8
TOPK = 16
SLOTS = PEER_HEADS * TOPK
GROUPS = SEQ // P

T_HGRN = 0
T_AOUT = T_HGRN + 4 * HEADS
T_KV = T_AOUT + KT
T_FORGET = T_KV + 2 * HEADS
T_QZ = T_FORGET + 1
T_BOUT = T_QZ + 2 * HEADS
T_CONV = T_BOUT + KT
T_SWK = T_CONV + 2 * CONV_T
T_SWV = T_SWK + 1
T_SWQ = T_SWV + 1
T_WOUT = T_SWQ + 8
T_PEERQ = T_WOUT + KT
TILES = T_PEERQ + 2 * PEER_HEADS
SUBKEYS = 128
SEGS = 2
SEG = SUBKEYS // SEGS
T_U = [TILES + 2 * SEG * n for n in range(SEGS)]
T_V = [t + SEG for t in T_U]
TILES_ALL = TILES + 2 * SUBKEYS
STEP = 8

PARAMS = {}
_at = 0
for _name, _n in (("a_norm", KT), ("gamma0", KT), ("gamma1", KT), ("a_out_norm", HEADS), ("kv_norm", KT),
                  ("k_norm", HEADS), ("b_norm", KT), ("q_norm", HEADS), ("norm1", KT), ("b_in", 26),
                  ("conv_w", CONV_T * TAPS), ("conv_b", CONV_T), ("ln_g", CONV_T), ("ln_b", CONV_T),
                  ("swq_g", 1), ("swk_g", 1), ("norm2", KT), ("b_f", 1), ("sinks", 16)):
    PARAMS[_name] = (_at, _n)
    _at += _n
N_PARAMS = _at

CONSTS = {}
_at = 0
for _name, _n in (("ident", P), ("ones", P), ("iota", SUBKEYS),
                  ("onehot", HEADS), ("freq", 1), ("eps", 1), ("one", 1)):
    CONSTS[_name] = (_at, _n)
    _at += _n
N_CONSTS = _at
MASK_H = P + META
TAB_H = MASK_H + L
MASK_F = 2 * META + 3 * P
MASK_S = 3 * P
TAB_S = MASK_S + 2 * P


def constants():
    c = np.zeros((P, N_CONSTS), np.float32)

    def put(name, a):
        at, n = CONSTS[name]
        c[:, at:at + n] = a

    r = np.arange(P)
    put("ident", np.eye(P))
    put("ones", 1.0)
    rot = np.zeros((P, P), np.float32)
    freq = np.zeros((P, 1), np.float32)
    inv = (np.float32(500000.0) ** (-np.arange(0, 16, 2, dtype=np.float32) / np.float32(16))).astype(np.float32)
    for base in (0, HD):
        for i in range(8):
            rot[base + 8 + i, base + i] = -1.0
            rot[base + i, base + 8 + i] = 1.0
            freq[base + i] = freq[base + 8 + i] = inv[i]
    put("freq", freq)
    reset = np.ones(L, np.float32)
    reset[0] = 0.0
    reset[META::CH] = 0.0
    put("iota", np.arange(SUBKEYS))
    onehot = np.zeros((P, HEADS), np.float32)
    onehot[r[:HEADS], r[:HEADS]] = 1.0
    onehot[32 + r[:HEADS], r[:HEADS]] = 1.0
    put("onehot", onehot)
    put("eps", EPS)
    put("one", 1.0)
    m = np.zeros((P, TAB_H + MASK_F + TAB_S), np.float32)
    m[:, MASK_H:TAB_H] = reset
    m[:, TAB_H + MASK_F + MASK_S:-P] = rot
    m[:, -P:] = r[:, None] // HD == r[None, :] // HD
    s, t = r[:, None] % CH, np.arange(CH)[None, :]
    m[:, 0:P] = np.tile(s <= t, (1, 2))
    m[:META, P:MASK_H] = r[:META, None] <= r[None, :META]
    k1, k2 = np.arange(META + P)[None, :], np.arange(L)[None, :]
    f = m[:, TAB_H:TAB_H + MASK_F]
    f[:, :META + P] = np.where(k1 <= META + r[:, None], 0.0, NEG)
    f[:, META + P:] = np.where(k2 <= META + P + r[:, None], 0.0, NEG)
    w = m[:, TAB_H + MASK_F:TAB_H + MASK_F + MASK_S]
    kpos = np.arange(P)[None, :]
    w[:, :P] = np.where(kpos <= r[:, None], 0.0, NEG)
    kpos = np.arange(2 * P)[None, :]
    qpos = P + r[:, None]
    w[:, P:] = np.where((kpos <= qpos) & (qpos - kpos < 128), 0.0, NEG)
    return c, m


def static(v):
    return isinstance(v, int)


def need(eng, sem, value):
    if not static(value) or value > 0:
        eng.wait_ge(sem, value)


def within(i, n):
    return not static(i) or 0 <= i < n


class Chain:

    def __init__(self, eng, sem):
        self.eng, self.sem, self.base, self.n = eng, sem, 0, 0

    def link(self, ins):
        ins.then_inc(self.sem, 1)
        self.n += 1
        self.eng.wait_ge(self.sem, self.base + self.n)

    def run(self, body, full, count, tail):
        for i in range(full + 1):
            before = self.n
            body(i)
        per = self.n - before
        total = self.base + self.n
        with self.eng.Fori(full + 1, count) as i:
            self.base, self.n = total + (i - (full + 1)) * per, 0
            body(i)
            assert self.n == per
        self.base, self.n = total + (count - full - 1) * per, 0
        for i in range(count, count + tail):
            body(i)


class Named:
    pass


class Tile:

    def __init__(self, base, i, s):
        self.q = (base + s) % 4
        self.m = i + (base + s) // 4
        self.n = 4 * self.m + self.q

    def next(self):
        t = Tile.__new__(Tile)
        t.q = (self.q + 1) % 4
        t.m = self.m + (self.q == 3)
        t.n = self.n + 1
        return t


def build(nc, hT_in, params_in, consts_in, masks_in, pos_in, keys_in, w_in, u_in, v_in, out):
    with ExitStack() as ctx:
        def sem(name):
            return ctx.enter_context(nc.semaphore(name))

        def tensor(stack, name, shape, dt=F32, **kw):
            return stack.enter_context(nc.sbuf_tensor(name, shape, dt, **kw))

        params = tensor(ctx, "params", [P, N_PARAMS])
        consts = tensor(ctx, "consts", [P, N_CONSTS])
        rinv = tensor(ctx, "rinv", [P, L])
        root = tensor(ctx, "root", [P, L])
        sq2 = tensor(ctx, "sq2", [P, 2, L])
        raw = tensor(ctx, "raw", [P, 4, D])
        zt = tensor(ctx, "zeros", [P, P], F32R)
        token = tensor(ctx, "token", [P, 24])
        whi = tensor(ctx, "whi", [P, 4, D // 2], F32R)
        wlo = tensor(ctx, "wlo", [P, 4, D // 2], F32R)
        hT = tensor(ctx, "hT", [P, KT, L])
        xb = (tensor(ctx, "xb_hi", [P, KT, L], F32R), tensor(ctx, "xb_lo", [P, KT, L], F32R))
        innermost = ExitStack()
        xa = (tensor(innermost, "xa_hi", [P, KT, L], F32R), tensor(innermost, "xa_lo", [P, KT, L], F32R))
        bank = [ctx.enter_context(nc.psum_tensor(f"bank{i}", [P, 512], F32)) for i in range(8)]

        g = Named()
        with ExitStack() as st:
            (g.qr, g.fr, g.vr, g.zr, g.qs, g.fg, g.kk, g.zs, g.sq_q, g.sq_f, g.sq_z, g.logf, g.cum, g.dmid, g.dlast,
             g.e_mid, g.e_nmid, g.e_cum, g.e_last, g.qi, g.ki, g.qe, g.ks, g.osq, g.lnv, g.rn, g.on, g.mm) = (
                tensor(st, "g_" + name, [P, L]) for name in ("qr", "fr", "vr", "zr", "qs", "fg", "kk", "zs", "sq_q",
                                                             "sq_f", "sq_z", "logf", "cum", "dmid", "dlast", "e_mid",
                                                             "e_nmid", "e_cum", "e_last", "qi", "ki", "qe", "ks",
                                                             "osq", "lnv", "rn", "on", "mm"))
            g.v = tensor(st, "g_v", [P, 3, P])
            g.kst = tensor(st, "g_kst", [P, 3, P])
            g.att = tensor(st, "g_att", [P, MASK_H])
            g.state = tensor(st, "g_state", [P, NCH, P])
            g.lb = tensor(st, "g_lb", [P, KT])
            g.oml = tensor(st, "g_oml", [P, KT])
            g.tmp = tensor(st, "g_tmp", [P, 4, KT])
            g.mask = tensor(st, "g_mask", [P, TAB_H])
        f = Named()
        with ExitStack() as st:
            f.kT = tensor(st, "f_kT", [P, HEADS, L])
            f.vT = tensor(st, "f_vT", [P, HEADS, L])
            f.LF = tensor(st, "f_LF", [P, SEQ])
            f.LA = tensor(st, "f_LA", [P, SEQ])
            f.RA = tensor(st, "f_RA", [P, L])
            f.mask = tensor(st, "f_mask", [P, MASK_F])
            f.stat = tensor(st, "f_stat", [P, 8])
            f.qg = tensor(st, "f_qg", [P, HEADS])
            with ExitStack() as s2:
                (f.kr, f.ksq, f.lnv, f.rn) = (
                    tensor(s2, "fk_" + name, [P, L]) for name in ("kr", "ksq", "lnv", "rn"))
                (f.fx, f.fa, f.fl, f.fF, f.ones) = (
                    tensor(s2, "ff_" + name, [HEADS, L]) for name in ("fx", "fa", "fl", "fF", "ones"))
            with ExitStack() as s2:
                (f.qr, f.qn, f.zr, f.zz, f.mm) = (
                    tensor(s2, "fq_" + name, [P, SEQ]) for name in ("qr", "qn", "zr", "zz", "mm"))
                f.qsq, f.zsig, f.qrn = sq2[:, 0, 0:SEQ], sq2[:, 1, 0:SEQ], root[:, 0:SEQ]
                f.vs = tensor(s2, "f_vs", [P, L])
                f.pr = tensor(s2, "f_pr", [P, MASK_F])
                f.pt = tensor(s2, "f_pt", [P, 4, P])
                f.v1 = tensor(s2, "f_v1", [P, P])
                f.pm = tensor(s2, "f_pm", [META, 3, P])
        c = Named()
        with ExitStack() as st:
            (c.gr, c.ar, c.sg, c.kr, c.vr, c.v1, c.k1, c.qr, c.q1, c.qsq, c.qln, c.qrn, c.qn, c.qf, c.t1,
             c.mm, c.cos, c.sin, c.mu, c.rstd, c.lnv, c.ct, c.cy, c.csig, c.cm) = (
                tensor(st, "c_" + name, [P, SEQ]) for name in ("gr", "ar", "sg", "kr", "vr", "v1", "k1",
                                                               "qr", "q1", "qsq", "qln", "qrn", "qn", "qf", "t1",
                                                               "mm", "cos", "sin", "mu", "rstd", "lnv", "ct", "cy",
                                                               "csig", "cm"))
            c.csq = tensor(st, "c_csq", [P, SEQ])
            c.ksq, c.kln, c.krn = c.csq, c.lnv, c.rstd
            c.hc = tensor(st, "c_hc", [P, SEQ + TAPS - 1])
            c.acc = tensor(st, "c_acc", [P, SEQ])
            c.acc1 = tensor(st, "c_acc1", [P, SEQ])
            with ExitStack() as s2:
                c.side = tensor(s2, "c_side", [P, 8, SEQ])
            c.kn = tensor(st, "c_kn", [P, SEQ])
            c.kf = tensor(st, "c_kf", [P, SEQ])
            c.pr = [tensor(st, f"c_pr{i}", [P, MASK_S]) for i in range(2)]
            c.pt = [tensor(st, f"c_pt{i}", [P, 3, P]) for i in range(2)]
            c.wt = tensor(st, "c_wt", [P, TAPS + 1])
            c.cv = tensor(st, "c_cv", [P, CONV_T, SEQ])
            c.v = tensor(st, "c_v", [P, 2, P])
            c.mask = tensor(st, "c_mask", [P, TAB_S])
            c.stat = tensor(st, "c_stat", [P, 2, 16])
            c.posi = tensor(st, "c_posi", [P, SEQ], I32)
        innermost.close()
        e = Named()
        e.slots = tensor(ctx, "e_slots", [P, 2, SEQ], BF16)
        e.slot_gate = root[:, 0:SEQ]
        e.gates = tensor(ctx, "e_gates", [P, 3, SEQ], BF16)
        e.iota = tensor(ctx, "e_iota", [P, SUBKEYS], BF16)
        with ExitStack() as st:
            e.row = tensor(st, "e_row", [P, 2, STEP, SUBKEYS], BF16)
            e.one = tensor(st, "e_one", [P, 2, STEP, SEG], BF16)
            e.col = tensor(st, "e_col", [P, 2, 3, STEP, SEG], BF16)
            e.rest = tensor(st, "e_rest", [P, 2, SEQ])
        with ExitStack() as st:
            e.hid = tensor(st, "e_hid", [P, 2, SEQ])
            e.act = tensor(st, "e_act", [P, 2, SEQ])
            e.coef_hi = tensor(st, "e_coef_hi", [P, 2, SEQ], F32R)
            e.coef_lo = tensor(st, "e_coef_lo", [P, 2, SEQ], F32R)
        with ExitStack() as st:
            st.enter_context(nc.sbuf_tensor("e_skip", [P, STEP * (SUBKEYS + 4 * SEG) + 2 * SEQ], F32))
            e.coef = tensor(st, "e_coef", [P, SEG, SEQ])
        r = Named()
        with ExitStack() as st:
            st.enter_context(nc.sbuf_tensor("r_skip", [P, STEP * (SUBKEYS + 4 * SEG) + 2 * SEQ], F32))
            e.e1 = tensor(st, "e_e1", [P, GROUPS, SLOTS])
            e.e2 = tensor(st, "e_e2", [P, GROUPS, SLOTS])
            e.gate = tensor(st, "e_gate", [P, GROUPS, SLOTS])
            r.keys = tensor(st, "r_keys", [P, 2 * PEER_HEADS, P])
            r.qT = tensor(st, "r_qT", [P, SEQ])
            r.work = tensor(st, "r_work", [P, GROUPS, SEQ])
            r.top = tensor(st, "r_top", [P, GROUPS, 2, TOPK])
            r.topi = tensor(st, "r_topi", [P, GROUPS, 2, TOPK], U32)
            r.topf = tensor(st, "r_topf", [P, GROUPS, 2, TOPK])
            r.cand = tensor(st, "r_cand", [P, GROUPS, TOPK * TOPK])
            r.val = tensor(st, "r_val", [P, GROUPS, TOPK])
            r.ci = tensor(st, "r_ci", [P, GROUPS, TOPK], U32)
            r.cij = tensor(st, "r_cij", [P, 2, GROUPS, TOPK], U32)
            r.cf = tensor(st, "r_cf", [P, 2, GROUPS, TOPK])
            r.oh = tensor(st, "r_oh", [P, GROUPS, TOPK, TOPK])
            r.ex = tensor(st, "r_ex", [P, 2, GROUPS, TOPK])
            r.st = tensor(st, "r_st", [P, 2, GROUPS * PEER_HEADS])
            r.vals = tensor(st, "r_vals", [P, GROUPS, SLOTS])

        def par(name, j=0, n=1, rows=P):
            at = PARAMS[name][0]
            return params[0:rows, bass.ds(at + j, n)]

        def con(name, rows=P):
            at, n = CONSTS[name]
            return consts[0:rows, at:at + n]

        token_at = {nc.scalar: 0, nc.vector: 0, nc.gpsimd: 0}

        def lone(eng):
            token_at[eng] = (token_at[eng] + 1) % 8
            k = 8 * list(token_at).index(eng) + token_at[eng]
            if eng is nc.scalar:
                eng.activation(token[:, k:k + 1], con("one"), ACT.Copy)
            elif eng is nc.vector:
                eng.memset(token[:, k:k + 1], 0.0)
            else:
                eng.tensor_tensor(token[:, k:k + 1], con("one"), con("one"), ALU.add)

        def at3(t, j, cols=slice(None)):
            return t[:, bass.ds(j, 1), cols]

        def one3(ap):
            return ap.rearrange("p (a n) -> p a n", a=1)

        inputs_in = sem("inputs_in")
        w_loaded = [sem(f"w_loaded{i}") for i in range(4)]
        w_hi_done = sem("w_hi_done")
        w_lo_done = [sem("w_lo_done0"), sem("w_lo_done1")]
        halves_done = sem("halves_done")
        evacuated = sem("evacuated")
        x_hi_done = sem("x_hi_done")
        x_split = sem("x_split")
        sq_done = sem("sq_done")
        sq_added = sem("sq_added")
        sum_done = sem("sum_done")
        root_done = sem("root_done")
        rinv_done = sem("rinv_done")
        act_chain = sem("act_chain")
        dve_chain = sem("dve_chain")
        pool_chain = sem("pool_chain")
        preset = sem("preset")
        ones_set = sem("ones_set")
        cols_all, cols_q = slice(0, L), slice(META, L)

        block = ctx.enter_context(nc.Block())

        def split_hi(act, t):
            act.wait_ge(w_loaded[t.q], 16 * t.m + 16)
            for half in range(2):
                need(act, halves_done, 2 * t.n + half - 3)
                act.activation(whi[:, (2 * t.q + half) % 4, :], raw[:, t.q, half * 1024:(half + 1) * 1024],
                               ACT.Copy).then_inc(w_hi_done, 1)

        def split_lo(eng, t, half):
            eng.wait_ge(w_hi_done, 2 * t.n + half + 1)
            slot = (2 * t.q + half) % 4
            eng.tensor_tensor(wlo[:, slot, :], raw[:, t.q, half * 1024:(half + 1) * 1024],
                              whi[:, slot, :].bitcast(F32), ALU.subtract).then_inc(w_lo_done[half], 1)

        def project(te, t, x, cols, skipped=0):
            n = cols.stop - cols.start
            need(te, evacuated, t.n - 1 - skipped)
            ps = bank[t.q % 2][:, 0:n]
            for half in range(2):
                te.wait_ge(w_lo_done[half], t.n + 1)
                if static(t.n) and t.n in FIRST:
                    te.wait_ge(x_split, SPLITS[t.n] - (8 if half == 0 else 0))
                slot = (2 * t.q + half) % 4
                for k in range(8):
                    kk = half * 8 + k
                    hi, lo = whi[:, slot, k * P:(k + 1) * P], wlo[:, slot, k * P:(k + 1) * P]
                    te.matmul(ps, hi, x[0][:, kk, cols], start=(kk == 0), stop=False)
                    te.matmul(ps, hi, x[1][:, kk, cols], start=False, stop=False)
                    last = te.matmul(ps, lo, x[0][:, kk, cols], start=False, stop=(kk == KT - 1))
                last.then_inc(halves_done, 1)

        def landed(eng, t):
            eng.wait_ge(halves_done, 2 * t.n + 2)

        def proj_ps(t, n):
            return bank[t.q % 2][:, 0:n]

        SUM = bank[2]

        def out_steps(base, i, s):
            j = 4 * i + s
            return j, Tile(base, i, s)

        OUT = ((T_AOUT, xb, cols_all, "kv_norm", xa, 1), (T_BOUT, xa, cols_q, "norm1", xb, 3),
               (T_WOUT, xa, cols_q, "norm2", xb, 4))
        SPLITS = {T_HGRN: 16, T_AOUT: 32, T_KV: 48, T_QZ: 64, T_BOUT: 80, T_CONV: 96, T_WOUT: 112, T_PEERQ: 128}
        FIRST = (T_AOUT, T_KV, T_QZ, T_BOUT, T_CONV, T_PEERQ)
        SQ_BEFORE = {T_AOUT: 4, T_BOUT: 4 + 16, T_WOUT: 4 + 32}

        def out_tensor(te, ch, spec):
            base, x, cols, _, _, _ = spec
            n = cols.stop - cols.start
            if base not in FIRST:
                te.wait_ge(x_split, SPLITS[base])
            def body(i):
                for s in range(4):
                    project(te, Tile(base, i, s), x, slice(0, n))
            ch.run(body, 0, KT // 4, 0)
            te.wait_ge(sq_added, ADDED_BEFORE[base] + KT)
            te.wait_ge(root_done, {T_AOUT: 1, T_BOUT: 2, T_WOUT: 3}[base])
            te.matmul(SUM[:, 0:n], con("ones"), root[:, 0:n], start=True, stop=True).then_inc(sum_done, 1)

        def out_scalar(act, ch, spec):
            base, _, cols, gain, y, _ = spec
            n = cols.stop - cols.start

            def body(i):
                for s in range(4):
                    j, t = out_steps(base, i, s)
                    if within(j, KT):
                        split_hi(act, t.next())
                    if within(j - 1, KT):
                        act.wait_ge(evacuated, t.n)
                        lone(act)
                        act.activation(at3(y[0], j - 1, slice(0, n)), at3(hT, j - 1, cols), ACT.Copy,
                                       scale=par(gain, j - 1)).then_inc(x_hi_done, 1)
                        need(act, sq_added, ADDED_BEFORE[base] + j - 2)
                        lone(act)
                        act.activation(one3(sq2[:, (s - 1) % 2, 0:n]), at3(hT, j - 1, cols), ACT.Square)\
                            .then_inc(sq_done, 1)
                    if static(j) and j == KT:
                        break
            ch.run(body, 1, 4, 1)
            act.wait_ge(sum_done, SUM_BEFORE[base] + 1)
            act.activation(root[:, 0:n], SUM[:, 0:n], ACT.Sqrt, bias=con("eps"), scale=1.0 / D)\
                .then_inc(root_done, 1)

        SUM_BEFORE = {T_AOUT: 1, T_BOUT: 2, T_WOUT: 3}
        ADDED_BEFORE = {T_AOUT: 0, T_BOUT: KT, T_WOUT: 2 * KT}

        def out_vector(ve, ch, spec, halves):
            base, _, cols, gain, y, nroot = spec
            n = cols.stop - cols.start

            def body(i):
                for s in range(4):
                    j, t = out_steps(base, i, s)
                    if within(j - 1, KT):
                        ve.wait_ge(halves_done, 2 * t.n)
                        ve.tensor_tensor(at3(hT, j - 1, cols), one3(bank[(t.q + 3) % 4 % 2][:, 0:n]),
                                         at3(hT, j - 1, cols), ALU.add).then_inc(evacuated, 1)
                    if within(j, KT):
                        for half in halves:
                            split_lo(ve, t.next(), half)
                    if within(j - 1, KT):
                        ve.wait_ge(x_hi_done, SPLITS[base] + j)
                        ve.scalar_tensor_tensor(at3(y[1], j - 1, slice(0, n)), at3(hT, j - 1, cols),
                                                par(gain, j - 1), at3(y[0], j - 1, slice(0, n)).bitcast(F32),
                                                ALU.mult, ALU.subtract).then_inc(x_split, 1)
                        ve.wait_ge(sq_done, SQ_BEFORE[base] + j)
                        if static(j) and j == 1:
                            ins = ve.tensor_copy(root[:, 0:n], sq2[:, 0, 0:n])
                        else:
                            ve.wait_ge(sq_added, ADDED_BEFORE[base] + j - 1)
                            ins = ve.tensor_tensor(root[:, 0:n], root[:, 0:n], sq2[:, (s - 1) % 2, 0:n], ALU.add)
                        ins.then_inc(sq_added, 1)
                    if static(j) and j == KT:
                        break
            ve.wait_ge(w_lo_done[0], base + 1)
            ch.run(body, 1, 4, 1)
            ve.wait_ge(root_done, ROOT_AFTER[base])
            ve.reciprocal(rinv[:, 0:n], root[:, 0:n]).then_inc(rinv_done, 1)

        ROOT_AFTER = {T_AOUT: 2, T_BOUT: 3, T_WOUT: 4}

        def out_pool(po, ch, spec, halves):
            base = spec[0]

            def body(i):
                for s in range(4):
                    for half in halves:
                        split_lo(po, Tile(base, i, s).next(), half)
            ch.run(body, 0, 4, 0)

        zeros_l = zt[:]

        masks_f, masks_c, masks_r = sem("masks_f"), sem("masks_c"), sem("masks_r")
        gates_done = sem("gates_done")
        fg_done = sem("fg_done")
        logf_done = sem("logf_done")
        cum_done = sem("cum_done")
        exps_done = sem("exps_done")
        factors_done = sem("factors_done")
        vT_done = sem("vT_done")
        v_done = sem("v_done")
        kT_done = sem("kT_done")
        kst_done = sem("kst_done")
        att_done = sem("att_done")
        masked_done = sem("masked_done")
        ds_done = sem("ds_done")
        lower_rows = sem("lower_rows")
        states_done = sem("states_done")
        o_done = sem("o_done")
        osq_done = sem("osq_done")
        osum_done = sem("osum_done")
        orn_done = sem("orn_done")
        m_done = sem("m_done")
        mhi_done = x_hi_done

        B_VT, B_KT, B_AT, B_DS, B_O = bank[3], bank[4], bank[5], bank[6], bank[7]
        tok = [slice(META, META + P), slice(META + P, L)]

        def span(c_):
            if c_ == 0:
                return slice(0, META), slice(0, META), 2
            c1 = c_ - 1
            return (slice(META + CH * c1, META + CH * (c1 + 1)), slice(CH * (c1 % 2), CH * (c1 % 2) + CH), c1 // 2)

        def att_cols(c_):
            return slice(P, P + META) if c_ == 0 else slice(CH * ((c_ - 1) // 2), CH * ((c_ - 1) // 2) + CH)

        def hgrn_tensor(te, ch):
            te.wait_ge(inputs_in, IN_ALL)
            for k in range(4):
                te.wait_ge(sq_done, k + 1)
                for kk in range(4):
                    last = te.matmul(SUM[:, 0:L], con("ones"), sqi[:, 4 * k + kk, :], start=(k + kk == 0),
                                     stop=(k + kk == 6))
            last.then_inc(sum_done, 1)
            te.wait_ge(x_split, SPLITS[T_HGRN])

            def body(h):
                t = [Tile(T_HGRN, h, s) for s in range(4)]
                p = h - 1
                if within(h, HEADS):
                    project(te, t[0], xa, cols_all)
                if within(h - 2, HEADS):
                    te.wait_ge(osq_done, h - 1)
                    te.matmul(SUM[:, 0:L], con("ones"), g.osq[:], start=True, stop=True).then_inc(osum_done, 1)
                if within(p, HEADS):
                    te.wait_ge(evacuated, 4 * p + 3)
                    need(te, v_done, p)
                    for n, cs in enumerate(tok):
                        te.transpose(B_VT[:, n * P:(n + 1) * P], g.vr[:, cs], con("ident"))
                    te.transpose(B_VT[0:META, 2 * P:3 * P], g.vr[:, 0:META], con("ident")).then_inc(vT_done, 1)
                if within(h, HEADS):
                    project(te, t[1], xa, cols_all)
                if within(p, HEADS):
                    te.wait_ge(factors_done, h)
                    need(te, kst_done, p)
                    te.transpose(B_KT[:, 0:P], g.ks[:, tok[0]], con("ident"))
                    te.transpose(B_KT[0:CH, P:2 * P], g.ks[:, META + P:META + P + CH], con("ident"))
                    te.transpose(B_KT[0:META, 2 * P:3 * P], g.ks[:, 0:META], con("ident")).then_inc(kT_done, 1)
                    need(te, masked_done, p)
                    for c_ in range(NCH + 1):
                        cs, rows, _ = span(c_)
                        last = te.matmul(B_AT[rows, att_cols(c_)], g.ki[:, cs], g.qi[:, cs], start=True, stop=True)
                    last.then_inc(att_done, 1)
                if within(h, HEADS):
                    project(te, t[2], xa, cols_all)
                if within(p, HEADS):
                    te.wait_ge(kst_done, h)
                    te.wait_ge(v_done, h)
                    need(te, states_done, p)
                    te.wait_ge(masked_done, h)
                    need(te, m_done, p)
                    te.matmul(B_O[:, 0:L], zeros_l, xa[0][:, 0, :], start=True, stop=False)
                    for chs in ((0, 1, 3), (2, 4)):
                        for c_ in chs:
                            cs, rows, n = span(c_)
                            if c_ < NCH:
                                ds = te.matmul(B_DS[:, c_ * P:(c_ + 1) * P], g.kst[rows, n, :], g.v[rows, n, :],
                                               start=True, stop=True)
                                if c_ == 2:
                                    ds.then_inc(ds_done, 1)
                            last = te.matmul(B_O[:, cs], g.v[rows, n, :], g.att[rows, att_cols(c_)], start=False,
                                             stop=False)
                        if chs[0] == 0:
                            last.then_inc(lower_rows, 1)
                            te.wait_ge(lower_rows, h)
                if within(h, HEADS):
                    project(te, t[3], xa, cols_all)
                if within(p, HEADS):
                    te.wait_ge(states_done, h)
                    for c_ in range(1, NCH + 1):
                        cs, _, _ = span(c_)
                        last = te.matmul(B_O[:, cs], g.state[:, c_ - 1, :], g.qe[:, cs], start=False,
                                         stop=(c_ == NCH))
                    last.then_inc(o_done, 1)
            ch.run(body, 2, HEADS, 2)

        def hgrn_scalar(act, ch):
            act.wait_ge(inputs_in, IN_ALL)
            act.wait_ge(preset, 2)
            act.activation(g.tmp[:, 0:2, :], g.tmp[:, 2:4, :], ACT.Exp).then_inc(act_chain, 1)
            ch.n += 1
            for k in range(4):
                act.activation(sqi[:, 4 * k:4 * k + 4, :], hT[:, 4 * k:4 * k + 4, :], ACT.Square)\
                    .then_inc(sq_done, 1)
                for kk in range(4 * k, 4 * k + 4):
                    act.activation(xa[0][:, kk, :], hT[:, kk, :], ACT.Copy, scale=par("a_norm", kk))\
                        .then_inc(x_hi_done, 1)
                if k == 0:
                    split_hi(act, Tile(T_HGRN, 0, 0))
            act.wait_ge(sum_done, 1)
            act.activation(root[:], SUM[:, 0:L], ACT.Sqrt, bias=con("eps"), scale=1.0 / D).then_inc(root_done, 1)

            def body(h):
                t = [Tile(T_HGRN, h, s) for s in range(4)]
                p = h - 1
                if within(h, HEADS):
                    split_hi(act, t[0].next())
                if within(h - 2, HEADS):
                    act.wait_ge(o_done, h - 1)
                    act.activation(g.osq[:], B_O[:, 0:L], ACT.Square).then_inc(osq_done, 1)
                if within(p, HEADS):
                    act.wait_ge(evacuated, 4 * p + 4)
                    act.activation(g.sq_f[:], g.fr[:], ACT.Sigmoid).then_inc(gates_done, 1)
                    act.activation(g.sq_q[:], g.qr[:], ACT.Sigmoid)
                    act.activation(g.sq_z[:], g.zr[:], ACT.Sigmoid).then_inc(gates_done, 1)
                    act.wait_ge(fg_done, h)
                    act.activation(g.logf[:], g.fg[:], ACT.Ln).then_inc(logf_done, 1)
                if within(h, HEADS):
                    split_hi(act, t[1].next())
                if within(p, HEADS):
                    act.wait_ge(vT_done, h)
                    act.activation(g.v[:, 0:2, :], B_VT[:, 0:2 * P].rearrange("p (a b) -> p a b", a=2), ACT.Copy)
                    act.activation(g.v[0:META, 2, :], B_VT[0:META, 2 * P:3 * P], ACT.Copy).then_inc(v_done, 1)
                    act.wait_ge(cum_done, h)
                    act.activation(g.e_mid[:], g.dmid[:], ACT.Exp)
                    act.activation(g.e_nmid[:], g.dmid[:], ACT.Exp, scale=-1.0)
                    act.activation(g.e_cum[:], g.cum[:], ACT.Exp)
                    act.activation(g.e_last[:], g.dlast[:], ACT.Exp, scale=-1.0).then_inc(exps_done, 1)
                if within(h - 2, HEADS):
                    act.wait_ge(osum_done, h - 1)
                    ch.link(act.activation(g.lnv[:], SUM[:, 0:L], ACT.Ln, bias=con("eps"), scale=1.0 / P))
                    act.activation(g.rn[:], g.lnv[:], ACT.Exp, scale=-0.5).then_inc(orn_done, 1)
                if within(h, HEADS):
                    split_hi(act, t[2].next())
                if within(p, HEADS):
                    act.wait_ge(kT_done, h)
                    act.activation(g.kst[:, 0, :], B_KT[:, 0:P], ACT.Copy)
                    act.activation(g.kst[0:CH, 1, :], B_KT[0:CH, P:2 * P], ACT.Copy)
                    act.activation(g.kst[0:META, 2, :], B_KT[0:META, 2 * P:3 * P], ACT.Copy).then_inc(kst_done, 1)
                if within(h - 2, HEADS):
                    act.wait_ge(m_done, h - 1)
                    lone(act)
                    act.activation(at3(xb[0], h - 2), one3(g.mm[:]), ACT.Copy).then_inc(mhi_done, 1)
                if within(h, HEADS):
                    split_hi(act, t[3].next())
            ch.run(body, 2, HEADS, 2)

        def chunks(ap):
            return ap[:, META:L].rearrange("p (c t) -> p c t", t=CH)

        def hgrn_vector(ve, ch):
            ve.memset(zt[:].bitcast(F32), 0.0).then_inc(preset, 1)
            ve.memset(g.att[:], 0.0)
            ve.wait_ge(inputs_in, IN_ALL)
            ch.link(ve.tensor_tensor(g.tmp[:, 0, :], par("gamma0", 0, KT), par("gamma1", 0, KT), ALU.max))
            ve.tensor_tensor(g.tmp[:, 2, :], par("gamma0", 0, KT), g.tmp[:, 0, :], ALU.subtract)
            ve.tensor_tensor(g.tmp[:, 3, :], par("gamma1", 0, KT), g.tmp[:, 0, :], ALU.subtract).then_inc(preset, 1)
            for k in range(KT):
                if k == 4:
                    split_lo(ve, Tile(T_HGRN, 0, 0), 0)
                ve.wait_ge(x_hi_done, k + 1)
                ve.scalar_tensor_tensor(xa[1][:, k, :], hT[:, k, :], par("a_norm", k), xa[0][:, k, :].bitcast(F32),
                                        ALU.mult, ALU.subtract).then_inc(x_split, 1)
            ve.wait_ge(act_chain, 1)
            ch.link(ve.tensor_tensor(g.tmp[:, 2, :], g.tmp[:, 0, :], g.tmp[:, 1, :], ALU.add))
            ch.link(ve.reciprocal(g.tmp[:, 3, :], g.tmp[:, 2, :]))
            ch.link(ve.tensor_tensor(g.lb[:], g.tmp[:, 0, :], g.tmp[:, 3, :], ALU.mult))
            ch.link(ve.tensor_scalar(g.oml[:], g.lb[:], -1.0, 1.0, ALU.mult, ALU.add))
            ve.wait_ge(root_done, 1)
            ch.link(ve.reciprocal(rinv[:], root[:]))

            def evac(t, dst):
                landed(ve, t)
                ve.tensor_tensor(dst[:], proj_ps(t, L), rinv[:], ALU.mult).then_inc(evacuated, 1)

            def body(h):
                t = [Tile(T_HGRN, h, s) for s in range(4)]
                p = h - 1
                if within(p, HEADS):
                    evac(Tile(T_HGRN, p, 3), g.zr)
                if within(h, HEADS):
                    split_lo(ve, t[0].next(), 0)
                if within(p, HEADS):
                    ve.wait_ge(gates_done, 2 * h - 1)
                    ch.link(ve.tensor_scalar(g.fg[:], g.sq_f[:], g.oml[:, bass.ds(p, 1)], g.lb[:, bass.ds(p, 1)],
                                             ALU.mult, ALU.add))
                    ve.tensor_scalar(g.kk[:], g.fg[:], -1.0, 1.0, ALU.mult, ALU.add).then_inc(fg_done, 1)
                    ve.wait_ge(gates_done, 2 * h)
                    ve.tensor_tensor(g.qs[:], g.qr[:], g.sq_q[:], ALU.mult)
                    ve.wait_ge(logf_done, h)
                    ch.link(ve.tensor_tensor_scan(g.cum[:], g.mask[:, MASK_H:TAB_H], g.logf[:], 0.0, ALU.mult, ALU.add))
                    ve.tensor_copy(g.dmid[:, 0:META], g.cum[:, 0:META])
                    cc = chunks(g.cum)
                    ve.tensor_tensor(chunks(g.dmid), cc, cc[:, :, MID:MID + 1].broadcast_to([P, NCH, CH]),
                                     ALU.subtract)
                    ve.tensor_scalar(g.dlast[:, 0:META], g.cum[:, 0:META], g.cum[:, META - 1:META], None,
                                     ALU.subtract)
                    ve.tensor_tensor(chunks(g.dlast), cc, cc[:, :, CH - 1:CH].broadcast_to([P, NCH, CH]),
                                     ALU.subtract).then_inc(cum_done, 1)
                if within(h, HEADS):
                    evac(t[0], g.qr)
                    split_lo(ve, t[1].next(), 0)
                if within(p, HEADS):
                    ve.wait_ge(exps_done, h)
                    ve.tensor_tensor(g.ks[:], g.kk[:], g.e_last[:], ALU.mult)
                    ve.tensor_tensor(g.ki[:], g.kk[:], g.e_nmid[:], ALU.mult)
                    ve.tensor_tensor(g.qi[:], g.qs[:], g.e_mid[:], ALU.mult)
                    ve.tensor_tensor(g.qe[:], g.qs[:], g.e_cum[:], ALU.mult).then_inc(factors_done, 1)
                if within(h - 2, HEADS):
                    ve.wait_ge(orn_done, h - 1)
                    ch.link(ve.scalar_tensor_tensor(g.on[:], B_O[:, 0:L], par("a_out_norm", h - 2), g.rn[:],
                                                    ALU.mult, ALU.mult))
                    ve.tensor_tensor(g.mm[:], g.on[:], g.zs[:], ALU.mult).then_inc(m_done, 1)
                if within(h, HEADS):
                    evac(t[1], g.fr)
                    split_lo(ve, t[2].next(), 0)
                if within(p, HEADS):
                    ve.wait_ge(att_done, h)
                    lone(ve)
                    ve.copy_predicated(g.att[:, 0:P], g.mask[:, 0:P].bitcast(U32), B_AT[:, 0:P])
                    ve.copy_predicated(g.att[0:META, P:MASK_H], g.mask[0:META, P:MASK_H].bitcast(U32),
                                       B_AT[0:META, P:MASK_H]).then_inc(masked_done, 1)
                if within(h - 2, HEADS):
                    ve.wait_ge(mhi_done, 16 + h - 1)
                    ve.tensor_tensor(at3(xb[1], h - 2), one3(g.mm[:]), at3(xb[0], h - 2).bitcast(F32),
                                     ALU.subtract).then_inc(x_split, 1)
                if within(p, HEADS):
                    ve.tensor_tensor(g.zs[:], g.zr[:], g.sq_z[:], ALU.mult)
                if within(h, HEADS):
                    evac(t[2], g.vr)
                    split_lo(ve, t[3].next(), 0)
                if within(p, HEADS):
                    ve.wait_ge(ds_done, h)
                    ch.link(ve.tensor_copy(g.state[:, 0, :], B_DS[:, 0:P]))
                    for c_ in range(1, NCH):
                        end = META + CH * c_ - 1
                        ins = ve.scalar_tensor_tensor(g.state[:, c_, :], g.state[:, c_ - 1, :],
                                                      g.e_cum[:, end:end + 1], B_DS[:, c_ * P:(c_ + 1) * P],
                                                      ALU.mult, ALU.add)
                        if c_ < NCH - 1:
                            ch.link(ins)
                    ins.then_inc(states_done, 1)
            ch.run(body, 2, HEADS, 2)

        def hgrn_pool(po, ch):
            split_lo(po, Tile(T_HGRN, 0, 0), 1)

            def body(h):
                for s in range(4):
                    split_lo(po, Tile(T_HGRN, h, s).next(), 1)
            ch.run(body, 0, HEADS, 0)

        sqi = f.kT

        ksq_done = sem("ksq_done")
        ksum_done = sem("ksum_done")
        krn_done = sem("krn_done")
        kn_done = sem("kn_done")
        fpart = sem("fpart")

        def kv_tensor(te, ch):
            def body(i):
                for u in range(2):
                    h = 2 * i + u
                    if within(h, HEADS):
                        project(te, Tile(T_KV, i, 2 * u), xa, cols_all)
                        project(te, Tile(T_KV, i, 2 * u + 1), xa, cols_all)
                        te.wait_ge(ksq_done, h + 1)
                        need(te, krn_done, h)
                        if static(h) and h == 0:
                            te.wait_ge(root_done, 2)
                        te.matmul(SUM[:, 0:L], con("ones"), f.ksq[:], start=True, stop=True).then_inc(ksum_done, 1)
            ch.run(body, 0, HEADS // 2, 0)
            project(te, Tile(T_FORGET, 0, 0), xa, cols_all)

        def kv_scalar(act, ch):
            def body(i):
                for u in range(2):
                    h = 2 * i + u
                    tk, tv = Tile(T_KV, i, 2 * u), Tile(T_KV, i, 2 * u + 1)
                    if within(h, HEADS):
                        split_hi(act, tk.next())
                    if within(h - 1, HEADS):
                        act.wait_ge(ksum_done, h)
                        ch.link(act.activation(f.lnv[:], SUM[:, 0:L], ACT.Ln, bias=con("eps"), scale=1.0 / P))
                        act.activation(f.rn[:], f.lnv[:], ACT.Exp, scale=-0.5).then_inc(krn_done, 1)
                    if within(h, HEADS):
                        lone(act)
                        act.activation(at3(xb[0], h), at3(hT, h), ACT.Copy, scale=par("b_norm", h))\
                            .then_inc(x_hi_done, 1)
                        split_hi(act, tv.next())
                        act.wait_ge(evacuated, tk.n + 1)
                        act.activation(f.ksq[:], f.kr[:], ACT.Square).then_inc(ksq_done, 1)
                    if static(h) and h == HEADS:
                        break
            ch.run(body, 1, HEADS // 2, 1)
            split_hi(act, Tile(T_QZ, 0, 0))
            act.wait_ge(evacuated, T_FORGET + 1)
            ch.link(act.activation(f.fa[:], f.fx[:], ACT.Abs, bias=par("b_f", rows=HEADS)))
            ch.link(act.activation(f.fl[:], f.fa[:], ACT.Exp, scale=-1.0))
            act.activation(f.fa[:], f.fl[:], ACT.Ln, bias=con("one", HEADS)).then_inc(fpart, 1)

        def kv_vector(ve, ch):
            def body(i):
                for u in range(2):
                    h = 2 * i + u
                    tk, tv = Tile(T_KV, i, 2 * u), Tile(T_KV, i, 2 * u + 1)
                    if within(h - 1, HEADS):
                        pv_ = Tile(T_KV, i, 2 * u - 1)
                        landed(ve, pv_)
                        ve.tensor_tensor(at3(f.vT, h - 1), one3(proj_ps(pv_, L)), one3(rinv[:]), ALU.mult)\
                            .then_inc(evacuated, 1)
                    if within(h, HEADS):
                        split_lo(ve, tk.next(), 0)
                    if within(h - 1, HEADS):
                        ve.wait_ge(krn_done, h)
                        ve.scalar_tensor_tensor(at3(f.kT, h - 1), one3(f.kr[:]), par("k_norm", h - 1), one3(f.rn[:]),
                                                ALU.mult, ALU.mult).then_inc(kn_done, 1)
                    if within(h, HEADS):
                        landed(ve, tk)
                        need(ve, kn_done, h)
                        ve.tensor_tensor(f.kr[:], proj_ps(tk, L), rinv[:], ALU.mult).then_inc(evacuated, 1)
                        split_lo(ve, tv.next(), 0)
                        ve.wait_ge(x_hi_done, SPLITS[T_KV] + h + 1)
                        ve.scalar_tensor_tensor(at3(xb[1], h), at3(hT, h), par("b_norm", h),
                                                at3(xb[0], h).bitcast(F32), ALU.mult, ALU.subtract)\
                            .then_inc(x_split, 1)
                    if static(h) and h == HEADS:
                        break
            ve.wait_ge(rinv_done, 1)
            ch.run(body, 1, HEADS // 2, 1)
            ve.memset(f.LF[:], 0.0)
            ve.memset(f.RA[:], 0.0)
            tf = Tile(T_FORGET, 0, 0)
            landed(ve, tf)
            ve.tensor_tensor(f.fx[:], bank[tf.q % 2][0:HEADS, 0:L], rinv[0:HEADS, :], ALU.mult).then_inc(evacuated, 1)
            split_lo(ve, tf.next(), 0)
            ve.wait_ge(evacuated, T_FORGET + 1)
            ch.link(ve.tensor_scalar(f.fF[:], f.fx[:], par("b_f", rows=HEADS), 0.0, ALU.add, ALU.min))
            ve.wait_ge(fpart, 1)
            ch.link(ve.tensor_tensor(f.fl[:], f.fF[:], f.fa[:], ALU.subtract))
            ch.link(ve.tensor_tensor_scan(f.fF[:], con_row_ones, f.fl[:], 0.0, ALU.mult, ALU.add))
            ch.link(ve.memset(f.LF[32:32 + HEADS, :], 1.0))
            ve.tensor_copy(f.LF[0:HEADS, :], f.fF[:, META:L])
            ve.memset(f.RA[0:HEADS, :], 1.0)
            ve.tensor_scalar(f.RA[32:32 + HEADS, :], f.fF[:], -1.0, None, ALU.mult)
            ve.tensor_scalar(f.qg[:], par("q_norm", 0, HEADS), float(P) ** -0.5, None, ALU.mult).then_inc(fpart, 1)

        con_row_ones = f.ones[:]

        def kv_pool(po, ch):
            po.memset(f.ones[:], 1.0).then_inc(ones_set, 1)

            def body(i):
                for s in range(4):
                    split_lo(po, Tile(T_KV, i, s).next(), 1)
            ch.run(body, 0, HEADS // 2, 0)
            split_lo(po, Tile(T_QZ, 0, 0), 1)

        qsq_done = sem("qsq_done")
        qsum_done = sem("qsum_done")
        qrn_done = sem("qrn_done")
        qn_done = sem("qn_done")
        aug_done = sem("aug_done")
        vs_done = sem("vs_done")
        zsig_done = sem("zsig_done")
        zz_done = sem("zz_done")
        scores_done = sem("scores_done")
        logits_done = sem("logits_done")
        expp_done = sem("expp_done")
        probs_done = sem("probs_done")
        pt_done = sem("pt_done")
        ptc_done = sem("ptc_done")
        fo_done = sem("fo_done")
        fm_done = sem("fm_done")
        B_SC, B_PT, B_PM, B_FO = bank[3], bank[4], bank[5], bank[6]
        K0 = META + P
        GS = (slice(0, K0), slice(K0, MASK_F))

        def qz_tensor(te, ch):
            te.wait_ge(fpart, 2)

            def body(i):
                for u in range(2):
                    h = 2 * i + u
                    if within(h, HEADS):
                        project(te, Tile(T_QZ, i, 2 * u), xb, cols_q)
                    if within(h - 2, HEADS):
                        te.wait_ge(ptc_done, h - 1)
                        need(te, fm_done, h - 2)
                        te.matmul(B_FO[:, 0:SEQ], f.pt[:, 3, :], f.pt[:, 0:2, :], start=True, stop=False)
                        te.matmul(B_FO[:, 0:SEQ], f.pm[:, 2, :], f.pm[:, 0:2, :], start=False, stop=False)
                        te.matmul(B_FO[:, P:SEQ], f.v1[:], f.pt[:, 2, :], start=False, stop=True)\
                            .then_inc(fo_done, 1)
                    if within(h - 1, HEADS):
                        te.wait_ge(qn_done, h)
                        te.wait_ge(aug_done, h)
                        need(te, logits_done, h - 1)
                        for n in range(2):
                            qs = slice(n * P, (n + 1) * P)
                            keys = slice(0, K0) if n == 0 else slice(0, L)
                            te.matmul(one3(B_SC[:, GS[n]]), f.qn[:, qs], at3(f.kT, h - 1, keys), start=True,
                                      stop=False)
                            last = te.matmul(B_SC[:, GS[n]], f.LA[:, qs], f.RA[:, keys], start=False, stop=True)
                        last.then_inc(scores_done, 1)
                    if within(h, HEADS):
                        project(te, Tile(T_QZ, i, 2 * u + 1), xb, cols_q)
                        te.wait_ge(qsq_done, h + 1)
                        need(te, qrn_done, h)
                        te.matmul(SUM[:, 0:SEQ], con("ones"), f.qsq, start=True, stop=True).then_inc(qsum_done, 1)
                    if within(h - 1, HEADS):
                        te.wait_ge(vs_done, h)
                        need(te, ptc_done, h - 1)
                        te.transpose(B_PT[:, 3 * P:4 * P], f.vs[:, META:K0], con("ident"))
                        te.transpose(B_PM[:, 3 * P:4 * P], f.vs[:, K0:L], con("ident"))
                        te.transpose(B_PM[0:META, 2 * P:3 * P], f.vs[:, 0:META], con("ident"))
                        te.wait_ge(probs_done, h)
                        te.transpose(B_PT[:, 0:P], f.pr[:, META:K0], con("ident"))
                        te.transpose(B_PT[:, P:2 * P], f.pr[:, K0 + META:K0 + META + P], con("ident"))
                        te.transpose(B_PT[:, 2 * P:3 * P], f.pr[:, K0 + META + P:MASK_F], con("ident"))
                        te.transpose(B_PM[0:META, 0:P], f.pr[:, 0:META], con("ident"))
                        te.transpose(B_PM[0:META, P:2 * P], f.pr[:, K0:K0 + META], con("ident"))\
                            .then_inc(pt_done, 1)
            ch.run(body, 1, HEADS // 2, 1)

        def qz_scalar(act, ch):
            def body(i):
                for u in range(2):
                    h = 2 * i + u
                    if within(h, HEADS):
                        split_hi(act, Tile(T_QZ, i, 2 * u).next())
                    if within(h - 2, HEADS):
                        act.wait_ge(pt_done, h - 1)
                        need(act, fo_done, h - 2)
                        act.activation(f.pt[:], B_PT[:].rearrange("p (a b) -> p a b", a=4), ACT.Copy)
                        act.activation(f.pm[:], B_PM[0:META, 0:3 * P].rearrange("p (a b) -> p a b", a=3), ACT.Copy)
                        act.activation(f.v1[:], B_PM[:, 3 * P:4 * P], ACT.Copy).then_inc(ptc_done, 1)
                    if within(h - 1, HEADS):
                        act.wait_ge(qsum_done, h)
                        ch.link(act.activation(f.qrn, SUM[:, 0:SEQ], ACT.Ln, bias=con("eps"), scale=1.0 / P))
                        act.activation(f.qrn, f.qrn, ACT.Exp, scale=-0.5).then_inc(qrn_done, 1)
                    if within(h, HEADS):
                        split_hi(act, Tile(T_QZ, i, 2 * u + 1).next())
                        act.wait_ge(evacuated, Tile(T_QZ, i, 2 * u).n + 1)
                        act.activation(f.qsq, f.qr[:], ACT.Square).then_inc(qsq_done, 1)
                    if within(h - 1, HEADS):
                        act.wait_ge(logits_done, h)
                        act.activation(f.pr[:, GS[0]], f.pr[:, GS[0]], ACT.Exp, bias=f.stat[:, 0:1],
                                       accum_out=f.stat[:, 2:3])
                        act.activation(f.pr[:, GS[1]], f.pr[:, GS[1]], ACT.Exp, bias=f.stat[:, 1:2],
                                       accum_out=f.stat[:, 3:4]).then_inc(expp_done, 1)
                        act.activation(f.zsig, f.zr[:], ACT.Sigmoid).then_inc(zsig_done, 1)
                    if within(h - 2, HEADS):
                        act.wait_ge(fm_done, h - 1)
                        lone(act)
                        act.activation(at3(xa[0], h - 2, slice(0, SEQ)), one3(f.mm[:]), ACT.Copy)\
                            .then_inc(x_hi_done, 1)
            ch.run(body, 1, HEADS // 2, 1)

        def qz_vector(ve, ch):
            def body(i):
                for u in range(2):
                    h = 2 * i + u
                    tq, tz = Tile(T_QZ, i, 2 * u), Tile(T_QZ, i, 2 * u + 1)
                    if within(h - 1, HEADS):
                        tp = Tile(T_QZ, i, 2 * u - 1)
                        landed(ve, tp)
                        need(ve, zz_done, h - 1)
                        ve.tensor_tensor(f.zr[:], proj_ps(tp, SEQ), rinv[:, cols_q], ALU.mult).then_inc(evacuated, 1)
                    if within(h, HEADS):
                        split_lo(ve, tq.next(), 0)
                    if within(h - 1, HEADS):
                        ve.wait_ge(qrn_done, h)
                        need(ve, scores_done, h - 1)
                        ve.scalar_tensor_tensor(f.qn[:], f.qr[:], f.qg[:, bass.ds(h - 1, 1)], f.qrn,
                                                ALU.mult, ALU.mult).then_inc(qn_done, 1)
                    if within(h, HEADS):
                        landed(ve, tq)
                        need(ve, qn_done, h)
                        ve.tensor_tensor(f.qr[:], proj_ps(tq, SEQ), rinv[:, cols_q], ALU.mult).then_inc(evacuated, 1)
                        split_lo(ve, tz.next(), 0)
                    if within(h - 1, HEADS):
                        ve.wait_ge(scores_done, h)
                        need(ve, pt_done, h - 1)
                        ch.link(ve.tensor_tensor(f.pr[:], B_SC[:, 0:MASK_F], f.mask[:], ALU.add))
                        ve.tensor_reduce(f.stat[:, 0:1], f.pr[:, GS[0]], AX_X, ALU.max, negate=True)
                        ve.tensor_reduce(f.stat[:, 1:2], f.pr[:, GS[1]], AX_X, ALU.max, negate=True)\
                            .then_inc(logits_done, 1)
                    if within(h - 2, HEADS):
                        ve.wait_ge(fo_done, h - 1)
                        need(ve, zz_done, h - 1)
                        ve.wait_ge(x_split, SPLITS[T_QZ] + h - 2)
                        ve.tensor_tensor(f.mm[:], B_FO[:, 0:SEQ], f.zz[:], ALU.mult).then_inc(fm_done, 1)
                    if within(h - 1, HEADS):
                        ve.wait_ge(expp_done, h)
                        ch.link(ve.reciprocal(f.stat[:, 4:6], f.stat[:, 2:4]))
                        ve.tensor_scalar(f.pr[:, GS[0]], f.pr[:, GS[0]], f.stat[:, 4:5], None, ALU.mult)
                        ve.tensor_scalar(f.pr[:, GS[1]], f.pr[:, GS[1]], f.stat[:, 5:6], None, ALU.mult)\
                            .then_inc(probs_done, 1)
                        ve.wait_ge(zsig_done, h)
                        ve.tensor_tensor(f.zz[:], f.zr[:], f.zsig, ALU.mult).then_inc(zz_done, 1)
                    if within(h - 2, HEADS):
                        ve.wait_ge(x_hi_done, SPLITS[T_QZ] + h - 1)
                        ve.tensor_tensor(at3(xa[1], h - 2, slice(0, SEQ)), one3(f.mm[:]),
                                         at3(xa[0], h - 2, slice(0, SEQ)).bitcast(F32), ALU.subtract)\
                            .then_inc(x_split, 1)
            ch.run(body, 1, HEADS // 2, 1)

        def qz_pool(po, ch):
            po.wait_ge(fpart, 2)
            po.wait_ge(kn_done, HEADS)

            def body(i):
                for u in range(2):
                    h = 2 * i + u
                    if within(h, HEADS):
                        split_lo(po, Tile(T_QZ, i, 2 * u).next(), 1)
                    if within(h - 1, HEADS):
                        need(po, scores_done, h - 1)
                        po.tensor_tensor(f.LA[:], f.LF[:], con_onehot(h - 1).broadcast_to([P, SEQ]), ALU.mult).then_inc(aug_done, 1)
                        need(po, pt_done, h - 1)
                        po.tensor_copy(one3(f.vs[:]), at3(f.vT, h - 1)).then_inc(vs_done, 1)
                    if within(h, HEADS):
                        split_lo(po, Tile(T_QZ, i, 2 * u + 1).next(), 1)
                    if static(h) and h == HEADS:
                        break
            ch.run(body, 1, HEADS // 2, 1)

        def con_onehot(h):
            return consts[:, bass.ds(CONSTS["onehot"][0] + h, 1)]

        csig_done = sem("csig_done")
        wt_set, acc1_done = sem("wt_set"), sem("acc1_done")
        side_products_done, side_step, side_done = sem("side_products_done"), sem("side_step"), sem("side_done")
        SIDE_TAPS = 8
        MAIN_TAPS = TAPS - 1 - SIDE_TAPS
        hconv_done = sem("hconv_done")
        cv_done = sem("cv_done")
        cv_part = sem("cv_part")
        tap_done = sem("tap_done")

        def conv_tensor(te, ch):
            def body(i):
                for s in range(4):
                    project(te, Tile(T_CONV, i, s), xb, slice(0, SEQ))
            ch.run(body, 0, CONV_T // 2, 0)

        def conv_scalar(act, ch):
            def body(i):
                for u in range(2):
                    j = 2 * i + u
                    if within(j, CONV_T):
                        split_hi(act, Tile(T_CONV, i, 2 * u).next())
                    if within(j - 1, CONV_T):
                        act.wait_ge(evacuated, Tile(T_CONV, i, 2 * u).n)
                        need(act, hconv_done, j - 1)
                        act.activation(c.sg[:], c.gr[:], ACT.Sigmoid, bias=par("b_in", CONV_T + j - 1))\
                            .then_inc(csig_done, 1)
                    if within(j, CONV_T):
                        split_hi(act, Tile(T_CONV, i, 2 * u + 1).next())
                    if within(j - 1, CONV_T):
                        side_products(act, j)
            ch.run(body, 1, CONV_T // 2, 0)

        def conv_steps(ve, ch, i, u, first):
            j = 2 * i + u
            if first:
                ve.wait_ge(csig_done, j)
                ve.scalar_tensor_tensor(c.hc[:, TAPS - 1:], c.ar[:], par("b_in", j - 1), c.sg[:], ALU.add, ALU.mult)\
                    .then_inc(hconv_done, 1)
                ve.tensor_copy(c.wt[:, 0:TAPS], par("conv_w", (j - 1) * TAPS, TAPS)).then_inc(wt_set, 1)
                ve.wait_ge(wt_set, j)
                a0 = SIDE_TAPS
                ve.tensor_scalar(c.acc[:], c.hc[:, a0:a0 + SEQ], c.wt[:, a0:a0 + 1], par("conv_b", j - 1),
                                 ALU.mult, ALU.add).then_inc(tap_done, 1)
                ve.tensor_scalar(c.acc1[:], c.hc[:, a0 + 1:a0 + 1 + SEQ], c.wt[:, a0 + 1:a0 + 2], None, ALU.mult)\
                    .then_inc(tap_done, 1)
                taps(ve, j, range(a0 + 2, a0 + 12))
            else:
                taps(ve, j, range(SIDE_TAPS + 12, TAPS - 1))
                ve.wait_ge(tap_done, j * MAIN_TAPS - 1)
                ve.scalar_tensor_tensor(c.acc[:], c.hc[:, TAPS - 1:], c.wt[:, TAPS - 1:TAPS], c.acc[:],
                                        ALU.mult, ALU.add).then_inc(cv_part, 1)
                ve.wait_ge(tap_done, j * MAIN_TAPS)
                ve.wait_ge(side_done, j)
                ve.tensor_tensor(c.acc1[:], c.acc1[:], c.side[:, 0, :], ALU.add).then_inc(acc1_done, 1)
                ve.wait_ge(cv_part, j)
                ve.wait_ge(acc1_done, j)
                ve.tensor_tensor(at3(c.cv, j - 1), one3(c.acc[:]), one3(c.acc1[:]), ALU.add).then_inc(cv_done, 1)

        def taps(ve, j, which):
            for k in which:
                acc = (c.acc, c.acc1)[k % 2]
                ve.wait_ge(tap_done, (j - 1) * MAIN_TAPS + k - SIDE_TAPS - 1)
                ve.scalar_tensor_tensor(acc[:], c.hc[:, k:k + SEQ], c.wt[:, k:k + 1], acc[:], ALU.mult, ALU.add)\
                    .then_inc(tap_done, 1)

        def side_products(act, j):
            act.wait_ge(wt_set, j)
            need(act, acc1_done, j - 1)
            for k in range(SIDE_TAPS):
                last = act.activation(c.side[:, k, :], c.hc[:, k:k + SEQ], ACT.Copy, scale=c.wt[:, k:k + 1])
            last.then_inc(side_products_done, 1)

        def side_sum(po, j):
            po.wait_ge(side_products_done, j)
            for m, w in enumerate((4, 2, 1)):
                ins = po.tensor_tensor(c.side[:, 0:w, :], c.side[:, 0:w, :], c.side[:, w:2 * w, :], ALU.add)
                if w > 1:
                    ins.then_inc(side_step, 1)
                    po.wait_ge(side_step, 2 * (j - 1) + m + 1)
            ins.then_inc(side_done, 1)

        def conv_vector(ve, ch):
            ve.memset(c.hc[:], 0.0)
            ve.wait_ge(rinv_done, 2)

            def body(i):
                for u in range(2):
                    j = 2 * i + u
                    ta = Tile(T_CONV, i, 2 * u)
                    if within(j - 1, CONV_T):
                        tp = Tile(T_CONV, i, 2 * u - 1)
                        landed(ve, tp)
                        need(ve, csig_done, j - 1)
                        ve.tensor_tensor(c.gr[:], proj_ps(tp, SEQ), rinv[:, 0:SEQ], ALU.mult).then_inc(evacuated, 1)
                        conv_steps(ve, ch, i, u, True)
                    if within(j, CONV_T):
                        landed(ve, ta)
                        ve.tensor_tensor(c.ar[:], proj_ps(ta, SEQ), rinv[:, 0:SEQ], ALU.mult).then_inc(evacuated, 1)
                    if within(j - 1, CONV_T):
                        conv_steps(ve, ch, i, u, False)
                    if static(j) and j == CONV_T:
                        break
            ch.run(body, 1, CONV_T // 2, 0)

        def conv_pool(po, ch):
            po.wait_ge(w_lo_done[0], T_CONV + 1)
            def body(i):
                for s in range(4):
                    for half in range(2):
                        split_lo(po, Tile(T_CONV, i, s).next(), half)
                    if s % 2 and within(2 * i + s // 2 - 1, CONV_T):
                        side_sum(po, 2 * i + s // 2)
            ch.run(body, 1, CONV_T // 2, 0)

        NQ = 8
        NSLOT = 2 + NQ
        S = Named()
        (S.k_bias, S.k_sum, S.k_rn, S.k_n, S.k_rot, S.v_bias, S.v_tr, S.v_copy, S.q_bias, S.q_sum, S.q_rn, S.q_n,
         S.q_rot, S.q_f, S.sc, S.mx, S.ex, S.pr, S.tr, S.trc, S.o, S.m, S.mean, S.mu, S.cen, S.csq, S.var, S.rstd,
         S.ct, S.cy, S.cm, S.table) = (
            sem("s_" + name) for name in ("k_bias", "k_sum", "k_rn", "k_n", "k_rot", "v_bias", "v_tr", "v_copy",
                                          "q_bias", "q_sum", "q_rn", "q_n", "q_rot", "q_f", "sc", "mx", "ex", "pr",
                                          "tr", "trc", "o", "m", "mean", "mu", "cen", "csq", "var", "rstd", "ct",
                                          "cy", "cm", "table"))
        B_RO, B_SA, B_SB, B_TA, B_TB = bank[3], bank[4], bank[5], bank[6], bank[7]
        B_SCS, B_TR = (B_SA, B_SB), (B_TA, B_TB)
        half_p = (slice(0, HD), slice(HD, P))

        def swa_tensor(te, ch):
            for s in range(NSLOT + 6):
                if s < NSLOT:
                    project(te, Tile(T_SWK, 0, s), xb, slice(0, SEQ))
                if s == 1:
                    te.wait_ge(S.k_bias, 1)
                    te.matmul(SUM[:, 0:SEQ], c.mask[:, MASK_S + P:TAB_S], c.ksq[:], start=True, stop=True).then_inc(S.k_sum, 1)
                if s == 2:
                    te.wait_ge(S.k_n, 1)
                    te.matmul(B_RO[:, 0:SEQ], c.mask[:, MASK_S:MASK_S + P], c.kn[:], start=True, stop=True).then_inc(S.k_rot, 1)
                    te.wait_ge(S.v_bias, 1)
                    for n in range(2):
                        last = te.transpose(B_SB[:, n * P:(n + 1) * P], c.v1[:, n * P:(n + 1) * P], con("ident"))
                    last.then_inc(S.v_tr, 1)
                    te.wait_ge(cv_done, CONV_T)
                    for k in range(CONV_T):
                        last = te.matmul(B_TB[:, 0:SEQ], con("ones"), c.cv[:, k, :], start=(k == 0),
                                         stop=(k == CONV_T - 1))
                    last.then_inc(S.mean, 1)
                if s == 4:
                    for k in range(CONV_T):
                        te.wait_ge(S.csq, k + 1)
                        te.matmul(B_TA[:, 0:SEQ], con("ones"), c.csqs[k % 2], start=(k == 0),
                                  stop=(k == CONV_T - 1)).then_inc(S.var, 1)
                j = s - 7
                if 0 <= j < NQ:
                    te.wait_ge(S.trc, j + 1)
                    need(te, S.m, j)
                    te.wait_ge(S.q_f, min(j + 3, NQ))
                    for hh in range(2):
                        o = B_RO[half_p[hh], SEQ:2 * SEQ]
                        vv = [c.v[:, n, half_p[hh]] for n in range(2)]
                        te.matmul(o[:, 0:SEQ], vv[0], c.pt[hh][:, 0:2, :], start=True, stop=False)
                        last = te.matmul(o[:, P:SEQ], vv[1], c.pt[hh][:, 2, :], start=False, stop=True)
                    last.then_inc(S.o, 1)
                j = s - 3
                if 0 <= j < NQ:
                    te.wait_ge(S.q_bias, j + 1)
                    need(te, S.q_rn, j)
                    if j == 0:
                        te.wait_ge(S.k_rn, 1)
                    te.matmul(SUM[:, 0:SEQ], c.mask[:, MASK_S + P:TAB_S], c.qsq[:], start=True, stop=True).then_inc(S.q_sum, 1)
                j = s - 4
                if 0 <= j < NQ:
                    te.wait_ge(S.q_n, j + 1)
                    if j == 0:
                        te.wait_ge(S.q_f_k, 1)
                    need(te, S.q_f, j)
                    need(te, S.m, j - 3)
                    te.matmul(B_RO[:, 0:SEQ], c.mask[:, MASK_S:MASK_S + P], c.qn[:], start=True, stop=True).then_inc(S.q_rot, 1)
                j = s - 5
                if 0 <= j < NQ:
                    te.wait_ge(S.q_f, j + 1)
                    need(te, S.mx, j)
                    te.wait_ge(S.v_copy, 1)
                    for hh in range(2):
                        hp = half_p[hh]
                        te.matmul(B_SCS[hh][:, 0:P], c.qf[hp, 0:P], c.kf[hp, 0:P], start=True, stop=True)
                        last = te.matmul(B_SCS[hh][:, P:3 * P], c.qf[hp, P:SEQ], c.kf[hp, :], start=True, stop=True)
                    last.then_inc(S.sc, 1)
                j = s - 6
                if 0 <= j < NQ:
                    te.wait_ge(S.pr, j + 1)
                    te.wait_ge(S.rstd, 1)
                    need(te, S.trc, j)
                    for hh in range(2):
                        for n in range(3):
                            last = te.transpose(B_TR[hh][:, n * P:(n + 1) * P], c.pr[hh][:, n * P:(n + 1) * P],
                                                con("ident"))
                    last.then_inc(S.tr, 1)

        def swa_scalar(act, ch):
            for s in range(NSLOT + 6):
                if s < NSLOT:
                    split_hi(act, Tile(T_SWK, 0, s).next())
                if s == 0:
                    act.wait_ge(evacuated, T_SWK)
                    act.wait_ge(hconv_done, CONV_T - 1)
                    act.activation(c.sg[:], c.gr[:], ACT.Sigmoid, bias=par("b_in", 2 * CONV_T - 1))\
                        .then_inc(csig_done, 1)
                    side_products(act, CONV_T)
                    act.wait_ge(S.table, 1)
                    act.activation(c.sin[:], c.t1[:], ACT.Sin)
                    act.activation(c.cos[:], c.mm[:], ACT.Sin).then_inc(S.table, 1)
                if s == 1:
                    act.wait_ge(evacuated, T_SWK + 1)
                    act.activation(c.k1[:], c.kr[:], ACT.Identity, bias=par("b_in", 24))
                    act.activation(c.ksq[:], c.kr[:], ACT.Square, bias=par("b_in", 24)).then_inc(S.k_bias, 1)
                if s == 2:
                    act.wait_ge(evacuated, T_SWK + 2)
                    act.activation(c.v1[:], c.vr[:], ACT.Identity, bias=par("b_in", 25)).then_inc(S.v_bias, 1)
                    act.wait_ge(S.k_sum, 1)
                    ch.link(act.activation(c.kln[:], SUM[:, 0:SEQ], ACT.Ln, bias=con("eps"), scale=1.0 / HD))
                    act.activation(c.krn[:], c.kln[:], ACT.Exp, scale=-0.5).then_inc(S.k_rn, 1)
                if s == 3:
                    act.wait_ge(S.mean, 1)
                    act.activation(c.mu[:], B_TB[:, 0:SEQ], ACT.Copy, scale=1.0 / (CONV_T * P)).then_inc(S.mu, 1)
                    act.wait_ge(S.v_tr, 1)
                    act.activation(c.v[:], B_SB[:, 0:2 * P].rearrange("p (a b) -> p a b", a=2), ACT.Copy)\
                        .then_inc(S.v_copy, 1)
                if s == 4:
                    act.wait_ge(S.cen, 1)
                    for k in range(CONV_T):
                        need(act, S.var, k - 1)
                        act.activation(c.csqs[k % 2], c.cv[:, k, :], ACT.Square).then_inc(S.csq, 1)
                if s == 5:
                    act.wait_ge(S.var, CONV_T)
                    ch.link(act.activation(c.lnv[:], B_TA[:, 0:SEQ], ACT.Ln, bias=con("eps"),
                                           scale=1.0 / (CONV_T * P)))
                    act.activation(c.rstd[:], c.lnv[:], ACT.Exp, scale=-0.5).then_inc(S.rstd, 1)
                if s - 2 in CONV_SLOTS:
                    k = CONV_SLOTS.index(s - 2)
                    act.wait_ge(S.cm, k + 1)
                    act.activation(xa[0][:, k, 0:SEQ], c.cm[:], ACT.Copy).then_inc(x_hi_done, 1)
                j = s - 7
                if 0 <= j < NQ:
                    act.wait_ge(S.tr, j + 1)
                    need(act, S.o, j)
                    for hh in range(2):
                        last = act.activation(c.pt[hh][:], B_TR[hh][:, 0:3 * P].rearrange("p (a b) -> p a b", a=3),
                                              ACT.Copy)
                    last.then_inc(S.trc, 1)
                j = s - 4
                if 0 <= j < NQ:
                    act.wait_ge(S.q_sum, j + 1)
                    ch.link(act.activation(c.qln[:], SUM[:, 0:SEQ], ACT.Ln, bias=con("eps"), scale=1.0 / HD))
                    act.activation(c.qrn[:], c.qln[:], ACT.Exp, scale=-0.5).then_inc(S.q_rn, 1)
                j = s - 3
                if 0 <= j < NQ:
                    act.wait_ge(evacuated, T_SWQ + j + 1)
                    need(act, S.q_sum, j)
                    need(act, S.q_n, j)
                    act.activation(c.q1[:], c.qr[:], ACT.Identity, bias=par("b_in", 16 + j))
                    act.activation(c.qsq[:], c.qr[:], ACT.Square, bias=par("b_in", 16 + j)).then_inc(S.q_bias, 1)
                if s - 1 in CONV_SLOTS:
                    act.wait_ge(S.soft, CONV_SLOTS.index(s - 1) + 1)
                    act.activation(c.csig[:], c.gr[:], ACT.Exp, scale=-1.0).then_inc(S.csig, 1)
                j = s - 6
                if 0 <= j < NQ:
                    act.wait_ge(S.mx, j + 1)
                    for hh in range(2):
                        st_ = c.stat[:, hh, :]
                        for n, cs in enumerate((slice(0, P), slice(P, 3 * P))):
                            act.activation(c.pr[hh][:, cs], c.pr[hh][:, cs], ACT.Exp, bias=st_[:, 2 + n:3 + n],
                                           accum_out=st_[:, 4 + n:5 + n])
                    act.activation(c.stat[:, :, 6:8], c.stat[:, :, 12:14], ACT.Exp).then_inc(S.ex, 1)
                if s in CONV_SLOTS:
                    k = CONV_SLOTS.index(s)
                    act.wait_ge(S.ct, k + 1)
                    ch.link(act.activation(c.kr[:], c.ct[:], ACT.Exp, scale=-1.0))
                    act.activation(c.ar[:], c.kr[:], ACT.Ln, bias=con("one")).then_inc(S.cy, 1)
                j = s - 8
                if 0 <= j < NQ:
                    act.wait_ge(S.m, j + 1)
                    act.activation(xa[0][:, CONV_T + j, 0:SEQ], c.mm[:], ACT.Copy).then_inc(x_hi_done, 1)

        CONV_SLOTS = [6 + k for k in range(CONV_T)]

        def swa_vector(ve, ch):
            xcount = [0]

            def lo_part(tile_k, src):
                xcount[0] += 1
                ve.wait_ge(x_hi_done, SPLITS[T_CONV] + xcount[0])
                ve.tensor_tensor(xa[1][:, tile_k, 0:SEQ], src, xa[0][:, tile_k, 0:SEQ].bitcast(F32),
                                 ALU.subtract).then_inc(x_split, 1)

            for s in range(NSLOT + 6):
                t = Tile(T_SWK, 0, s)
                if s == 0:
                    tp = Tile(T_CONV, 0, 2 * CONV_T - 1)
                    landed(ve, tp)
                    ve.wait_ge(csig_done, CONV_T - 1)
                    ve.tensor_tensor(c.gr[:], proj_ps(tp, SEQ), rinv[:, 0:SEQ], ALU.mult).then_inc(evacuated, 1)
                    two_pi = 2 * np.pi
                    c1 = float(np.float32(6.28125))
                    c2 = float(np.float32(two_pi - c1) - np.float32(two_pi - c1) % np.float32(2.0 ** -20))
                    c3 = float(two_pi - c1 - c2)
                    ch.link(ve.tensor_copy(c.q1[:], c.posi[:]))
                    ch.link(ve.tensor_scalar(c.q1[:], c.q1[:], con("freq"), None, ALU.mult))
                    ch.link(ve.tensor_scalar(c.qn[:], c.q1[:], 1.0 / two_pi, 12582912.0, ALU.mult, ALU.add))
                    ch.link(ve.tensor_scalar(c.qn[:], c.qn[:], -12582912.0, None, ALU.add))
                    for cc in (c1, c2, c3):
                        ch.link(ve.scalar_tensor_tensor(c.q1[:], c.qn[:], -cc, c.q1[:], ALU.mult, ALU.add))
                    ch.link(ve.tensor_scalar(c.t1[:], c.q1[:], 3.1415925, -3.1415925, ALU.min, ALU.max))
                    ve.tensor_scalar(c.mm[:], c.t1[:], 0.5, None, ALU.mult).then_inc(S.table, 1)
                    conv_steps(ve, ch, CONV_T // 2, 0, True)
                if s == 1:
                    landed(ve, Tile(T_SWK, 0, 0))
                    ve.tensor_tensor(c.kr[:], proj_ps(Tile(T_SWK, 0, 0), SEQ), rinv[:, 0:SEQ], ALU.mult)\
                        .then_inc(evacuated, 1)
                    conv_steps(ve, ch, CONV_T // 2, 0, False)
                    ve.wait_ge(S.table, 2)
                    ch.link(ve.tensor_tensor(c.cos[:], c.cos[:], c.cos[:], ALU.mult))
                    ch.link(ve.tensor_scalar(c.cos[:], c.cos[:], -2.0, 1.0, ALU.mult, ALU.add))
                if s == 2:
                    landed(ve, Tile(T_SWV, 0, 0))
                    ve.tensor_tensor(c.vr[:], proj_ps(Tile(T_SWV, 0, 0), SEQ), rinv[:, 0:SEQ], ALU.mult)\
                        .then_inc(evacuated, 1)
                    ve.wait_ge(S.k_rn, 1)
                    ve.scalar_tensor_tensor(c.kn[:], c.k1[:], par("swk_g"), c.krn[:], ALU.mult, ALU.mult)\
                        .then_inc(S.k_n, 1)
                    ch.link(ve.tensor_scalar(c.wt[:, TAPS:TAPS + 1], par("swq_g"), HD ** -0.5, None, ALU.mult))
                j = s - 3
                if 0 <= j < NQ:
                    tq = Tile(T_SWQ, 0, j)
                    landed(ve, tq)
                    need(ve, S.q_bias, j)
                    ve.tensor_tensor(c.qr[:], proj_ps(tq, SEQ), rinv[:, 0:SEQ], ALU.mult).then_inc(evacuated, 1)
                if s - 2 in CONV_SLOTS:
                    lo_part(CONV_SLOTS.index(s - 2), c.cm[:])
                if s - 1 in CONV_SLOTS:
                    k = CONV_SLOTS.index(s - 1)
                    ve.wait_ge(S.cy, k + 1)
                    ve.scalar_tensor_tensor(c.gr[:], c.cys[k % 2], -1.0, c.ar[:], ALU.mult, ALU.max)\
                        .then_inc(S.soft, 1)
                if s in CONV_SLOTS:
                    k = CONV_SLOTS.index(s)
                    if k == 0:
                        ve.wait_ge(S.rstd, 1)
                    ch.link(ve.tensor_tensor(c.mu[:], c.cv[:, k, :], c.rstd[:], ALU.mult))
                    ch.link(ve.tensor_scalar(c.cys[k % 2], c.mu[:], par("ln_g", k), par("ln_b", k), ALU.mult, ALU.add))
                    ve.tensor_scalar(c.ct[:], c.cys[k % 2], -40.0, None, ALU.max).then_inc(S.ct, 1)
                j = s - 5
                if 0 <= j < NQ:
                    ve.wait_ge(S.q_rot, j + 1)
                    if j > 0:
                        ve.wait_ge(S.sc, j)
                    rotary(ve, ch, c.qn, c.qf, S.q_f)
                j = s - 4
                if 0 <= j < NQ:
                    ve.wait_ge(S.q_rn, j + 1)
                    ve.scalar_tensor_tensor(c.qn[:], c.q1[:], c.wt[:, TAPS:TAPS + 1], c.qrn[:], ALU.mult, ALU.mult)\
                        .then_inc(S.q_n, 1)
                if s == 3:
                    ve.wait_ge(S.k_rot, 1)
                    rotary(ve, ch, c.kn, c.kf, S.q_f_k)
                    ve.wait_ge(S.mu, 1)
                    ve.tensor_tensor(c.cv[:], c.cv[:], one3(c.mu[:]).broadcast_to([P, CONV_T, SEQ]),
                                     ALU.subtract).then_inc(S.cen, 1)
                j = s - 8
                if 0 <= j < NQ:
                    ve.wait_ge(S.o, j + 1)
                    ve.wait_ge(x_split, SPLITS[T_CONV] + xcount[0])
                    ve.tensor_copy(c.mm[:], B_RO[:, SEQ:2 * SEQ]).then_inc(S.m, 1)
                j = s - 6
                if 0 <= j < NQ:
                    ve.wait_ge(S.sc, j + 1)
                    need(ve, S.tr, j)
                    for hh in range(2):
                        last = ve.tensor_tensor(c.pr[hh][:], B_SCS[hh][:, 0:3 * P], c.mask[:, 0:MASK_S], ALU.add)
                    ch.link(last)
                    for hh in range(2):
                        ve.tensor_reduce(c.stat[:, hh, 0:1], c.pr[hh][:, 0:P], AX_X, ALU.max)
                        last = ve.tensor_reduce(c.stat[:, hh, 1:2], c.pr[hh][:, P:3 * P], AX_X, ALU.max)
                    ch.link(last)
                    for hh in range(2):
                        last = ve.tensor_scalar(c.stat[:, hh, 2:4], c.stat[:, hh, 0:2], par("sinks", j + 8 * hh),
                                                -1.0, ALU.max, ALU.mult)
                    ch.link(last)
                    for hh in range(2):
                        last = ve.tensor_scalar(c.stat[:, hh, 12:14], c.stat[:, hh, 2:4], par("sinks", j + 8 * hh),
                                                None, ALU.add)
                    last.then_inc(S.mx, 1)
                j = s - 6
                if 0 <= j < NQ:
                    ve.wait_ge(S.ex, j + 1)
                    ch.link(ve.tensor_tensor(c.stat[:, :, 8:10], c.stat[:, :, 4:6], c.stat[:, :, 6:8], ALU.add))
                    ch.link(ve.reciprocal(c.stat[:, :, 10:12], c.stat[:, :, 8:10]))
                    for hh in range(2):
                        ve.tensor_scalar(c.pr[hh][:, 0:P], c.pr[hh][:, 0:P], c.stat[:, hh, 10:11], None, ALU.mult)
                        last = ve.tensor_scalar(c.pr[hh][:, P:3 * P], c.pr[hh][:, P:3 * P], c.stat[:, hh, 11:12],
                                                None, ALU.mult)
                    last.then_inc(S.pr, 1)
                if s - 1 in CONV_SLOTS:
                    k = CONV_SLOTS.index(s - 1)
                    ve.wait_ge(S.csig, k + 1)
                    need(ve, x_split, SPLITS[T_CONV] + xcount[0])
                    ve.tensor_tensor(c.cm[:], c.cys[k % 2], c.csig[:], ALU.mult).then_inc(S.cm, 1)
                j = s - 8
                if 0 <= j < NQ:
                    lo_part(CONV_T + j, c.mm[:])

        def rotary(ve, ch, src, dst, done):
            ve.tensor_tensor(dst[:], src[:], c.cos[:], ALU.mult)
            ch.link(ve.tensor_tensor(c.t1[:], B_RO[:, 0:SEQ], c.sin[:], ALU.mult))
            ve.tensor_tensor(dst[:], dst[:], c.t1[:], ALU.add).then_inc(done, 1)

        S.q_f_k = sem("s_k_f")
        c.csqs = [c.csq[:], c.acc[:]]
        c.cys = [c.cy[:], c.sg[:]]
        S.soft, S.csig = sem("s_soft"), sem("s_csig")

        def swa_pool(po, ch):
            for s in range(NSLOT):
                for half in range(2):
                    split_lo(po, Tile(T_SWK, 0, s).next(), half)
                if s == 0:
                    side_sum(po, CONV_T)

        R = Named()
        (R.sub, R.top, R.soft) = (
            sem("r_" + name) for name in ("sub", "top", "soft"))
        B_SUB = (bank[3], bank[4])

        def route_tensor(te, ch):
            te.wait_ge(rinv_done, 3)

            def body(i):
                for s in range(4):
                    j, t = 4 * i + s, Tile(T_PEERQ, i, s)
                    if within(j, 16):
                        project(te, t, xb, slice(0, SEQ))
                    if within(j - 1, 16):
                        te.wait_ge(evacuated, t.n)
                        need(te, R.top, j - 2)
                        for n in range(2):
                            last = te.matmul(one3(B_SUB[(s - 1) % 2][:, n * P:(n + 1) * P]),
                                             r.qT[:, n * P:(n + 1) * P], at3(r.keys, j - 1), start=True, stop=True)
                        last.then_inc(R.sub, 1)
                    if static(j) and j == 16:
                        break
            ch.run(body, 1, 4, 1)

        def route_scalar(act, ch):
            def body(i):
                for s in range(4):
                    split_hi(act, Tile(T_PEERQ, i, s).next())
            ch.run(body, 0, 4, 0)
            act.wait_ge(R.soft, 1)
            act.activation(e.gate[:], e.gate[:], ACT.Exp).then_inc(R.soft, 1)

        def route_vector(ve, ch):
            def head(h):
                for n in range(GROUPS):
                    cand3 = r.cand[:, n, :].rearrange("p (a b) -> p a b", a=TOPK)
                    last = ve.tensor_tensor(
                        cand3, r.top[:, n, 0, :].rearrange("p (a b) -> p a b", b=1).broadcast_to([P, TOPK, TOPK]),
                        r.top[:, n, 1, :].rearrange("p (a b) -> p a b", a=1).broadcast_to([P, TOPK, TOPK]), ALU.add)
                ch.link(last)
                top16(ve, ch, lambda n: r.cand[:, n, :], lambda n: r.val[:, n, :], lambda n: r.ci[:, n, :])
                ve.tensor_single_scalar(r.cij[:, 0, :, :], r.ci[:], 4, op=ALU.logical_shift_right)
                ve.tensor_single_scalar(r.cij[:, 1, :, :], r.ci[:], 15, op=ALU.bitwise_and)
                ch.link(ve.tensor_copy(r.topf[:], r.topi[:]))
                ch.link(ve.tensor_copy(r.cf[:], r.cij[:]))
                iota = con("iota")[:, 0:TOPK].rearrange("p (a b) -> p a b", a=1).broadcast_to([P, TOPK, TOPK])
                for w in range(2):
                    for n in range(GROUPS):
                        last = ve.tensor_tensor(
                            r.oh[:, n, :, :],
                            r.cf[:, w, n, :].rearrange("p (a b) -> p a b", b=1).broadcast_to([P, TOPK, TOPK]),
                            iota, ALU.is_equal)
                    ch.link(last)
                    for n in range(GROUPS):
                        last = ve.tensor_tensor(
                            r.oh[:, n, :, :], r.oh[:, n, :, :],
                            r.topf[:, n, w, :].rearrange("p (a b) -> p a b", a=1).broadcast_to([P, TOPK, TOPK]),
                            ALU.mult)
                    ch.link(last)
                    ch.link(ve.tensor_reduce(r.ex[:, w, :, :], r.oh[:], AX_X, ALU.add))
                for w, dst in enumerate((e.e1, e.e2)):
                    ve.tensor_copy(dst[:, :, bass.ds(h * TOPK, TOPK)], r.ex[:, w, :, :])
                ch.link(ve.tensor_copy(r.vals[:, :, bass.ds(h * TOPK, TOPK)], r.val[:]))

            def body(i):
                for s in range(4):
                    j, t = 4 * i + s, Tile(T_PEERQ, i, s)
                    if within(j, 16):
                        landed(ve, t)
                        need(ve, R.sub, j)
                        ve.tensor_tensor(r.qT[:], proj_ps(t, SEQ), rinv[:, 0:SEQ], ALU.mult).then_inc(evacuated, 1)
                    if within(j - 1, 16):
                        ve.wait_ge(R.sub, j)
                        w = (s - 1) % 2
                        top16(ve, ch, lambda n: B_SUB[w][:, n * P:(n + 1) * P], lambda n: r.top[:, n, w, :],
                              lambda n: r.topi[:, n, w, :], j - 1)
                        if w == 1:
                            head((j - 2) // 2 if static(j) else 2 * i + (s - 2) // 2)
                    if static(j) and j == 16:
                        break
            ch.run(body, 1, 4, 1)
            v4 = r.vals[:].rearrange("p g (h k) -> p (g h) k", k=TOPK)
            g4 = e.gate[:].rearrange("p g (h k) -> p (g h) k", k=TOPK)
            ve.tensor_tensor(g4, v4, v4[:, :, 0:1].broadcast_to([P, GROUPS * PEER_HEADS, TOPK]), ALU.subtract)\
                .then_inc(R.soft, 1)
            ve.wait_ge(R.soft, 2)
            ch.link(ve.tensor_reduce(r.st[:, 0, :], g4, AX_X, ALU.add))
            ch.link(ve.reciprocal(r.st[:, 1, :], r.st[:, 0, :]))
            rs = r.st[:, 1, :].rearrange("p (a b) -> p a b", b=1)
            ve.tensor_tensor(g4, g4, rs.broadcast_to([P, GROUPS * PEER_HEADS, TOPK]), ALU.mult).then_inc(R.soft, 1)
            ve.wait_ge(R.soft, 3)

        def top16(ve, ch, src, val, idx, tile=None):
            work = r.work[:, :, 0:src(0).shape[1]]
            ns = range(GROUPS)

            def turns(op):
                lone(ve)
                for n in ns:
                    last = op(n)
                return last
            ch.link(turns(lambda n: ve.max(val(n)[:, 0:8], src(n))))
            turns(lambda n: ve.max_index(idx(n)[:, 0:8], val(n)[:, 0:8], src(n)))
            for n in ns:
                last = ve.match_replace(work[:, n, :], val(n)[:, 0:8], src(n), -3.0e38)
            if tile is None:
                ch.link(last)
            else:
                last.then_inc(R.top, 1)
                ve.wait_ge(R.top, tile + 1)
            ch.link(turns(lambda n: ve.max(val(n)[:, 8:16], work[:, n, :])))
            ch.link(turns(lambda n: ve.max_index(idx(n)[:, 8:16], val(n)[:, 8:16], work[:, n, :])))

        def route_pool(po, ch):
            po.wait_ge(w_lo_done[0], T_PEERQ + 1)

            def body(i):
                for s in range(4):
                    for half in range(2):
                        split_lo(po, Tile(T_PEERQ, i, s).next(), half)
            ch.run(body, 0, 4, 0)

        slots_tr, slots_in = sem("slots_tr"), sem("slots_in")
        one_set, cols_set = sem("one_set"), sem("cols_set")
        rows_set, spread, spread_in = sem("rows_set"), sem("spread"), sem("spread_in")
        gelu_done, coef_done = sem("gelu_done"), sem("coef_done")
        coef_hi_done, coef_split = sem("coef_hi_done"), sem("coef_split")
        flushed, stored = sem("flushed"), sem("stored")
        STEPS = SEQ // STEP

        def slots_tensor(te, ch):
            te.wait_ge(R.soft, 3)
            te.wait_ge(R.top, 16)
            for w, src in enumerate((e.e1, e.e2, e.gate)):
                for n in range(GROUPS):
                    last = te.transpose(bank[3 + w // 2][:, (w % 2 * GROUPS + n) * P:(w % 2 * GROUPS + n + 1) * P],
                                        src[:, n, :], con("ident"))
            last.then_inc(slots_tr, 1)

        def slots_scalar(act, ch):
            act.wait_ge(slots_tr, 1)
            act.activation(e.slots[:], bank[3][:].rearrange("p (a b) -> p a b", a=2), ACT.Copy)
            act.activation(e.slot_gate, bank[4][:, 0:SEQ], ACT.Copy).then_inc(slots_in, 1)

        def spread_tensor(te, ch, g_):
            def body(i):
                for b in range(2):
                    q = 2 * i + b + g_ * STEPS
                    te.wait_ge(rows_set, q + 1)
                    te.wait_ge(cols_set, q + 1)
                    need(te, spread_in, q - 1)
                    if g_ and static(i) and i == 0:
                        te.wait_ge(flushed, 8 * g_)
                    for k in range(STEP):
                        ps = bank[3 + b][:, k * SEG:(k + 1) * SEG]
                        for w in range(3):
                            last = te.matmul(ps, e.row[:, b, k, :], e.col[:, b, w, k, :], start=(w == 0), stop=(w == 2))
                    last.then_inc(spread, 1)
            ch.run(body, 0, STEPS // 2, 0)

        def spread_vector(ve, ch, g_):
            ve.wait_ge(slots_in, 1)
            if g_:
                ve.wait_ge(halves_done, 2 * (T_V[g_ - 1] + SEG))

            if g_ == 0:
                ve.tensor_copy(e.iota[:], con("iota"))
                ch.link(ve.tensor_copy(e.gates[:, 0, :], e.slot_gate))
                ch.link(ve.tensor_tensor(e.rest[:, 0, :], e.slot_gate, e.gates[:, 0, :], ALU.subtract))
                ch.link(ve.tensor_copy(e.gates[:, 1, :], e.rest[:, 0, :]))
                ch.link(ve.tensor_tensor(e.rest[:, 1, :], e.rest[:, 0, :], e.gates[:, 1, :], ALU.subtract))
                ch.link(ve.tensor_copy(e.gates[:, 2, :], e.rest[:, 1, :]))

            def body(i):
                for b in range(2):
                    q = 2 * i + b
                    need(ve, spread, q + g_ * STEPS - 1)
                    need(ve, cols_set, q + g_ * STEPS - 1)
                    ve.tensor_tensor(e.one[:, b, :, :], mine_of(g_), per_token(e.slots[:, 1, bass.ds(q * STEP, STEP)]),
                                     ALU.is_equal).then_inc(one_set, 1)
                    ve.tensor_tensor(e.row[:, b, :, :],
                                     e.iota[:].rearrange("p (a b) -> p a b", a=1).broadcast_to([P, STEP, SUBKEYS]),
                                     e.slots[:, 0, bass.ds(q * STEP, STEP)].rearrange("p (a b) -> p a b", b=1)
                                     .broadcast_to([P, STEP, SUBKEYS]), ALU.is_equal)
                    ve.wait_ge(one_set, q + 1 + g_ * STEPS)
                    ve.tensor_tensor(e.col[:, b, 0, :, :], e.one[:, b, :, :],
                                     per_token(e.gates[:, 0, bass.ds(q * STEP, STEP)]), ALU.mult).then_inc(rows_set, 1)
            ch.run(body, 0, STEPS // 2, 0)

        def per_token(ap):
            return ap.rearrange("p (a b) -> p a b", b=1).broadcast_to([P, STEP, SEG])

        def mine_of(g_):
            return e.iota[:, g_ * SEG:(g_ + 1) * SEG].rearrange("p (a b) -> p a b", a=1)\
                .broadcast_to([P, STEP, SEG])

        def spread_pool(po, ch, g_):
            def body(i):
                for b in range(2):
                    q = 2 * i + b
                    po.wait_ge(one_set, q + 1 + g_ * STEPS)
                    for w in (1, 2):
                        last = po.tensor_tensor(e.col[:, b, w, :, :], e.one[:, b, :, :],
                                                per_token(e.gates[:, w, bass.ds(q * STEP, STEP)]), ALU.mult)
                    last.then_inc(cols_set, 1)
            ch.run(body, 0, STEPS // 2, 0)

        def spread_scalar(act, ch, g_):
            if g_:
                act.wait_ge(coef_split, SEG * g_)

            def body(i):
                for b in range(2):
                    q = 2 * i + b
                    act.wait_ge(spread, q + g_ * STEPS + 1)
                    lone(act)
                    act.activation(e.coef[:, :, bass.ds(q * STEP, STEP)],
                                   bank[3 + b][:].rearrange("p (c e) -> p e c", c=STEP), ACT.Copy)\
                        .then_inc(spread_in, 1)
            ch.run(body, 0, STEPS // 2, 0)

        def up_tensor(te, ch, g_):
            te.wait_ge(spread_in, STEPS * (g_ + 1))

            def body(i):
                for s in range(4):
                    project(te, Tile(T_U[g_], i, s), xb, slice(0, SEQ), g_ * SEG)
            ch.run(body, 0, SEG // 4, 0)

        def up_scalar(act, ch, g_):
            def body(i):
                for s in range(4):
                    j, t = 4 * i + s, Tile(T_U[g_], i, s)
                    if within(j, SEG):
                        split_hi(act, t.next())
                    if within(j - 1, SEG):
                        act.wait_ge(evacuated, t.n - g_ * SEG)
                        need(act, coef_done, j - 2 + g_ * SEG)
                        act.activation(e.act[:, (s + 1) % 2, :], e.hid[:, (s + 1) % 2, :], ACT.Gelu)\
                            .then_inc(gelu_done, 1)
                    if static(j) and j == SEG:
                        break
            ch.run(body, 0, SEG // 4, 1)

        def up_vector(ve, ch, g_):
            ve.wait_ge(w_lo_done[0], T_U[g_] + 1)
            ve.wait_ge(spread_in, STEPS * (g_ + 1))

            def body(i):
                for s in range(4):
                    j, t = 4 * i + s, Tile(T_U[g_], i, s)
                    if within(j - 1, SEG):
                        ve.wait_ge(halves_done, 2 * t.n)
                        need(ve, gelu_done, j - 2 + g_ * SEG)
                        ve.tensor_tensor(e.hid[:, (s + 1) % 2, :], bank[(t.q + 3) % 4 % 2][:, 0:SEQ], rinv[:, 0:SEQ],
                                         ALU.mult).then_inc(evacuated, 1)
                    if within(j, SEG):
                        split_lo(ve, t.next(), 0)
                    if within(j - 1, SEG):
                        ve.wait_ge(gelu_done, j + g_ * SEG)
                        ve.tensor_tensor(at3(e.coef, j - 1), one3(e.act[:, (s + 1) % 2, :]), at3(e.coef, j - 1),
                                         ALU.mult).then_inc(coef_done, 1)
                    if static(j) and j == SEG:
                        break
            ch.run(body, 0, SEG // 4, 1)

        def lo_pool(po, ch, base, count):
            def body(i):
                for s in range(4):
                    t = Tile(base, i, s).next()
                    if within_all(t, i):
                        split_lo(po, t, 1)
            ch.run(body, 0, count // 4 - 1, 1)

        def within_all(t, i):
            return not static(i) or t.n < TILES_ALL

        def down_tensor(te, ch, g_):
            te.wait_ge(evacuated, T_V[g_] - g_ * SEG)
            for b in range(8):
                te.matmul(bank[b][:].rearrange("p (a b) -> p a b", a=2), zeros_l, xb[0][:, 0:2, 0:SEQ], start=True,
                          stop=False)

            def body(i):
                for s in range(4):
                    j, t = 4 * i + s, Tile(T_V[g_], i, s)
                    te.wait_ge(coef_split, j + 1 + g_ * SEG)
                    final = static(j) and j == SEG - 1
                    for half in range(2):
                        te.wait_ge(w_lo_done[half], t.n + 1)
                        slot = (2 * t.q + half) % 4
                        for k in range(8):
                            kk = half * 8 + k
                            ps = bank[kk // 2][:, kk % 2 * SEQ:(kk % 2 + 1) * SEQ]
                            hi, lo = whi[:, slot, k * P:(k + 1) * P], wlo[:, slot, k * P:(k + 1) * P]
                            te.matmul(ps, hi, e.coef_hi[:, s % 2, :], start=False, stop=False)
                            te.matmul(ps, hi, e.coef_lo[:, s % 2, :], start=False, stop=False)
                            last = te.matmul(ps, lo, e.coef_hi[:, s % 2, :], start=False, 
                                             stop=(final and kk % 2 == 1))
                        last.then_inc(halves_done, 1)
            ch.run(body, 0, SEG // 4 - 1, 1)

        def down_scalar(act, ch, g_):
            def coef_hi(j, b):
                act.activation(one3(e.coef_hi[:, b, :]), at3(e.coef, j), ACT.Copy).then_inc(coef_hi_done, 1)

            act.wait_ge(coef_done, SEG * (g_ + 1))
            coef_hi(0, 0)

            def body(i):
                for s in range(4):
                    j, t = 4 * i + s, Tile(T_V[g_], i, s)
                    if within_all(t.next(), i):
                        split_hi(act, t.next())
                    if within(j + 1, SEG):
                        act.wait_ge(halves_done, 2 * t.n)
                        lone(act)
                        coef_hi(j + 1, (s + 1) % 2)
            ch.run(body, 0, SEG // 4 - 1, 1)

        def down_vector(ve, ch, g_):
            def coef_lo(j, b):
                ve.wait_ge(coef_hi_done, j + 1 + g_ * SEG)
                ve.tensor_tensor(one3(e.coef_lo[:, b, :]), at3(e.coef, j), one3(e.coef_hi[:, b, :].bitcast(F32)),
                                 ALU.subtract).then_inc(coef_split, 1)

            coef_lo(0, 0)

            def body(i):
                for s in range(4):
                    j, t = 4 * i + s, Tile(T_V[g_], i, s)
                    if within_all(t.next(), i):
                        split_lo(ve, t.next(), 0)
                    if within(j + 1, SEG):
                        coef_lo(j + 1, (s + 1) % 2)
            ch.run(body, 0, SEG // 4 - 1, 1)
            ve.wait_ge(halves_done, 2 * (T_V[g_] + SEG))
            for b in range(8):
                h2 = hT[:, 2 * b:2 * b + 2, cols_q]
                ve.wait_ge(flushed, 8 * g_)
                ve.tensor_tensor(h2, bank[b][:].rearrange("p (a b) -> p a b", a=2), h2, ALU.add).then_inc(flushed, 1)

        IN_ALL = 16 * 7

        @block.sync
        def _(sp):
            sp.dma_start(params[:], params_in).then_inc(inputs_in, 16)
            sp.dma_start(consts[:], consts_in).then_inc(inputs_in, 16)
            for k in range(4):
                sp.dma_start(hT[:, 4 * k:4 * k + 4, :], hT_in[:, 4 * k:4 * k + 4, :]).then_inc(inputs_in, 16)
                if k == 0:
                    sp.dma_start(raw[:, 0, :], w_in[0]).then_inc(w_loaded[0], 16)
            sp.dma_start(g.mask[:], masks_in[:, 0:TAB_H]).then_inc(inputs_in, 16)
            for q in range(1, 4):
                sp.dma_start(raw[:, q, :], w_in[q]).then_inc(w_loaded[q], 16)

            def weights(n0, n1, source):
                def load(q, m):
                    n = 4 * m + q
                    for half in range(2):
                        sp.wait_ge(w_lo_done[half], n - 3)
                    sp.dma_start(raw[:, q, :].rearrange("p (a b) -> p a b", a=1),
                                 source(n)).then_inc(w_loaded[q], 16)
                while n0 % 4 and n0 < n1:
                    load(n0 % 4, n0 // 4)
                    n0 += 1
                if n1 // 4 > n0 // 4:
                    with sp.Fori(n0 // 4, n1 // 4) as m:
                        for q in range(4):
                            load(q, m)
                for n in range(n1 // 4 * 4, n1):
                    load(n % 4, n // 4)

            weights(4, TILES, lambda n: w_in[bass.ds(n, 1)].rearrange("a p c -> p a c"))
            for g_ in range(SEGS):
                weights(T_U[g_], T_V[g_],
                        lambda n: u_in[bass.ds(n - T_U[g_] + g_ * SEG, 1)].rearrange("a p c -> p a c"))
                weights(T_V[g_], T_V[g_] + SEG, lambda n: v_in[:, bass.ds(n - T_V[g_] + g_ * SEG, 1), :])
            for b in range(8):
                sp.wait_ge(flushed, 8 * (SEGS - 1) + b + 1)
                sp.dma_start(out[:, 2 * b:2 * b + 2, :], hT[:, 2 * b:2 * b + 2, cols_q]).then_inc(stored, 16)
            sp.wait_ge(stored, 16 * 8)

        @block.tensor
        def _(te):
            ch = Chain(te, pool_chain)
            te.wait_ge(preset, 1)
            hgrn_tensor(te, ch)
            out_tensor(te, ch, OUT[0])
            kv_tensor(te, ch)
            qz_tensor(te, ch)
            out_tensor(te, ch, OUT[1])
            conv_tensor(te, ch)
            swa_tensor(te, ch)
            out_tensor(te, ch, OUT[2])
            te.wait_ge(masks_r, 16)
            route_tensor(te, ch)
            slots_tensor(te, ch)
            for g_ in range(SEGS):
                spread_tensor(te, ch, g_)
                up_tensor(te, ch, g_)
                down_tensor(te, ch, g_)

        @block.scalar
        def _(act):
            ch = Chain(act, act_chain)
            hgrn_scalar(act, ch)
            out_scalar(act, ch, OUT[0])
            act.dma_start(f.mask[:], masks_in[:, TAB_H:TAB_H + MASK_F]).then_inc(masks_f, 16)
            kv_scalar(act, ch)
            qz_scalar(act, ch)
            out_scalar(act, ch, OUT[1])
            act.wait_ge(fo_done, HEADS)
            act.dma_start(c.mask[:], masks_in[:, TAB_H + MASK_F:]).then_inc(masks_c, 16)
            act.dma_start(c.posi[:], pos_in.partition_broadcast(P)).then_inc(masks_c, 16)
            conv_scalar(act, ch)
            swa_scalar(act, ch)
            out_scalar(act, ch, OUT[2])
            act.dma_start(r.keys[:], keys_in).then_inc(masks_r, 16)
            route_scalar(act, ch)
            slots_scalar(act, ch)
            for g_ in range(SEGS):
                spread_scalar(act, ch, g_)
                up_scalar(act, ch, g_)
                down_scalar(act, ch, g_)

        @block.vector
        def _(ve):
            ch = Chain(ve, dve_chain)
            hgrn_vector(ve, ch)
            out_vector(ve, ch, OUT[0], (0,))
            ve.wait_ge(ones_set, 1)
            kv_vector(ve, ch)
            ve.wait_ge(masks_f, 16)
            qz_vector(ve, ch)
            out_vector(ve, ch, OUT[1], (0,))
            conv_vector(ve, ch)
            ve.wait_ge(masks_c, 32)
            swa_vector(ve, ch)
            out_vector(ve, ch, OUT[2], (0,))
            route_vector(ve, ch)
            for g_ in range(SEGS):
                spread_vector(ve, ch, g_)
                up_vector(ve, ch, g_)
                down_vector(ve, ch, g_)

        @block.gpsimd
        def _(po):
            ch = Chain(po, pool_chain)
            hgrn_pool(po, ch)
            out_pool(po, ch, OUT[0], (1,))
            kv_pool(po, ch)
            qz_pool(po, ch)
            out_pool(po, ch, OUT[1], (1,))
            conv_pool(po, ch)
            swa_pool(po, ch)
            out_pool(po, ch, OUT[2], (1,))
            route_pool(po, ch)
            for g_ in range(SEGS):
                spread_pool(po, ch, g_)
                lo_pool(po, ch, T_U[g_], SEG)
                lo_pool(po, ch, T_V[g_], SEG)


def kernel(**inputs):
    import concourse.bacc as bacc
    from concourse.bass_utils import run_bass_kernel_spmd

    a = {k: np.asarray(v) for k, v in inputs.items()}

    def cols(v):
        return v.reshape(-1, P).T

    def tiles(w):
        n = w.shape[1] // P
        return w.reshape(KT, P, n, P).transpose(2, 1, 0, 3).reshape(n, P, D)

    def interleave(*ws):
        return np.stack(ws, 1).reshape(-1, P, D)

    w_a = tiles(a["a_w_in"][0])
    kv = a["kv_w"]
    forget = np.zeros((D, P), np.float32)
    forget[:, :HEADS] = kv[:, 2 * D:]
    kvt, bt = tiles(kv[:, :2 * D]), tiles(a["b_w_in"][0])
    qmap = np.concatenate([np.r_[j * HD:(j + 1) * HD, (j + 8) * HD:(j + 9) * HD] for j in range(8)])
    w2, b2 = a["w_in_2"], a["b_in_2"]
    C = CONV_T * P
    q_w, q_b = w2[:, 2 * C:3 * C][:, qmap], b2[2 * C:3 * C][qmap]
    wo2 = np.concatenate([a["w_out_2"][:C], a["w_out_2"][C:][qmap]], 0)
    w_all = np.concatenate([
        interleave(w_a[:16], w_a[16:32], w_a[32:48], w_a[48:]), tiles(a["a_w_out"][0]),
        interleave(kvt[:16], kvt[16:]), tiles(forget), interleave(bt[:16], bt[16:]), tiles(a["b_w_out"][0]),
        interleave(tiles(w2[:, :C]), tiles(w2[:, C:2 * C])), tiles(w2[:, 3 * C:]), tiles(q_w), tiles(wo2),
        tiles(a["peer_w_q_2"])])
    assert w_all.shape[0] == TILES
    pk = np.zeros((P, N_PARAMS), np.float32)

    def put(name, v):
        at, n = PARAMS[name]
        pk[:v.shape[0], at:at + n] = v

    put("a_norm", cols(a["a_norm"][0]))
    put("gamma0", cols(a["gamma_lb"][0]))
    put("gamma1", cols(a["gamma_lb"][1]))
    put("a_out_norm", cols(a["a_out_norm"][0]))
    put("kv_norm", cols(a["kv_norm"]))
    put("k_norm", a["fox_k_norm"].T)
    put("b_norm", cols(a["b_norm"][0]))
    put("q_norm", a["b_q_norm"][0].T)
    put("norm1", cols(a["norm1_g_2"]))
    put("b_in", cols(np.concatenate([b2[:2 * C], q_b, b2[3 * C:]])))
    put("conv_w", a["conv_dw_w_2"].T.reshape(CONV_T, P, TAPS).transpose(1, 0, 2).reshape(P, -1))
    put("conv_b", cols(a["conv_dw_b_2"]))
    put("ln_g", cols(a["conv_ln_g_2"]))
    put("ln_b", cols(a["conv_ln_b_2"]))
    put("swq_g", np.tile(a["q_norm_g_2"], 2)[:, None])
    put("swk_g", np.tile(a["k_norm_g_2"], 2)[:, None])
    put("norm2", cols(a["norm2_g_2"]))
    put("b_f", a["fox_b_f"][:, None])
    put("sinks", np.tile(a["attn_sinks_2"][None], (P, 1)))
    h0 = np.concatenate([a["meta"], a["x"][0]], 0).T.reshape(KT, P, L).transpose(1, 0, 2)
    cst, msk = constants()
    arrays = {
        "hT": h0, "params": pk, "consts": cst, "masks": msk, "pos": a["positions_2"].reshape(SEQ),
        "keys": a["peer_sub_keys_2"].transpose(3, 0, 1, 2).reshape(P, 2 * PEER_HEADS, P),
        "w": w_all, "u": a["peer_u_2"].reshape(SUBKEYS, SUBKEYS, KT, P).transpose(1, 3, 2, 0)
        .reshape(SUBKEYS, P, D), "v": a["peer_v_2"].reshape(SUBKEYS, SUBKEYS, D),
    }
    arrays = {k: np.ascontiguousarray(v) for k, v in arrays.items()}
    nc = bacc.Bacc("TRN2", target_bir_lowering=False, num_devices=1)
    args = [nc.dram_tensor("in_" + k, v.shape, mybir.dt.from_np(v.dtype), kind="ExternalInput").ap()
            for k, v in arrays.items()]
    res = nc.dram_tensor("out", (P, KT, SEQ), F32, kind="ExternalOutput").ap()
    build(nc, *args, res)
    r = run_bass_kernel_spmd(nc, [{"in_" + k: v for k, v in arrays.items()}], core_ids=[0])
    return r.results[0]["out"].transpose(2, 1, 0).reshape(1, SEQ, D)
```
